# Optimizing a Trainium2 kernel written in Bass

```python
import math
import jax
import jax.numpy as jnp
from jax import lax
import numpy as np
import jax, jax.numpy as jnp

D_MODEL = 1024
BATCH = 1
SEQ = 512
DEPTH = 2

GRID_W = 64
CTX_LEN = 256
N_MIXERS = 4
HEAD_DIM = 64
ATTN_SCALE = HEAD_DIM ** -0.5
ROPE_THETA = 10000.0
NORM_EPS = 1e-6
Q_BLOCK = 128
N_MOD = 6
DA_HEADS = D_MODEL // (2 * HEAD_DIM)
NA_HEADS = D_MODEL // HEAD_DIM
NA_ROWS_MAX = 8
NA_COLS = 16
LRU_WIDTH = D_MODEL
LRU_BLOCK = 256
LRU_BLOCKS = LRU_WIDTH // LRU_BLOCK
LRU_CONV = 4
LRU_C = 8.0
GQA_Q_HEADS = D_MODEL // HEAD_DIM
GQA_KV_HEADS = GQA_Q_HEADS // 4
D_FF = 4 * D_MODEL


def n_uses(kind):
    return len(range(kind, DEPTH, N_MIXERS))

def rms_norm(x, g):
    xf = x.astype(jnp.float32)
    y = xf * lax.rsqrt(jnp.mean(xf * xf, axis=-1, keepdims=True) + NORM_EPS)
    return (y * g.astype(jnp.float32)).astype(x.dtype)

def modulate(h, shift, scale):
    return h * (1 + scale) + shift

def squared_relu_mlp(h, w1, w2):
    return jnp.square(jax.nn.relu(h @ w1)) @ w2

def axial_rope_table(n_tok):
    t = jnp.arange(n_tok)
    row = (t // GRID_W).astype(jnp.float32)
    col = (t % GRID_W).astype(jnp.float32)
    n_freq = HEAD_DIM // 4
    inv = ROPE_THETA ** (-jnp.arange(n_freq, dtype=jnp.float32) / n_freq)
    ang = jnp.concatenate([row[:, None] * inv, col[:, None] * inv], axis=-1)
    return jnp.cos(ang), jnp.sin(ang)

def apply_axial_rope(x, cos, sin):
    T = x.shape[1]
    half = x.shape[-1] // 2
    shp = (1, T) + (1,) * (x.ndim - 3) + (half,)
    cs = cos.reshape(shp)
    sn = sin.reshape(shp)
    xf = x.astype(jnp.float32).reshape(x.shape[:-1] + (half, 2))
    x0 = xf[..., 0]
    x1 = xf[..., 1]
    out = jnp.stack([x0 * cs - x1 * sn, x0 * sn + x1 * cs], axis=-1)
    return out.reshape(x.shape).astype(x.dtype)

def sweep_query_blocks(fn, q, k, v):
    B, S = q.shape[:2]
    nb = S // Q_BLOCK
    qb = q.reshape((B, nb, Q_BLOCK) + q.shape[2:]).swapaxes(0, 1)
    ob = lax.map(lambda qq: fn(qq, k, v), qb)
    return ob.swapaxes(0, 1).reshape((B, S) + ob.shape[3:])

def gqa_attend(q, k, v):
    B, Tq, Hq, dh = q.shape
    Hkv = k.shape[2]
    qg = q.reshape(B, Tq, Hkv, Hq // Hkv, dh)
    s = jnp.einsum('bqhgd,bkhd->bhgqk', qg, k).astype(jnp.float32) * ATTN_SCALE
    p = jax.nn.softmax(s, axis=-1).astype(v.dtype)
    o = jnp.einsum('bhgqk,bkhd->bqhgd', p, v)
    return o.reshape(B, Tq, Hq, dh)

def diff_attend(q, k, v, lam):
    s = jnp.einsum('bqhmd,bkhmd->bhmqk', q, k).astype(jnp.float32) * ATTN_SCALE
    p = jax.nn.softmax(s, axis=-1)
    w = (p[:, :, 0] - lam * p[:, :, 1]).astype(v.dtype)
    return jnp.einsum('bhqk,bkhe->bqhe', w, v)

def diff_attention_mixer(h_lat, h_ctx, p, layer_idx, cos, sin, need_ctx):
    w_qkv, q_gain, k_gain, lq1, lk1, lq2, lk2, subln_g, w_o = p
    lam_init = 0.8 - 0.6 * math.exp(-0.3 * layer_idx)
    lam = (jnp.exp(jnp.sum(lq1.astype(jnp.float32) * lk1.astype(jnp.float32)))
           - jnp.exp(jnp.sum(lq2.astype(jnp.float32) * lk2.astype(jnp.float32))) + lam_init)

    def proj_q(h):
        B, T, _ = h.shape
        q = (h @ w_qkv[:, :D_MODEL]).reshape(B, T, DA_HEADS, 2, HEAD_DIM)
        return rms_norm(q, q_gain)

    def proj_kv(h):
        B, T, _ = h.shape
        k, v = jnp.split(h @ w_qkv[:, D_MODEL:], 2, axis=-1)
        k = rms_norm(k.reshape(B, T, DA_HEADS, 2, HEAD_DIM), k_gain)
        return k, v.reshape(B, T, DA_HEADS, 2 * HEAD_DIM)

    def finish(o):
        B, T = o.shape[:2]
        o = rms_norm(o, subln_g) * (1.0 - lam_init)
        return o.reshape(B, T, D_MODEL) @ w_o

    q_l = apply_axial_rope(proj_q(h_lat), cos, sin)
    k_l, v_l = proj_kv(h_lat)
    k_l = apply_axial_rope(k_l, cos, sin)
    k_c, v_c = proj_kv(h_ctx)
    k_all = jnp.concatenate([k_c, k_l], axis=1)
    v_all = jnp.concatenate([v_c, v_l], axis=1)
    o_l = sweep_query_blocks(lambda qb, kb, vb: diff_attend(qb, kb, vb, lam), q_l, k_all, v_all)
    y_l = finish(o_l)
    y_c = finish(diff_attend(proj_q(h_ctx), k_c, v_c, lam)) if need_ctx else None
    return y_l, y_c

def heads_q(h, w_q, n_heads, gain):
    B, T, _ = h.shape
    return rms_norm((h @ w_q).reshape(B, T, n_heads, HEAD_DIM), gain)

def heads_kv(h, w_kv, n_heads, gain):
    B, T, _ = h.shape
    k, v = jnp.split(h @ w_kv, 2, axis=-1)
    k = rms_norm(k.reshape(B, T, n_heads, HEAD_DIM), gain)
    return k, v.reshape(B, T, n_heads, HEAD_DIM)

def neighbourhood_mixer(h_lat, h_ctx, p, need_ctx):
    w_qkv, q_gain, k_gain, rpb, w_o = p
    B, S, _ = h_lat.shape
    rows = S // GRID_W
    kr = min(NA_ROWS_MAX, rows)
    n_loc = kr * GRID_W
    w_q = w_qkv[:, :D_MODEL]
    w_kv = w_qkv[:, D_MODEL:]
    q_l = heads_q(h_lat, w_q, NA_HEADS, q_gain)
    k_l, v_l = heads_kv(h_lat, w_kv, NA_HEADS, k_gain)
    k_c, v_c = heads_kv(h_ctx, w_kv, NA_HEADS, k_gain)
    k_grid = k_l.reshape(B, rows, GRID_W, NA_HEADS, HEAD_DIM)
    v_grid = v_l.reshape(B, rows, GRID_W, NA_HEADS, HEAD_DIM)
    q_rows = q_l.reshape(B, rows, GRID_W, NA_HEADS, HEAD_DIM).swapaxes(0, 1)
    r_idx = jnp.arange(rows)
    row_start = jnp.clip(r_idx - kr // 2, 0, rows - kr)
    col = jnp.arange(GRID_W)
    col_start = jnp.clip(col - NA_COLS // 2, 0, GRID_W - NA_COLS)
    col_in = (col[None, :] >= col_start[:, None]) & (col[None, :] < col_start[:, None] + NA_COLS)
    col_bias_idx = jnp.clip(col[None, :] - col[:, None], -(NA_COLS - 1), NA_COLS - 1) + NA_COLS - 1

    def row_block(args):
        q_row, r, r0 = args
        k_band = lax.dynamic_slice_in_dim(k_grid, r0, kr, axis=1)
        v_band = lax.dynamic_slice_in_dim(v_grid, r0, kr, axis=1)
        s_loc = jnp.einsum('bqhd,brkhd->bhqrk', q_row, k_band).astype(jnp.float32) * ATTN_SCALE
        row_off = r0 + jnp.arange(kr) - r + NA_ROWS_MAX - 1
        bias = rpb[:, row_off][:, :, col_bias_idx].transpose(0, 2, 1, 3)
        s_loc = jnp.where(col_in[None, None, :, None, :], s_loc + bias[None].astype(jnp.float32), -jnp.inf)
        s_ctx = jnp.einsum('bqhd,bkhd->bhqk', q_row, k_c).astype(jnp.float32) * ATTN_SCALE
        s_all = jnp.concatenate([s_loc.reshape(B, NA_HEADS, GRID_W, n_loc), s_ctx], axis=-1)
        prob = jax.nn.softmax(s_all, axis=-1).astype(v_band.dtype)
        p_loc = prob[..., :n_loc].reshape(B, NA_HEADS, GRID_W, kr, GRID_W)
        o = (jnp.einsum('bhqrk,brkhd->bqhd', p_loc, v_band)
             + jnp.einsum('bhqk,bkhd->bqhd', prob[..., n_loc:], v_c))
        return o.reshape(B, GRID_W, NA_HEADS * HEAD_DIM)

    o = lax.map(row_block, (q_rows, r_idx, row_start))
    y_l = o.swapaxes(0, 1).reshape(B, S, D_MODEL) @ w_o
    y_c = None
    if need_ctx:
        q_c = heads_q(h_ctx, w_q, NA_HEADS, q_gain)
        y_c = gqa_attend(q_c, k_c, v_c).reshape(B, h_ctx.shape[1], D_MODEL) @ w_o
    return y_l, y_c

def centred_depthwise_conv(u, w, b):
    T = u.shape[1]
    left = LRU_CONV // 2
    right = LRU_CONV - 1 - left
    up = jnp.pad(u, ((0, 0), (left, right), (0, 0)))
    out = b + up[:, 0:T] * w[0]
    for j in range(1, LRU_CONV):
        out = out + up[:, j:j + T] * w[j]
    return out

def rglru_coeffs(u, w_a, b_a, w_x, b_x, lam):
    B, T, _ = u.shape
    ub = u.reshape(B, T, LRU_BLOCKS, LRU_BLOCK)
    r = jax.nn.sigmoid((jnp.einsum('btnd,nde->btne', ub, w_a).reshape(B, T, LRU_WIDTH) + b_a).astype(jnp.float32))
    i = jax.nn.sigmoid((jnp.einsum('btnd,nde->btne', ub, w_x).reshape(B, T, LRU_WIDTH) + b_x).astype(jnp.float32))
    log_a = -LRU_C * r * jax.nn.softplus(-lam.astype(jnp.float32))
    a = jnp.exp(log_a)
    b = jnp.sqrt(-jnp.expm1(2.0 * log_a)) * (i * u.astype(jnp.float32))
    return a, b

def scan_combine(left, right):
    a1, b1 = left
    a2, b2 = right
    return a1 * a2, a2 * b1 + b2

def linear_scan(a, b, h0, reverse):
    if reverse:
        b = b.at[:, -1].add(a[:, -1] * h0)
    else:
        b = b.at[:, 0].add(a[:, 0] * h0)
    _, h = lax.associative_scan(scan_combine, (a, b), reverse=reverse, axis=1)
    return h

def rglru_mixer(h_lat, h_ctx, p, need_ctx):
    (w_in, conv_w, conv_b, f_wa, f_ba, f_wx, f_bx, f_lam,
     b_wa, b_ba, b_wx, b_bx, b_lam, w_o) = p
    w_gate = w_in[:, :LRU_WIDTH]
    w_rec = w_in[:, LRU_WIDTH:]
    u_l = centred_depthwise_conv(h_lat @ w_rec, conv_w, conv_b)
    u_c = centred_depthwise_conv(h_ctx @ w_rec, conv_w, conv_b)
    h0 = jnp.zeros((h_ctx.shape[0], LRU_WIDTH), jnp.float32)
    a, b = rglru_coeffs(u_c, f_wa, f_ba, f_wx, f_bx, f_lam)
    hc_f = linear_scan(a, b, h0, False)
    a, b = rglru_coeffs(u_c, b_wa, b_ba, b_wx, b_bx, b_lam)
    hc_b = linear_scan(a, b, h0, True)
    a, b = rglru_coeffs(u_l, f_wa, f_ba, f_wx, f_bx, f_lam)
    hl_f = linear_scan(a, b, hc_f[:, -1], False)
    a, b = rglru_coeffs(u_l, b_wa, b_ba, b_wx, b_bx, b_lam)
    hl_b = linear_scan(a, b, hc_b[:, 0], True)

    def out(hf, hb, h):
        gate = jax.nn.gelu(h @ w_gate)
        return ((hf + hb).astype(gate.dtype) * gate) @ w_o

    y_l = out(hl_f, hl_b, h_lat)
    y_c = out(hc_f, hc_b, h_ctx) if need_ctx else None
    return y_l, y_c

def gqa_mixer(h_lat, h_ctx, p, cos, sin, need_ctx):
    w_qkv, q_gain, k_gain, w_o = p
    B, S, _ = h_lat.shape
    nq = GQA_Q_HEADS * HEAD_DIM
    w_q = w_qkv[:, :nq]
    w_kv = w_qkv[:, nq:]
    q_l = apply_axial_rope(heads_q(h_lat, w_q, GQA_Q_HEADS, q_gain), cos, sin)
    k_l, v_l = heads_kv(h_lat, w_kv, GQA_KV_HEADS, k_gain)
    k_l = apply_axial_rope(k_l, cos, sin)
    k_c, v_c = heads_kv(h_ctx, w_kv, GQA_KV_HEADS, k_gain)
    k_all = jnp.concatenate([k_c, k_l], axis=1)
    v_all = jnp.concatenate([v_c, v_l], axis=1)
    o_l = sweep_query_blocks(gqa_attend, q_l, k_all, v_all)
    y_l = o_l.reshape(B, S, D_MODEL) @ w_o
    y_c = None
    if need_ctx:
        q_c = heads_q(h_ctx, w_q, GQA_Q_HEADS, q_gain)
        y_c = gqa_attend(q_c, k_c, v_c).reshape(B, h_ctx.shape[1], D_MODEL) @ w_o
    return y_l, y_c

def first_inputs(seed: int = 0) -> dict:
    key = jax.random.key(seed)
    ks = iter(jax.random.split(key, 64))
    D = D_MODEL

    def normal(shape, scale):
        return jax.random.normal(next(ks), shape, jnp.float32) * scale

    def gain(shape):
        return 1.0 + normal(shape, 0.02)

    def lru_lambda(n):
        a0 = jax.random.uniform(next(ks), (n, LRU_WIDTH), jnp.float32, minval=0.9, maxval=0.999)
        s = a0 ** (1.0 / LRU_C)
        return jnp.log(s) - jnp.log1p(-s)

    na, nb, nc, nd = n_uses(0), n_uses(1), n_uses(2), n_uses(3)
    return {
        'x': normal((BATCH, SEQ, D), 1.0),
        'c': normal((BATCH, D), 1.0),
        'ctx': normal((BATCH, CTX_LEN, D), 1.0),
        'c_ctx': normal((D,), 1.0),
        'norm1_g': gain((DEPTH, D)),
        'norm2_g': gain((DEPTH, D)),
        'w_mod': normal((DEPTH, D, N_MOD * D), 0.5 * D ** -0.5),
        'b_mod': normal((DEPTH, N_MOD * D), 0.02),
        'w_mlp1': normal((DEPTH, D, D_FF), D ** -0.5),
        'w_mlp2': normal((DEPTH, D_FF, D), D_FF ** -0.5),
        'a_w_qkv': normal((na, D, 3 * D), D ** -0.5),
        'a_q_norm_g': gain((na, HEAD_DIM)),
        'a_k_norm_g': gain((na, HEAD_DIM)),
        'a_lambda_q1': normal((na, HEAD_DIM), 0.1),
        'a_lambda_k1': normal((na, HEAD_DIM), 0.1),
        'a_lambda_q2': normal((na, HEAD_DIM), 0.1),
        'a_lambda_k2': normal((na, HEAD_DIM), 0.1),
        'a_subln_g': gain((na, 2 * HEAD_DIM)),
        'a_w_o': normal((na, D, D), D ** -0.5),
        'b_w_qkv': normal((nb, D, 3 * D), D ** -0.5),
        'b_q_norm_g': gain((nb, HEAD_DIM)),
        'b_k_norm_g': gain((nb, HEAD_DIM)),
        'b_rpb': normal((nb, NA_HEADS, 2 * NA_ROWS_MAX - 1, 2 * NA_COLS - 1), 0.02),
        'b_w_o': normal((nb, D, D), D ** -0.5),
        'c_w_in': normal((nc, D, 2 * LRU_WIDTH), D ** -0.5),
        'c_conv_w': normal((nc, LRU_CONV, LRU_WIDTH), LRU_CONV ** -0.5),
        'c_conv_b': normal((nc, LRU_WIDTH), 0.01),
        'c_fwd_w_a': normal((nc, LRU_BLOCKS, LRU_BLOCK, LRU_BLOCK), LRU_BLOCK ** -0.5),
        'c_fwd_b_a': normal((nc, LRU_WIDTH), 0.01),
        'c_fwd_w_x': normal((nc, LRU_BLOCKS, LRU_BLOCK, LRU_BLOCK), LRU_BLOCK ** -0.5),
        'c_fwd_b_x': normal((nc, LRU_WIDTH), 0.01),
        'c_fwd_lam': lru_lambda(nc),
        'c_bwd_w_a': normal((nc, LRU_BLOCKS, LRU_BLOCK, LRU_BLOCK), LRU_BLOCK ** -0.5),
        'c_bwd_b_a': normal((nc, LRU_WIDTH), 0.01),
        'c_bwd_w_x': normal((nc, LRU_BLOCKS, LRU_BLOCK, LRU_BLOCK), LRU_BLOCK ** -0.5),
        'c_bwd_b_x': normal((nc, LRU_WIDTH), 0.01),
        'c_bwd_lam': lru_lambda(nc),
        'c_w_o': normal((nc, LRU_WIDTH, D), LRU_WIDTH ** -0.5),
        'd_w_qkv': normal((nd, D, (GQA_Q_HEADS + 2 * GQA_KV_HEADS) * HEAD_DIM), D ** -0.5),
        'd_q_norm_g': gain((nd, HEAD_DIM)),
        'd_k_norm_g': gain((nd, HEAD_DIM)),
        'd_w_o': normal((nd, D, D), D ** -0.5),
    }

def first_block(x, c, ctx, c_ctx, norm1_g, norm2_g, w_mod, b_mod, w_mlp1, w_mlp2,
              a_w_qkv, a_q_norm_g, a_k_norm_g, a_lambda_q1, a_lambda_k1, a_lambda_q2, a_lambda_k2,
              a_subln_g, a_w_o,
              b_w_qkv, b_q_norm_g, b_k_norm_g, b_rpb, b_w_o,
              c_w_in, c_conv_w, c_conv_b, c_fwd_w_a, c_fwd_b_a, c_fwd_w_x, c_fwd_b_x, c_fwd_lam,
              c_bwd_w_a, c_bwd_b_a, c_bwd_w_x, c_bwd_b_x, c_bwd_lam, c_w_o,
              d_w_qkv, d_q_norm_g, d_k_norm_g, d_w_o):
    S = x.shape[1]
    cos, sin = axial_rope_table(S)
    mixer_params = (
        (a_w_qkv, a_q_norm_g, a_k_norm_g, a_lambda_q1, a_lambda_k1, a_lambda_q2, a_lambda_k2, a_subln_g, a_w_o),
        (b_w_qkv, b_q_norm_g, b_k_norm_g, b_rpb, b_w_o),
        (c_w_in, c_conv_w, c_conv_b, c_fwd_w_a, c_fwd_b_a, c_fwd_w_x, c_fwd_b_x, c_fwd_lam,
         c_bwd_w_a, c_bwd_b_a, c_bwd_w_x, c_bwd_b_x, c_bwd_lam, c_w_o),
        (d_w_qkv, d_q_norm_g, d_k_norm_g, d_w_o),
    )
    for i in range(DEPTH):
        kind = i % N_MIXERS
        p = tuple(arr[i // N_MIXERS] for arr in mixer_params[kind])
        need_ctx = i < DEPTH - 1
        mod_l = jnp.split((jax.nn.silu(c) @ w_mod[i] + b_mod[i])[:, None, :], N_MOD, axis=-1)
        mod_c = jnp.split((jax.nn.silu(c_ctx) @ w_mod[i] + b_mod[i])[None, None, :], N_MOD, axis=-1)
        h_l = modulate(rms_norm(x, norm1_g[i]), mod_l[0], mod_l[1])
        h_c = modulate(rms_norm(ctx, norm1_g[i]), mod_c[0], mod_c[1])
        if kind == 0:
            y_l, y_c = diff_attention_mixer(h_l, h_c, p, i, cos, sin, need_ctx)
        elif kind == 1:
            y_l, y_c = neighbourhood_mixer(h_l, h_c, p, need_ctx)
        elif kind == 2:
            y_l, y_c = rglru_mixer(h_l, h_c, p, need_ctx)
        else:
            y_l, y_c = gqa_mixer(h_l, h_c, p, cos, sin, need_ctx)
        x = x + mod_l[2] * y_l
        x = x + mod_l[5] * squared_relu_mlp(modulate(rms_norm(x, norm2_g[i]), mod_l[3], mod_l[4]),
                                            w_mlp1[i], w_mlp2[i])
        if need_ctx:
            ctx = ctx + mod_c[2] * y_c
            ctx = ctx + mod_c[5] * squared_relu_mlp(modulate(rms_norm(ctx, norm2_g[i]), mod_c[3], mod_c[4]),
                                                    w_mlp1[i], w_mlp2[i])
    return x


N_MIXERS_2 = 2
N_ATT_LAYERS = (DEPTH + 1) // 2
N_SSM_LAYERS = DEPTH // 2

ATT_HEADS = 16
ATT_KV_HEADS = 4
ATT_GROUP = ATT_HEADS // ATT_KV_HEADS
ATT_DIM = ATT_HEADS * HEAD_DIM
ATT_IN_DIM = ATT_DIM + 2 * ATT_KV_HEADS * HEAD_DIM
WINDOW = 128
BLOCK = 128
SPAN = BLOCK + 2 * WINDOW
ROPE_BASE = 10000.0
ROPE_AXIS_DIM = HEAD_DIM // 2

SSM_D_INNER = 2 * D_MODEL
SSM_HEAD_DIM = 64
SSM_HEADS = SSM_D_INNER // SSM_HEAD_DIM
SSM_GROUPS = 4
SSM_GROUP_HEADS = SSM_HEADS // SSM_GROUPS
SSM_STATE = 128
SSM_CONV_W = 5
SSM_CHUNK = 128
SSM_CONV_DIM = SSM_D_INNER + 2 * SSM_GROUPS * SSM_STATE
SSM_IN_DIM = SSM_D_INNER + SSM_CONV_DIM + 2 * SSM_HEADS
SSM_NORM_GROUPS = SSM_GROUPS

FF_DIM = 4 * D_MODEL
ALPHA = (2.0 * DEPTH) ** 0.25
BETA = (8.0 * DEPTH) ** -0.25
LN_EPS = 1e-5
RMS_EPS = 1e-5
NEG_INF = -1e30


def layer_norm(x, g, b):
    xf = x.astype(jnp.float32)
    mu = jnp.mean(xf, axis=-1, keepdims=True)
    var = jnp.mean(jnp.square(xf - mu), axis=-1, keepdims=True)
    y = (xf - mu) * lax.rsqrt(var + LN_EPS) * g.astype(jnp.float32) + b.astype(jnp.float32)
    return y.astype(x.dtype)

def modulate_2(h, shift, scale):
    return h * (1.0 + scale) + shift

def squared_relu_mlp_2(h, w1, w2):
    return jnp.square(jax.nn.relu(h @ w1)) @ w2

def axial_rope_tables(rows):
    row = jnp.repeat(jnp.arange(rows), GRID_W).astype(jnp.float32)
    col = jnp.tile(jnp.arange(GRID_W), rows).astype(jnp.float32)
    inv_freq = ROPE_BASE ** (-jnp.arange(0, ROPE_AXIS_DIM, 2, dtype=jnp.float32) / ROPE_AXIS_DIM)
    ang_r = row[:, None] * inv_freq[None, :]
    ang_c = col[:, None] * inv_freq[None, :]
    return (jnp.cos(ang_r), jnp.sin(ang_r), jnp.cos(ang_c), jnp.sin(ang_c))

def rotate_half(x, cos, sin):
    x1, x2 = jnp.split(x, 2, axis=-1)
    return jnp.concatenate([x1 * cos - x2 * sin, x2 * cos + x1 * sin], axis=-1)

def apply_axial_rope_2(x, tables):
    cos_r, sin_r, cos_c, sin_c = tables
    bshape = (x.shape[1],) + (1,) * (x.ndim - 3) + (-1,)
    xf = x.astype(jnp.float32)
    xr = rotate_half(xf[..., :ROPE_AXIS_DIM], cos_r.reshape(bshape), sin_r.reshape(bshape))
    xc = rotate_half(xf[..., ROPE_AXIS_DIM:], cos_c.reshape(bshape), sin_c.reshape(bshape))
    return jnp.concatenate([xr, xc], axis=-1).astype(x.dtype)

def attention_mixer(u_lat, u_ctx, w_in, w_out, sink, rope, need_ctx_out):
    bsz, n, _ = u_lat.shape
    n_ctx = u_ctx.shape[1]
    nb = n // BLOCK
    scale = HEAD_DIM ** -0.5
    sink_f = sink.astype(jnp.float32).reshape(ATT_KV_HEADS, ATT_GROUP)

    def project(u):
        length = u.shape[1]
        q, k, v = jnp.split(u @ w_in, [ATT_DIM, ATT_DIM + ATT_KV_HEADS * HEAD_DIM], axis=-1)
        return (q.reshape(bsz, length, ATT_KV_HEADS, ATT_GROUP, HEAD_DIM),
                k.reshape(bsz, length, ATT_KV_HEADS, HEAD_DIM),
                v.reshape(bsz, length, ATT_KV_HEADS, HEAD_DIM))

    def sink_softmax(logits):
        s = jnp.broadcast_to(sink_f[None, :, :, None, None], logits.shape[:-1] + (1,))
        return jax.nn.softmax(jnp.concatenate([logits, s], axis=-1), axis=-1)

    q_l, k_l, v_l = project(u_lat)
    q_c, k_c, v_c = project(u_ctx)
    qr_l = apply_axial_rope_2(q_l, rope)
    kr_l = apply_axial_rope_2(k_l, rope)
    pad = ((0, 0), (WINDOW, WINDOW), (0, 0), (0, 0))
    k_pad = jnp.pad(kr_l, pad)
    v_pad = jnp.pad(v_l, pad)
    q_blocks = jnp.moveaxis(qr_l.reshape(bsz, nb, BLOCK, ATT_KV_HEADS, ATT_GROUP, HEAD_DIM), 1, 0)
    qp_blocks = jnp.moveaxis(q_l.reshape(bsz, nb, BLOCK, ATT_KV_HEADS, ATT_GROUP, HEAD_DIM), 1, 0)
    offs_q = jnp.arange(BLOCK)
    offs_k = jnp.arange(SPAN) - WINDOW

    def block_attend(args):
        blk, qb, qpb = args
        start = blk * BLOCK
        kw = lax.dynamic_slice_in_dim(k_pad, start, SPAN, axis=1)
        vw = lax.dynamic_slice_in_dim(v_pad, start, SPAN, axis=1)
        qi = start + offs_q
        kj = start + offs_k
        ok = (kj[None, :] >= 0) & (kj[None, :] < n) & (jnp.abs(qi[:, None] - kj[None, :]) <= WINDOW)
        s_win = jnp.einsum('blgrd,bsgd->bgrls', qb, kw).astype(jnp.float32) * scale
        s_win = jnp.where(ok, s_win, NEG_INF)
        s_ctx = jnp.einsum('blgrd,bsgd->bgrls', qpb, k_c).astype(jnp.float32) * scale
        p = sink_softmax(jnp.concatenate([s_win, s_ctx], axis=-1)).astype(vw.dtype)
        return (jnp.einsum('bgrls,bsgd->blgrd', p[..., :SPAN], vw)
                + jnp.einsum('bgrls,bsgd->blgrd', p[..., SPAN:SPAN + n_ctx], v_c))

    o = lax.map(block_attend, (jnp.arange(nb), q_blocks, qp_blocks))
    y_lat = jnp.moveaxis(o, 0, 1).reshape(bsz, n, ATT_DIM) @ w_out
    y_ctx = None
    if need_ctx_out:
        s = jnp.einsum('blgrd,bsgd->bgrls', q_c, k_c).astype(jnp.float32) * scale
        p = sink_softmax(s).astype(v_c.dtype)
        o_c = jnp.einsum('bgrls,bsgd->blgrd', p[..., :n_ctx], v_c)
        y_ctx = o_c.reshape(bsz, n_ctx, ATT_DIM) @ w_out
    return y_lat, y_ctx

def depthwise_conv(x, w, bias):
    ch = x.shape[-1]
    y = lax.conv_general_dilated(x, w[:, None, :].astype(x.dtype), window_strides=(1,),
                                 padding=[(SSM_CONV_W // 2, SSM_CONV_W // 2)],
                                 dimension_numbers=('NWC', 'WIO', 'NWC'), feature_group_count=ch)
    return y + bias

def segsum(a):
    t = a.shape[-1]
    a_rep = jnp.broadcast_to(a[..., None], a.shape + (t,))
    a_rep = jnp.where(jnp.tril(jnp.ones((t, t), dtype=bool), -1), a_rep, 0.0)
    cs = jnp.cumsum(a_rep, axis=-2)
    return jnp.where(jnp.tril(jnp.ones((t, t), dtype=bool)), cs, -jnp.inf)

def ssd_scan(xs, dt, a_neg, bm, cm, init_state, with_outputs):
    b, length, g, r, p = xs.shape
    n = bm.shape[-1]
    nc = length // SSM_CHUNK
    q = SSM_CHUNK
    dt4 = dt.reshape(b, length, g, r)
    x_dt = (xs.astype(jnp.float32) * dt4[..., None]).reshape(b, nc, q, g, r, p)
    a = jnp.moveaxis((dt4 * a_neg.reshape(g, r)).reshape(b, nc, q, g, r), 2, -1)
    a_cs = jnp.cumsum(a, axis=-1)
    bc = bm.astype(jnp.float32).reshape(b, nc, q, g, n)
    cc = cm.astype(jnp.float32).reshape(b, nc, q, g, n)
    decay_states = jnp.exp(a_cs[..., -1:] - a_cs)
    states = jnp.einsum('bcsgn,bcgrs,bcsgrp->bcgrpn', bc, decay_states, x_dt)
    states = jnp.concatenate([init_state[:, None], states], axis=1)
    chunk_a = jnp.pad(a_cs[..., -1], ((0, 0), (1, 0), (0, 0), (0, 0)))
    decay_chunk = jnp.exp(segsum(jnp.moveaxis(chunk_a, 1, -1)))
    new_states = jnp.einsum('bgrzc,bcgrpn->bzgrpn', decay_chunk, states)
    final_state = new_states[:, -1]
    if not with_outputs:
        return None, final_state
    prev_states = new_states[:, :-1]
    lmat = jnp.exp(segsum(a))
    cb = jnp.einsum('bclgn,bcsgn->bcgls', cc, bc)
    y_diag = jnp.einsum('bcgrls,bcsgrp->bclgrp', cb[:, :, :, None] * lmat, x_dt)
    y_off = jnp.einsum('bclgn,bcgrpn,bcgrl->bclgrp', cc, prev_states, jnp.exp(a_cs))
    return (y_diag + y_off).reshape(b, length, g, r, p), final_state

def ssm_mixer(u_lat, u_ctx, w_in, conv_w, conv_b, dt_bias, a_log, d_skip, norm_g, w_out, need_ctx_out):
    a_neg = -jnp.exp(a_log.astype(jnp.float32))
    bsz = u_lat.shape[0]

    def flip(t):
        return jnp.flip(t, axis=1)

    def prep(u):
        length = u.shape[1]
        z, xbc, dt = jnp.split(u @ w_in, [SSM_D_INNER, SSM_D_INNER + SSM_CONV_DIM], axis=-1)
        xbc = jax.nn.silu(depthwise_conv(xbc, conv_w, conv_b))
        xs, bm, cm = jnp.split(xbc, [SSM_D_INNER, SSM_D_INNER + SSM_GROUPS * SSM_STATE], axis=-1)
        xs = xs.reshape(bsz, length, SSM_GROUPS, SSM_GROUP_HEADS, SSM_HEAD_DIM)
        bm = bm.reshape(bsz, length, SSM_GROUPS, SSM_STATE)
        cm = cm.reshape(bsz, length, SSM_GROUPS, SSM_STATE)
        dt = jax.nn.softplus(dt.astype(jnp.float32).reshape(bsz, length, 2, SSM_HEADS)
                             + dt_bias.astype(jnp.float32))
        return z, xs, bm, cm, dt

    def finish(z, xs, y_f, y_b):
        length = xs.shape[1]
        y = y_f + y_b + xs.astype(jnp.float32) * d_skip.astype(jnp.float32).reshape(SSM_GROUPS, SSM_GROUP_HEADS, 1)
        y = y.reshape(bsz, length, SSM_D_INNER) * jax.nn.silu(z.astype(jnp.float32))
        y = y.reshape(bsz, length, SSM_NORM_GROUPS, -1)
        y = y * lax.rsqrt(jnp.mean(jnp.square(y), axis=-1, keepdims=True) + RMS_EPS)
        y = (y.reshape(bsz, length, SSM_D_INNER) * norm_g.astype(jnp.float32)).astype(z.dtype)
        return y @ w_out

    z_c, x_c, b_c, c_c, dt_c = prep(u_ctx)
    z_l, x_l, b_l, c_l, dt_l = prep(u_lat)
    init = jnp.zeros((bsz, SSM_GROUPS, SSM_GROUP_HEADS, SSM_HEAD_DIM, SSM_STATE), jnp.float32)
    yc_f, st_f = ssd_scan(x_c, dt_c[:, :, 0], a_neg[0], b_c, c_c, init, need_ctx_out)
    yc_b, st_b = ssd_scan(flip(x_c), flip(dt_c[:, :, 1]), a_neg[1], flip(b_c), flip(c_c), init, need_ctx_out)
    yl_f, _ = ssd_scan(x_l, dt_l[:, :, 0], a_neg[0], b_l, c_l, st_f, True)
    yl_b, _ = ssd_scan(flip(x_l), flip(dt_l[:, :, 1]), a_neg[1], flip(b_l), flip(c_l), st_b, True)
    y_lat = finish(z_l, x_l, yl_f, flip(yl_b))
    y_ctx = finish(z_c, x_c, yc_f, flip(yc_b)) if need_ctx_out else None
    return y_lat, y_ctx

def second_inputs(seed: int = 0) -> dict:
    key = jax.random.key(seed)
    ks = jax.random.split(key, 24)
    f = jnp.float32
    d = D_MODEL

    def nrm(k, shape, scale):
        return jax.random.normal(k, shape, f) * scale

    dt0 = jnp.exp(jax.random.uniform(ks[15], (N_SSM_LAYERS, 2, SSM_HEADS), f, math.log(1e-3), math.log(1e-1)))
    return {
        'x': nrm(ks[0], (BATCH, SEQ, d), 1.0),
        'c': nrm(ks[1], (BATCH, d), 1.0),
        'ctx': nrm(ks[2], (BATCH, CTX_LEN, d), 1.0),
        'c_ctx': nrm(ks[3], (d,), 1.0),
        'w_mod': nrm(ks[4], (DEPTH, d, N_MOD * d), 0.5 * d ** -0.5),
        'b_mod': nrm(ks[5], (DEPTH, N_MOD * d), 0.02),
        'ln_mix_g': 1.0 + nrm(ks[6], (DEPTH, d), 0.02),
        'ln_mix_b': nrm(ks[7], (DEPTH, d), 0.02),
        'ln_ff_g': 1.0 + nrm(ks[8], (DEPTH, d), 0.02),
        'ln_ff_b': nrm(ks[9], (DEPTH, d), 0.02),
        'att_w_in': nrm(ks[10], (N_ATT_LAYERS, d, ATT_IN_DIM), d ** -0.5),
        'att_w_out': nrm(ks[11], (N_ATT_LAYERS, ATT_DIM, d), BETA * ATT_DIM ** -0.5),
        'att_sink': nrm(ks[12], (N_ATT_LAYERS, ATT_HEADS), 0.5),
        'ssm_w_in': nrm(ks[13], (N_SSM_LAYERS, d, SSM_IN_DIM), d ** -0.5),
        'ssm_conv_w': nrm(ks[14], (N_SSM_LAYERS, SSM_CONV_W, SSM_CONV_DIM), SSM_CONV_W ** -0.5),
        'ssm_conv_b': nrm(ks[16], (N_SSM_LAYERS, SSM_CONV_DIM), 0.02),
        'ssm_dt_bias': dt0 + jnp.log(-jnp.expm1(-dt0)),
        'ssm_a_log': jnp.log(jax.random.uniform(ks[17], (N_SSM_LAYERS, 2, SSM_HEADS), f, 1.0, 16.0)),
        'ssm_d': 1.0 + nrm(ks[18], (N_SSM_LAYERS, SSM_HEADS), 0.1),
        'ssm_norm_g': 1.0 + nrm(ks[19], (N_SSM_LAYERS, SSM_D_INNER), 0.02),
        'ssm_w_out': nrm(ks[20], (N_SSM_LAYERS, SSM_D_INNER, d), BETA * SSM_D_INNER ** -0.5),
        'ff_w1': nrm(ks[21], (DEPTH, d, FF_DIM), d ** -0.5),
        'ff_w2': nrm(ks[22], (DEPTH, FF_DIM, d), BETA * FF_DIM ** -0.5),
    }

def second_block(x, c, ctx, c_ctx, w_mod, b_mod, ln_mix_g, ln_mix_b, ln_ff_g, ln_ff_b,
              att_w_in, att_w_out, att_sink, ssm_w_in, ssm_conv_w, ssm_conv_b, ssm_dt_bias,
              ssm_a_log, ssm_d, ssm_norm_g, ssm_w_out, ff_w1, ff_w2):
    rows = x.shape[1] // GRID_W
    rope = axial_rope_tables(rows)
    h_lat, h_ctx = x, ctx
    for i in range(DEPTH):
        last = i == DEPTH - 1
        j = i // N_MIXERS_2
        m_lat = (jax.nn.silu(c) @ w_mod[i] + b_mod[i])[:, None, :]
        m_ctx = (jax.nn.silu(c_ctx) @ w_mod[i] + b_mod[i])[None, None, :]
        sh_m_l, sc_m_l, g_m_l, sh_f_l, sc_f_l, g_f_l = jnp.split(m_lat, N_MOD, axis=-1)
        sh_m_c, sc_m_c, g_m_c, sh_f_c, sc_f_c, g_f_c = jnp.split(m_ctx, N_MOD, axis=-1)
        u_lat = modulate_2(h_lat, sh_m_l, sc_m_l)
        u_ctx = modulate_2(h_ctx, sh_m_c, sc_m_c)
        if i % N_MIXERS_2 == 0:
            y_lat, y_ctx = attention_mixer(u_lat, u_ctx, att_w_in[j], att_w_out[j], att_sink[j], rope, not last)
        else:
            y_lat, y_ctx = ssm_mixer(u_lat, u_ctx, ssm_w_in[j], ssm_conv_w[j], ssm_conv_b[j], ssm_dt_bias[j],
                                     ssm_a_log[j], ssm_d[j], ssm_norm_g[j], ssm_w_out[j], not last)
        h_lat = layer_norm(ALPHA * h_lat + g_m_l * y_lat, ln_mix_g[i], ln_mix_b[i])
        f_lat = squared_relu_mlp_2(modulate_2(h_lat, sh_f_l, sc_f_l), ff_w1[i], ff_w2[i])
        h_lat = layer_norm(ALPHA * h_lat + g_f_l * f_lat, ln_ff_g[i], ln_ff_b[i])
        if not last:
            h_ctx = layer_norm(ALPHA * h_ctx + g_m_c * y_ctx, ln_mix_g[i], ln_mix_b[i])
            f_ctx = squared_relu_mlp_2(modulate_2(h_ctx, sh_f_c, sc_f_c), ff_w1[i], ff_w2[i])
            h_ctx = layer_norm(ALPHA * h_ctx + g_f_c * f_ctx, ln_ff_g[i], ln_ff_b[i])
    return h_lat


def setup_inputs(seed=0):
    out = dict(first_inputs(seed))
    for name, value in second_inputs(seed + 1).items():
        if name != "x":
            out[name + "_2"] = value
    return out


def reference(
    x, c, ctx, c_ctx, norm1_g, norm2_g, w_mod, b_mod, w_mlp1, w_mlp2, a_w_qkv, a_q_norm_g,
    a_k_norm_g, a_lambda_q1, a_lambda_k1, a_lambda_q2, a_lambda_k2, a_subln_g, a_w_o, b_w_qkv,
    b_q_norm_g, b_k_norm_g, b_rpb, b_w_o, c_w_in, c_conv_w, c_conv_b, c_fwd_w_a, c_fwd_b_a,
    c_fwd_w_x, c_fwd_b_x, c_fwd_lam, c_bwd_w_a, c_bwd_b_a, c_bwd_w_x, c_bwd_b_x, c_bwd_lam,
    c_w_o, d_w_qkv, d_q_norm_g, d_k_norm_g, d_w_o, c_2, ctx_2, c_ctx_2, w_mod_2, b_mod_2,
    ln_mix_g_2, ln_mix_b_2, ln_ff_g_2, ln_ff_b_2, att_w_in_2, att_w_out_2, att_sink_2,
    ssm_w_in_2, ssm_conv_w_2, ssm_conv_b_2, ssm_dt_bias_2, ssm_a_log_2, ssm_d_2, ssm_norm_g_2,
    ssm_w_out_2, ff_w1_2, ff_w2_2,
):
    x = first_block(
        x, c, ctx, c_ctx, norm1_g, norm2_g, w_mod, b_mod, w_mlp1, w_mlp2, a_w_qkv, a_q_norm_g,
        a_k_norm_g, a_lambda_q1, a_lambda_k1, a_lambda_q2, a_lambda_k2, a_subln_g, a_w_o,
        b_w_qkv, b_q_norm_g, b_k_norm_g, b_rpb, b_w_o, c_w_in, c_conv_w, c_conv_b, c_fwd_w_a,
        c_fwd_b_a, c_fwd_w_x, c_fwd_b_x, c_fwd_lam, c_bwd_w_a, c_bwd_b_a, c_bwd_w_x, c_bwd_b_x,
        c_bwd_lam, c_w_o, d_w_qkv, d_q_norm_g, d_k_norm_g, d_w_o,
    )
    return second_block(
        x, c_2, ctx_2, c_ctx_2, w_mod_2, b_mod_2, ln_mix_g_2, ln_mix_b_2, ln_ff_g_2, ln_ff_b_2,
        att_w_in_2, att_w_out_2, att_sink_2, ssm_w_in_2, ssm_conv_w_2, ssm_conv_b_2,
        ssm_dt_bias_2, ssm_a_log_2, ssm_d_2, ssm_norm_g_2, ssm_w_out_2, ff_w1_2, ff_w2_2,
    )


_drawn_inputs = setup_inputs


def setup_inputs(seed=0):
    import zlib

    import numpy as np

    out = dict(_drawn_inputs(seed))
    spreads = {}
    factors = {'norm1_g': 8.0,
     'norm2_g': 4.361,
     'a_q_norm_g': 8.0,
     'a_k_norm_g': 8.0,
     'a_lambda_q1': 8.0,
     'a_lambda_k1': 8.0,
     'a_lambda_q2': 8.0,
     'a_lambda_k2': 8.0,
     'a_subln_g': 8.0,
     'b_q_norm_g': 8.0,
     'b_k_norm_g': 8.0,
     'b_rpb': 54.398,
     'ctx_2': 6.304,
     'c_ctx_2': 3.811,
     'b_mod_2': 3.087,
     'att_sink_2': 8.0,
     'ssm_conv_b_2': 8.0,
     'ssm_d_2': 8.0,
     'ssm_norm_g_2': 33.51}
    for name, (base, spread) in spreads.items():
        noise = np.random.default_rng([zlib.crc32(name.encode()), seed]).standard_normal(out[name].shape)
        drawn = base * np.exp(spread * noise) if base else spread * noise
        out[name] = jnp.asarray(drawn.astype(out[name].dtype))
    for name, factor in factors.items():
        out[name] = (out[name] * factor).astype(out[name].dtype)
    return out
```

```python
from contextlib import ExitStack

import numpy as np

import concourse.bass as bass
from concourse import mybir

P = 128
D = 1024
KD = D // P
LAT_TILES, CTX_TILES = 4, 2
TOK_TILES = LAT_TILES + CTX_TILES
N_LAT, N_CTX = LAT_TILES * P, CTX_TILES * P
N_TOK = N_LAT + N_CTX
GRID_W = 64
HEAD_DIM = 64
PAIRS = D // (2 * HEAD_DIM)
SLAB_K, SLAB_N = 4, 512
D_FF = 4 * D
FF_CHUNK = 512
LAM_INIT = 0.8 - 0.6 * float(np.exp(-0.3 * 0))
SCALE = HEAD_DIM ** -0.5
ALPHA = (2.0 * 2) ** 0.25
NORM_EPS = 1e-6
LN_EPS = 1e-5
NEG = -1e30
WINDOW_COLS = 16
N_ROWS = N_LAT // GRID_W
REL_ROWS, REL_COLS = 15, 31

F32 = mybir.dt.float32
F32R = mybir.dt.float32r
ALU = mybir.AluOpType
ACT = mybir.ActivationFunctionType
AX = mybir.AxisListType
ds = bass.ds


class Sem:

    def __init__(self, handle, credit=0):
        self.h = handle
        self.n = credit


class Chain:

    def __init__(self, eng, sem, start=0):
        self.eng, self.sem, self.start, self.k = eng, sem, start, 0

    def __call__(self, ins):
        self.k += 1
        ins.then_inc(self.sem.h, 1)
        self.eng.wait_ge(self.sem.h, self.sem.n + self.start + self.k)


class Kernel:
    pass


class Stream:

    def __init__(self, count, half):
        self.count, self.half = count, half


def columns_stream(w, n_slabs, col0=0):
    rows = w.rearrange("(k p) n -> p k n", p=P)
    return Stream(n_slabs, lambda n, h: rows[:, h * SLAB_K:(h + 1) * SLAB_K, ds(col0 + n * SLAB_N, SLAB_N)])


def rows_stream(w):
    rows = w.rearrange("(k p) n -> p k n", p=P)
    return Stream(4, lambda n, h: rows[:, (n % 2) * 8 + h * SLAB_K:(n % 2) * 8 + (h + 1) * SLAB_K,
                                       (n // 2) * SLAB_N:(n // 2 + 1) * SLAB_N])


def mlp_stream(w1, w2):
    up = w1.rearrange("(k p) n -> p k n", p=P)
    down = w2.rearrange("(k p) n -> p k n", p=P)

    def half(chunk, part, h):
        if part == 0:
            return up[:, h * SLAB_K:(h + 1) * SLAB_K, ds(chunk * FF_CHUNK, FF_CHUNK)]
        return down[:, ds(chunk * SLAB_K, SLAB_K), h * SLAB_N:(h + 1) * SLAB_N]

    s = Stream(2 * (D_FF // FF_CHUNK), lambda n, h: half(n // 2, n % 2, h))
    s.chunk_half = half
    return s


def load_half(K, sp, g, h, src, first=False):
    if not first:
        sp.wait_ge(K.lo_done.h, 2 * (g - 1) + h + 1)
    sp.dma_start(K.raw[h][:, :, :], src).then_inc(K.raw_loaded[h].h, 16)


def split_hi(K, act, g, h):
    act.wait_ge(K.raw_loaded[h].h, 16 * (g + 1))
    act.wait_ge(K.w_used.h, 2 * (g - 1) + h + 1)
    act.activation(K.w_hi[h][:, :, :], K.raw[h][:, :, :], ACT.Copy).then_inc(K.hi_done.h, 1)


def split_lo(K, dve, g, h):
    dve.wait_ge(K.hi_done.h, 2 * g + h + 1)
    dve.tensor_tensor(K.w_lo[h][:, :, :], K.raw[h][:, :, :], K.w_hi[h][:, :, :].bitcast(F32),
                      ALU.subtract).then_inc(K.lo_done.h, 1)


def stream_loads(K, sp, stage):
    g0, s, nxt = stage.g0, stage.stream, stage.next_stream
    if s.count > 2:
        if stage.chunked:
            with sp.Fori(1, s.count // 2) as c:
                for part in range(2):
                    for h in range(2):
                        load_half(K, sp, g0 + 2 * c + part, h, s.chunk_half(c, part, h))
        elif stage.unrolled:
            for n in range(2, s.count):
                for h in range(2):
                    load_half(K, sp, g0 + n, h, s.half(n, h))
        else:
            with sp.Fori(2, s.count) as n:
                for h in range(2):
                    load_half(K, sp, g0 + n, h, s.half(n, h))
    if nxt is not None:
        for n in range(2):
            for h in range(2):
                load_half(K, sp, g0 + s.count + n, h, nxt.half(n, h))


def product(pe, out, hi_a, lo_a, hi_w, lo_w, first, last):
    pe.matmul(out, hi_a, hi_w, start=first, stop=False)
    pe.matmul(out, hi_a, lo_w, start=False, stop=False)
    return pe.matmul(out, lo_a, hi_w, start=False, stop=last)


class Stage:
    def __init__(self, K, stream, next_stream, chunked=False, unrolled=False):
        self.g0, self.stream, self.next_stream = K.slabs, stream, next_stream
        self.chunked, self.unrolled = chunked, unrolled
        K.slabs += stream.count
        self.last = next_stream is None


def ahead_loop(eng, stage, body):
    n = stage.stream.count // (2 if stage.chunked else 1)
    if stage.unrolled:
        for i in range(n):
            body(i, not (stage.last and i == n - 1))
        return
    loops = n - 1 if stage.last else n
    if loops > 0:
        with eng.Fori(0, loops) as i:
            body(i, True)
    if stage.last:
        body(n - 1, False)


def gemm_stage(K, stream, nxt, k_tiles, tiles, evacuate, evac_on, hi_t=None, lo_t=None):
    nc = K.nc
    hi_t = hi_t or K.hT_hi
    lo_t = lo_t or K.hT_lo
    unrolled = k_tiles > 2 * SLAB_K
    st = Stage(K, stream, nxt, unrolled=unrolled)
    per = k_tiles // (2 * SLAB_K)
    nt = len(tiles)
    freed = K.scaled if evac_on == "dve" else K.evacuated
    mm0, ev0 = K.mm_done.n, freed.n

    def tile_done(eng, n, block_n, j):
        if j < nt - 1:
            eng.wait_ge(K.mm_done.h, mm0 + (nt - 1) * block_n + j + 1)
        else:
            eng.wait_ge(K.w_used.h, 2 * (st.g0 + n) + 2)

    def pe_body(n, _):
        part = n % per if unrolled else 0
        block_n = n // per if unrolled else n
        for h in range(2):
            pe = nc.tensor
            pe.wait_ge(K.lo_done.h, 2 * (st.g0 + n) + h + 1)
            for j, t in enumerate(tiles):
                first, last = part == 0 and h == 0, part == per - 1 and h == 1
                if first:
                    pe.wait_ge(freed.h, ev0 + nt * (block_n - 1) + j + 1)
                for k in range(SLAB_K):
                    kk = part * 2 * SLAB_K + h * SLAB_K + k
                    mm = product(pe, K.bank[j][:, :], hi_t[:, kk, t * P:(t + 1) * P], lo_t[:, kk, t * P:(t + 1) * P],
                                 K.w_hi[h][:, k, :], K.w_lo[h][:, k, :], first and k == 0, last and k == SLAB_K - 1)
                if last and j < nt - 1:
                    mm.then_inc(K.mm_done.h, 1)
            mm.then_inc(K.w_used.h, 1)

    def reads(eng, n, who):
        if who != evac_on:
            return
        part = n % per if unrolled else per - 1
        block_n = n // per if unrolled else n
        if part != per - 1:
            return
        for j, t in enumerate(tiles):
            tile_done(eng, n, block_n, j)
            evacuate(eng, K.scaled.n + nt * block_n + j, block_n, t, K.bank[j], j)

    with nc.Block() as block:
        @block.sync
        def _(sp):
            stream_loads(K, sp, st)

        @block.scalar
        def _(act):
            def body(n, ahead):
                if ahead:
                    split_hi(K, act, st.g0 + n + 1, 0)
                reads(act, n, "act")
                if ahead:
                    split_hi(K, act, st.g0 + n + 1, 1)
            ahead_loop(act, st, body)

        @block.vector
        def _(dve):
            def body(n, ahead):
                if ahead:
                    split_lo(K, dve, st.g0 + n + 1, 0)
                reads(dve, n, "dve")
                if ahead:
                    split_lo(K, dve, st.g0 + n + 1, 1)
            ahead_loop(dve, st, body)

        if evac_on == "dve":
            @block.gpsimd
            def _(pool):
                blocks = stream.count // per
                with pool.Fori(0, blocks) as n:
                    for j, t in enumerate(tiles):
                        residual_add(K, pool, K.scaled.n + nt * n + j, t, n, j)

        @block.tensor
        def _(pe):
            if unrolled:
                for n in range(stream.count):
                    pe_body(n, None)
            else:
                with pe.Fori(0, stream.count) as n:
                    pe_body(n, None)
    K.mm_done.n += (nt - 1) * (stream.count // per)
    freed.n += nt * (stream.count // per)


def copy_out(K, dst, act, _, n, t, bank, j):
    act.activation(dst[:, t, ds(n * SLAB_N, SLAB_N)], bank[:, :], ACT.Copy).then_inc(K.evacuated.h, 1)


def gate_out(K, dve, count, n, t, bank, j):
    dve.wait_ge(K.added.h, count - 1)
    cls = 0 if t < LAT_TILES else 1
    dve.tensor_tensor(K.scaled_buf[:, j % 2, :], bank[:, :], K.gate[:, cls, ds(n * SLAB_N, SLAB_N)], ALU.mult)\
       .then_inc(K.scaled.h, 1)


def residual_add(K, pool, count, t, n, j):
    pool.wait_ge(K.scaled.h, count + 1)
    x = K.x[:, t, ds(n * SLAB_N, SLAB_N)]
    pool.tensor_tensor(x, x, K.scaled_buf[:, j % 2, :], ALU.add).then_inc(K.added.h, 1)


def mlp_stage(K, stream, nxt, tiles):
    nc = K.nc
    st = Stage(K, stream, nxt, chunked=True)
    nt = len(tiles)
    mm0, tr0, re0, sq0, uh0, ul0, sc0 = (s.n for s in (
        K.mm_done, K.turned, K.relu_done, K.sq_done, K.u_hi_done, K.u_lo_done, K.scaled))
    chunks = D_FF // FF_CHUNK

    def tile_done(eng, c, which, j):
        if j < nt - 1:
            eng.wait_ge(K.mm_done.h, mm0 + (nt - 1) * (3 * c + which) + j + 1)
        else:
            eng.wait_ge(K.w_used.h, 2 * (st.g0 + 2 * c) + 2 + which)

    with nc.Block() as block:
        @block.sync
        def _(sp):
            stream_loads(K, sp, st)

        @block.scalar
        def _(act):
            def square(c, j):
                act.wait_ge(K.turned.h, tr0 + nt * c + j + 1)
                act.wait_ge(K.u_lo_done.h, ul0 + nt * c + j - 1)
                act.activation(K.sq[:, j % 2, :], K.bank[6 + j % 2][:, :], ACT.Square).then_inc(K.sq_done.h, 1)

            def body(c, ahead):
                g = st.g0 + 2 * c
                split_hi(K, act, g + 1, 0)
                for j in range(nt):
                    tile_done(act, c, 0, j)
                    act.wait_ge(K.turned.h, tr0 + nt * c + j - 1)
                    act.activation(K.relu[:, j % 2, :], K.bank[j][:, :], ACT.Relu).then_inc(K.relu_done.h, 1)
                    if j:
                        square(c, j - 1)
                square(c, nt - 1)
                split_hi(K, act, g + 1, 1)
                if ahead:
                    split_hi(K, act, g + 2, 0)
                    split_hi(K, act, g + 2, 1)
            ahead_loop(act, st, body)

        @block.vector
        def _(dve):
            def parts(c, j):
                t = tiles[j]
                view = lambda u: u[:, :, t * P:(t + 1) * P]
                square = K.sq[:, j % 2, :].rearrange("p (k t) -> p k t", k=SLAB_K)
                dve.wait_ge(K.sq_done.h, sq0 + nt * c + j + 1)
                dve.wait_ge(K.w_used.h, 2 * (st.g0 + 2 * c) - 1 + 1)
                dve.tensor_copy(view(K.uT_hi), square).then_inc(K.u_hi_done.h, 1)
                dve.wait_ge(K.u_hi_done.h, uh0 + nt * c + j + 1)
                dve.tensor_tensor(view(K.uT_lo), square, view(K.uT_hi).bitcast(F32), ALU.subtract)\
                   .then_inc(K.u_lo_done.h, 1)

            def body(c, ahead):
                g = st.g0 + 2 * c
                split_lo(K, dve, g + 1, 0)
                for j in range(nt):
                    parts(c, j)
                split_lo(K, dve, g + 1, 1)
                for h in range(2):
                    for j, t in enumerate(tiles):
                        tile_done(dve, c, 1 + h, j)
                        gate_out(K, dve, sc0 + 2 * nt * c + h * nt + j, h, t, K.bank[j], j)
                    if ahead:
                        split_lo(K, dve, g + 2, h)
            ahead_loop(dve, st, body)

        @block.gpsimd
        def _(pool):
            with pool.Fori(0, chunks) as c:
                for h in range(2):
                    for j, t in enumerate(tiles):
                        residual_add(K, pool, sc0 + 2 * nt * c + h * nt + j, t, h, j)

        @block.tensor
        def _(pe):
            def turn(c, j):
                pe.wait_ge(K.relu_done.h, re0 + nt * c + j + 1)
                pe.wait_ge(K.sq_done.h, sq0 + nt * c + j - 1)
                for k in range(SLAB_K):
                    mm = pe.transpose(K.bank[6 + j % 2][:, k * P:(k + 1) * P], K.relu[:, j % 2, k * P:(k + 1) * P], K.ident[:, :])
                mm.then_inc(K.turned.h, 1)

            with pe.Fori(0, chunks) as c:
                g = st.g0 + 2 * c
                for h in range(2):
                    pe.wait_ge(K.lo_done.h, 2 * g + h + 1)
                    for j, t in enumerate(tiles):
                        if h == 0:
                            pe.wait_ge(K.scaled.h, sc0 + 2 * nt * (c - 1) + nt + j + 1)
                        for k in range(SLAB_K):
                            kk = h * SLAB_K + k
                            mm = product(pe, K.bank[j][:, :], K.hT_hi[:, kk, t * P:(t + 1) * P],
                                         K.hT_lo[:, kk, t * P:(t + 1) * P], K.w_hi[h][:, k, :], K.w_lo[h][:, k, :],
                                         kk == 0, kk == KD - 1)
                        if j == nt - 1:
                            mm.then_inc(K.w_used.h, 1)
                        elif h == 1:
                            mm.then_inc(K.mm_done.h, 1)
                        if h == 1 and j:
                            turn(c, j - 1)
                for h in range(2):
                    pe.wait_ge(K.lo_done.h, 2 * (g + 1) + h + 1)
                    for j, t in enumerate(tiles):
                        if h == 0:
                            pe.wait_ge(K.u_lo_done.h, ul0 + nt * c + j + 1)
                            pe.wait_ge(K.relu_done.h, re0 + nt * c + j + 1)
                        else:
                            pe.wait_ge(K.scaled.h, sc0 + 2 * nt * c + j + 1)
                        for k in range(SLAB_K):
                            mm = product(pe, K.bank[j][:, :], K.uT_hi[:, k, t * P:(t + 1) * P],
                                         K.uT_lo[:, k, t * P:(t + 1) * P], K.w_hi[h][:, k, :], K.w_lo[h][:, k, :],
                                         k == 0, k == SLAB_K - 1)
                        mm.then_inc((K.w_used if j == nt - 1 else K.mm_done).h, 1)
                        if h == 0 and j == 0:
                            turn(c, nt - 1)
    K.mm_done.n += 3 * (nt - 1) * chunks
    K.scaled.n += 2 * nt * chunks
    for s in (K.turned, K.relu_done, K.sq_done, K.u_hi_done, K.u_lo_done):
        s.n += nt * chunks


def operand_stage(K, src, k_tiles, ctx, dst_hi, dst_lo, scale=None, bias=None, rms_of=None, feat=None):
    nc = K.nc
    classes = [(0, 0, LAT_TILES)] + ([(1, LAT_TILES, CTX_TILES)] if ctx else [])
    tiles = TOK_TILES if ctx else LAT_TILES
    cols = tiles * P
    feat = feat or K.feat
    nr0, tr0, ft0, fh0, fl0, rs0 = (s.n for s in (K.normed, K.turned, K.feat_done, K.feat_hi, K.feat_lo, K.rstd_done))
    def lo_parts(dve):
        for k in range(k_tiles):
            dve.wait_ge(K.feat_hi.h, fh0 + k + 1)
            dve.tensor_tensor(dst_lo[:, k, 0:cols], feat[:, k % 2, 0:cols], dst_hi[:, k, 0:cols].bitcast(F32),
                              ALU.subtract).then_inc(K.feat_lo.h, 1)

    with nc.Block() as block:
        if rms_of is not None:
            @block.vector
            def _(dve):
                for t in range(tiles):
                    dve.wait_ge(K.rstd_done.h, rs0 + 1)
                    dve.tensor_scalar(K.xhat[:, t, :], K.x[:, t, :], K.rstd[:, t:t + 1], None, ALU.mult)\
                       .then_inc(K.normed.h, 1)
                lo_parts(dve)
        else:
            @block.vector
            def _(dve):
                lo_parts(dve)

        @block.gpsimd
        def _(pool):
            for k in range(k_tiles):
                pool.wait_ge(K.feat_done.h, ft0 + len(classes) * (k + 1))
                pool.tensor_copy(dst_hi[:, k, 0:cols], feat[:, k % 2, 0:cols]).then_inc(K.feat_hi.h, 1)

        @block.scalar
        def _(act):
            if rms_of is not None:
                link = Chain(act, K.act_chain)
                for t in range(tiles):
                    ins = act.activation(feat[:, :, :].rearrange("p a b -> p (a b)")[:, 0:D], K.x[:, t, :], ACT.Square,
                                         accum_out=K.ssum[:, t:t + 1])
                    link(ins)
                link(act.activation(K.lnms[:, 0:tiles], K.ssum[:, 0:tiles], ACT.Ln, bias=K.eps6[:, 0:1], scale=1.0 / D))
                act.activation(K.rstd[:, 0:tiles], K.lnms[:, 0:tiles], ACT.Exp, scale=-0.5).then_inc(K.rstd_done.h, 1)
                act.wait_ge(K.rstd_done.h, rs0 + 1)
                K.act_chain.n += link.k
            for k in range(k_tiles):
                for c, (cls, t0, n) in enumerate(classes):
                    act.wait_ge(K.turned.h, tr0 + len(classes) * k + c + 1)
                    if k >= 2:
                        act.wait_ge(K.feat_lo.h, fl0 + k - 1)
                    bank = K.bank[2 * (k % 4) + c]
                    out = feat[:, k % 2, t0 * P:(t0 + n) * P]
                    if scale is None:
                        ins = act.activation(out, bank[:, 0:n * P], ACT.Copy)
                    else:
                        b = {} if bias is None else {"bias": bias(k, cls)}
                        ins = act.activation(out, bank[:, 0:n * P], ACT.Identity, scale=scale(k, cls), **b)
                    ins.then_inc(K.feat_done.h, 1)

        @block.tensor
        def _(pe):
            if rms_of is not None:
                pe.wait_ge(K.normed.h, nr0 + tiles)
            for k in range(k_tiles):
                for c, (cls, t0, n) in enumerate(classes):
                    if k >= 4:
                        pe.wait_ge(K.feat_done.h, ft0 + len(classes) * (k - 4) + c + 1)
                    for t in range(n):
                        mm = pe.transpose(K.bank[2 * (k % 4) + c][:, t * P:(t + 1) * P], src(t0 + t, k), K.ident[:, :])
                    mm.then_inc(K.turned.h, 1)
    if rms_of is not None:
        K.normed.n += tiles
        K.rstd_done.n += 1
    K.turned.n += len(classes) * k_tiles
    K.feat_done.n += len(classes) * k_tiles
    K.feat_hi.n += k_tiles
    K.feat_lo.n += k_tiles


def mod_stage(K, w_mod, b_mod, c, c_ctx, *more):
    nc = K.nc
    rows = w_mod.rearrange("(k p) n -> p k n", p=P)
    steps, slots = 4, 6
    vectors = (c, c_ctx, b_mod) + more
    n_rows = sum(v.shape[0] for v in vectors) // P
    ld0 = [s.n for s in K.mod_loaded]
    us0, mr0, ro0, tr0, cn0, sm0 = K.mod_used.n, K.mod_rows.n, K.row_out.n, K.turned.n, K.c_done.n, K.small_loaded.n
    dc0, de0 = K.dve_chain.n, K.mod_cols.n
    with nc.Block() as block:
        @block.sync
        def _(sp):
            row = 0
            for v in vectors:
                n = v.shape[0] // P
                sp.dma_start(K.vec_in[row:row + n, :], v.rearrange("(k p) -> k p", p=P)).then_inc(K.small_loaded.h, 16)
                row += n
            with sp.Fori(0, steps) as i:
                for s in range(slots):
                    h, b = s % 2, s // 2
                    if h == 0:
                        sp.wait_ge(K.mod_used.h, us0 + 3 * (i - 1) + b + 1)
                    else:
                        sp.wait_ge(K.mod_rows.h, mr0 + 3 * (i - 1) + b + 1)
                    sp.dma_start(K.mod_raw[s][:, :, :], rows[:, h * SLAB_K:(h + 1) * SLAB_K, ds((3 * i + b) * SLAB_N, SLAB_N)])\
                      .then_inc(K.mod_loaded[s].h, 16)

        @block.scalar
        def _(act):
            act.wait_ge(K.c_done.h, cn0 + 1)
            act.activation(K.cexp[:, :], K.vecs[:, 0:2 * KD], ACT.Exp, scale=-1.0).then_inc(K.c_done.h, 1)
            with act.Fori(0, steps) as i:
                for b in range(3):
                    act.wait_ge(K.mod_rows.h, mr0 + 3 * i + b + 1)
                    act.wait_ge(K.turned.h, tr0 + 1 + 3 * i + b)
                    act.activation(K.mod_row[0:2, :], K.bank[b][0:2, :], ACT.Copy).then_inc(K.row_out.h, 1)

        @block.vector
        def _(dve):
            link = Chain(dve, K.dve_chain)
            dve.wait_ge(K.turned.h, tr0 + 1)
            dve.tensor_copy(K.vecs[:, 0:n_rows], K.bank[6][:, 0:n_rows]).then_inc(K.c_done.h, 1)
            dve.wait_ge(K.c_done.h, cn0 + 2)
            link(dve.tensor_scalar(K.cexp[:, :], K.cexp[:, :], 1.0, None, ALU.add))
            link(dve.reciprocal(K.cexp[:, :], K.cexp[:, :]))
            dve.tensor_tensor(K.cT[:, :, :].rearrange("p k c -> p c k"), K.vecs[:, 0:2 * KD].rearrange("p (c k) -> p c k", c=2),
                              K.cexp[:, :].rearrange("p (c k) -> p c k", c=2), ALU.mult).then_inc(K.c_done.h, 1)
            with dve.Fori(0, steps) as i:
                for b in range(3):
                    dve.wait_ge(K.turned.h, tr0 + 1 + 3 * i + b + 1)
                    n = 3 * i + b
                    dve.tensor_tensor(K.modT[:, ds(n * 4, 4), :], K.bank[3 + b][:, 0:8].rearrange("p (j c) -> p j c", c=2),
                                      K.vecs[:, ds(n * 4 + 2 * KD, 4)].unsqueeze(2).to_broadcast([P, 4, 2]), ALU.add)\
                       .then_inc(K.mod_cols.h, 1)
            K.dve_chain.n += link.k

        @block.tensor
        def _(pe):
            pe.wait_ge(K.small_loaded.h, sm0 + 16 * len(vectors))
            pe.transpose(K.bank[6][:, 0:n_rows], K.vec_in[0:n_rows, :], K.ident[0:n_rows, 0:n_rows]).then_inc(K.turned.h, 1)
            pe.wait_ge(K.c_done.h, cn0 + 3)
            with pe.Fori(0, steps) as i:
                for b in range(3):
                    pe.wait_ge(K.row_out.h, ro0 + 3 * (i - 1) + b + 1)
                    for h in range(2):
                        s = 2 * b + h
                        pe.wait_ge(K.mod_loaded[s].h, ld0[s] + 16 * (i + 1))
                        for k in range(SLAB_K):
                            mm = pe.matmul(K.bank[b][0:2, :], K.cT[:, h * SLAB_K + k, :], K.mod_raw[s][:, k, :],
                                           start=h == 0 and k == 0, stop=h == 1 and k == SLAB_K - 1)
                        if h == 0:
                            mm.then_inc(K.mod_used.h, 1)
                    mm.then_inc(K.mod_rows.h, 1)
                    pe.wait_ge(K.row_out.h, ro0 + 3 * i + b + 1)
                    pe.wait_ge(K.mod_cols.h, de0 + 3 * (i - 1) + b + 1)
                    for j in range(4):
                        mm = pe.matmul(K.bank[3 + b][:, 2 * j:2 * j + 2], K.mod_row[0:2, j * P:(j + 1) * P], K.ident[0:2, 0:2],
                                       start=True, stop=True)
                    mm.then_inc(K.turned.h, 1)
    for s in K.mod_loaded:
        s.n += 16 * steps
    K.mod_used.n += 12
    K.mod_cols.n += 12
    K.mod_rows.n += 12
    K.row_out.n += 12
    K.turned.n += 13
    K.c_done.n += 3
    K.small_loaded.n += 16 * len(vectors)


def gate_stage(K, which, classes=2, alpha=None):
    nc = K.nc
    mm0, ev0 = K.mm_done.n, K.evacuated.n
    with nc.Block() as block:
        @block.tensor
        def _(pe):
            for cls in range(classes):
                for k in range(KD):
                    mm = pe.matmul(K.bank[2 * cls + k // 4][:, (k % 4) * P:(k % 4 + 1) * P],
                                   K.modT[:, which * KD + k, cls:cls + 1].to_broadcast([P, P]), K.ident[:, :],
                                   start=True, stop=True)
                mm.then_inc(K.mm_done.h, 1)

        @block.scalar
        def _(act):
            for cls in range(classes):
                act.wait_ge(K.mm_done.h, mm0 + cls + 1)
                for half in range(2):
                    act.activation(K.gate[:, cls, half * 512:(half + 1) * 512], K.bank[2 * cls + half][:, :], ACT.Copy)

        if alpha is not None:
            @block.vector
            def _(dve):
                for t in range(LAT_TILES if classes == 1 else TOK_TILES):
                    dve.tensor_scalar(K.x[:, t, :], K.x[:, t, :], alpha, None, ALU.mult)
    K.mm_done.n += classes


def scale_stage(K, part, gain_at=None):
    with K.nc.Block() as block:
        @block.vector
        def _(dve):
            link = Chain(dve, K.dve_chain)
            link(dve.tensor_scalar(K.mod_scale[:, :, :], K.modT[:, part * KD:(part + 1) * KD, :], 1.0, None, ALU.add))
            if gain_at is not None:
                dve.tensor_tensor(K.mod_scale[:, :, :], K.mod_scale[:, :, :],
                                  K.vecs[:, gain_at:gain_at + KD].unsqueeze(2).to_broadcast([P, KD, 2]), ALU.mult)
            K.dve_chain.n += link.k


def head_norm_stage(K, src, heads, dim, tiles, gains=None, rope=None):
    nc = K.nc
    width = heads * dim
    sq0, ss0, rs0, nm0, ga0, t20, sm0 = (s.n for s in (
        K.sq_done, K.sums_done, K.rstd_done, K.normed, K.gained, K.swapped, K.small_loaded))
    cols = lambda t: src[:, t, 0:width]
    by_head = lambda ap: ap.rearrange("p (h d) -> p h d", d=dim)
    loads = (2 if gains else 0) + (2 if rope else 0)
    def rotate(dve, i, t):
        x = by_head(cols(t))
        cos = K.rope_cos[:, t, :].unsqueeze(1).to_broadcast([P, heads, dim])
        if i == 0:
            dve.wait_ge(K.small_loaded.h, sm0 + 16 * loads)
        dve.wait_ge(K.swapped.h, t20 + i + 1)
        dve.tensor_tensor(x, x, cos, ALU.mult).then_inc(K.dve_chain.h, 1)
        dve.wait_ge(K.dve_chain.h, K.dve_chain.n + i + 1)
        dve.tensor_tensor(cols(t), cols(t), K.head_swap[:, i % 2, 0:width], ALU.add).then_inc(K.rotated.h, 1)

    with nc.Block() as block:
        if loads:
            @block.sync
            def _(sp):
                if gains:
                    for i, g in enumerate(gains):
                        sp.dma_start(K.head_gain[:, i, :], g.partition_broadcast(P)).then_inc(K.small_loaded.h, 16)
                if rope:
                    sp.dma_start(K.rope_cos[:, :, :], rope[0]).then_inc(K.small_loaded.h, 16)
                    sp.dma_start(K.rope_sin[:, :, :], rope[1]).then_inc(K.small_loaded.h, 16)

        @block.scalar
        def _(act):
            link = Chain(act, K.act_chain)

            def rstd(i):
                act.wait_ge(K.sums_done.h, ss0 + i + 1)
                link(act.activation(K.head_ln[:, i % 2, 0:heads], K.head_ss[:, i % 2, 0:heads], ACT.Ln,
                                    bias=K.eps6[:, 0:1], scale=1.0 / dim))
                act.activation(K.head_rstd[:, i % 2, 0:heads], K.head_ln[:, i % 2, 0:heads], ACT.Exp, scale=-0.5)\
                   .then_inc(K.rstd_done.h, 1)

            for i, t in enumerate(tiles):
                if i >= 2:
                    act.wait_ge(K.sums_done.h, ss0 + i - 1)
                act.activation(K.head_sq[:, i % 2, 0:width], cols(t), ACT.Square).then_inc(K.sq_done.h, 1)
                if i:
                    rstd(i - 1)
            rstd(len(tiles) - 1)
            K.act_chain.n += link.k

        @block.vector
        def _(dve):
            def sums(i):
                dve.wait_ge(K.sq_done.h, sq0 + i + 1)
                if i >= 2:
                    dve.wait_ge(K.rstd_done.h, rs0 + i - 1)
                dve.tensor_reduce(K.head_ss[:, i % 2, 0:heads], by_head(K.head_sq[:, i % 2, 0:width]), AX.X, ALU.add)\
                   .then_inc(K.sums_done.h, 1)

            sums(0)
            for i, t in enumerate(tiles):
                if i + 1 < len(tiles):
                    sums(i + 1)
                dve.wait_ge(K.rstd_done.h, rs0 + i + 1)
                x = by_head(cols(t))
                dve.tensor_tensor(x, x, K.head_rstd[:, i % 2, 0:heads].unsqueeze(2).to_broadcast([P, heads, dim]), ALU.mult)\
                   .then_inc(K.normed.h, 1)
                if rope and t < LAT_TILES:
                    rotate(dve, i, t)

        if gains:
            @block.gpsimd
            def _(pool):
                link = Chain(pool, K.pool_chain)
                pool.wait_ge(K.small_loaded.h, sm0 + 16 * loads)
                for i, t in enumerate(tiles):
                    pool.wait_ge(K.normed.h, nm0 + i + 1)
                    x = cols(t).rearrange("p (a h d) -> p a h d", a=2, d=dim)
                    gain = K.head_gain[:, :, :].unsqueeze(2).to_broadcast([P, 2, heads // 2, dim])
                    link(pool.tensor_tensor(x, x, gain, ALU.mult))
                    if rope and t < LAT_TILES:
                        if i >= 2:
                            pool.wait_ge(K.rotated.h, K.rotated.n + i - 1)
                        swap_products(K, pool, by_head(cols(t)), by_head(K.head_swap[:, i % 2, 0:width]), t, heads, "pairs")
                K.pool_chain.n += link.k
    n = len(tiles)
    for s in (K.sq_done, K.sums_done, K.rstd_done, K.normed):
        s.n += n
    if rope:
        for s in (K.swapped, K.rotated, K.dve_chain):
            s.n += LAT_TILES
    K.small_loaded.n += 16 * loads


def swap_products(K, pool, x, out, t, heads, kind):
    if kind == "pairs":
        a = lambda ap: (ap[:, :, 0::2], ap[:, :, 1::2])
        sin = K.rope_sin[:, t, :]
        s = [sin[:, i::2].unsqueeze(1).to_broadcast([P, heads, HEAD_DIM // 2]) for i in range(2)]
    else:
        q = HEAD_DIM // 4
        halves = lambda ap: ap.rearrange("p h (a b d) -> p h a b d", a=2, b=2)
        a = lambda ap: (halves(ap)[:, :, :, 0, :], halves(ap)[:, :, :, 1, :])
        sin = K.rope_sin[:, t, :].rearrange("p (a b d) -> p a b d", a=2, b=2)
        s = [sin[:, :, i, :].unsqueeze(1).to_broadcast([P, heads, 2, q]) for i in range(2)]
    (x0, x1), (o0, o1) = a(x), a(out)
    pool.tensor_tensor(o0, x1, s[0], ALU.mult)
    pool.tensor_tensor(o1, x0, s[1], ALU.mult).then_inc(K.swapped.h, 1)


def rope_stage(K, heads, rope):
    nc = K.nc
    width = heads * HEAD_DIM
    sm0, t20, ro0 = K.small_loaded.n, K.swapped.n, K.rotated.n
    by_head = lambda ap: ap.rearrange("p (h d) -> p h d", d=HEAD_DIM)
    with nc.Block() as block:
        @block.sync
        def _(sp):
            sp.dma_start(K.rope_cos[:, :, :], rope[0]).then_inc(K.small_loaded.h, 16)
            sp.dma_start(K.rope_sin[:, :, :], rope[1]).then_inc(K.small_loaded.h, 16)

        @block.gpsimd
        def _(pool):
            pool.wait_ge(K.small_loaded.h, sm0 + 32)
            for t in range(LAT_TILES):
                if t >= 2:
                    pool.wait_ge(K.rotated.h, ro0 + t - 1)
                swap_products(K, pool, by_head(K.qkv2[:, t, 0:width]), by_head(K.head_swap[:, t % 2, 0:width]), t, heads, "halves")

        @block.vector
        def _(dve):
            link = Chain(dve, K.dve_chain)
            dve.wait_ge(K.small_loaded.h, sm0 + 32)
            for t in range(LAT_TILES):
                cos = K.rope_cos[:, t, :].unsqueeze(1).to_broadcast([P, heads, HEAD_DIM])
                link(dve.tensor_tensor(by_head(K.roped[:, t, :]), by_head(K.qkv2[:, t, 0:width]), cos, ALU.mult))
                dve.wait_ge(K.swapped.h, t20 + t + 1)
                dve.tensor_tensor(K.roped[:, t, :], K.roped[:, t, :], K.head_swap[:, t % 2, 0:width], ALU.add)\
                   .then_inc(K.rotated.h, 1)
            K.dve_chain.n += link.k
    K.small_loaded.n += 32
    K.swapped.n += LAT_TILES
    K.rotated.n += LAT_TILES


class Unit:

    def __init__(self, tile, keys, masks=None, unrotated=0):
        self.tile, self.keys, self.masks, self.unrotated = tile, keys, masks or {}, unrotated
        self.width = len(keys) * P

    def segments(self):
        runs = []
        for i, kt in enumerate(self.keys):
            if runs and i % 4 and self.keys[i - 1] == kt - 1 and i not in self.masks and i - 1 not in self.masks \
                    and i != self.unrotated:
                runs[-1][1] += 1
            else:
                runs.append([i, 1])
        return runs


def attention_stage(K, units, steps, pairs, stage_heads, values, out, diff=False, rel_bias=False, sink=None, unrotated=False):
    nc = K.nc
    nu = len(units)
    X = pairs * nu * 2
    U = pairs * nu
    T = U if diff else X
    n_src = 3 if unrotated else 2
    S0 = pairs * n_src
    base = {s: s.n for s in (K.staged, K.src_turned, K.src_read, K.s_done, K.nm_done, K.p_done, K.w_done, K.pt_done,
                             K.pt_read[0], K.pt_read[1], K.o_done, K.o_read, K.g_done, K.g_ready)}
    at = lambda s, i, per, k: base[s] + i * per + k + 1
    S = [K.psum[:, 0:2, :].rearrange("p a b -> p (a b)"), K.psum[:, 2:4, :].rearrange("p a b -> p (a b)")]
    PT = [K.psum[:, 4:6, :].rearrange("p a b -> p (a b)"), K.psum[:, 6:8, :].rearrange("p a b -> p (a b)")]
    TOK = N_TOK
    ms = (0,) if diff else (0, 1)

    def o_bank(x):
        return PT[x % 2][:, TOK:TOK + P]

    with nc.Block() as block:
        @block.gpsimd
        def _(pool):
            with pool.Fori(0, steps) as i:
                for pi in range(pairs):
                    pool.wait_ge(K.src_turned.h, at(K.src_turned, i, S0, pi * n_src - 1))
                    stage_heads(pool, i, pi)

        @block.tensor
        def _(pe):
            def turn_sources(i, pi):
                pe.wait_ge(K.staged.h, at(K.staged, i, pairs, pi))
                for q in range(n_src):
                    x = pi * n_src + q
                    bank = PT[q % 2]
                    if q == 2:
                        pe.wait_ge(K.src_read.h, at(K.src_read, i, S0, x - 2))
                    else:
                        for m in ms:
                            pe.wait_ge(K.pt_read[m].h, at(K.pt_read[m], i, U, pi * nu - 1))
                        pe.wait_ge(K.o_read.h, at(K.o_read, i, U, pi * nu - 1))
                    for t in range(TOK_TILES):
                        mm = pe.transpose(bank[:, t * P:(t + 1) * P], K.heads[q][:, t, :], K.ident[:, :])
                    mm.then_inc(K.src_turned.h, 1)

            def bias_tiles(i, pi):
                pe.wait_ge(K.p_done.h, at(K.p_done, i, X, pi * nu * 2 - 1))
                flat = K.psum[:, 0:4, :].rearrange("p a b -> p (a b)")
                for kc in range(GRID_W):
                    mm = pe.matmul(flat[:, kc * 32:kc * 32 + 32], K.shift[:, GRID_W - 1 - kc:3 * GRID_W - 1 - kc],
                                   K.rpbT[:, ds(2 * (pairs * i + pi), 2), :], start=True, stop=True)
                    if kc % 16 == 15:
                        mm.then_inc(K.g_done.h, 1)

            def scores(i, pi, u, m):
                un, x = units[u], (pi * nu + u) * 2 + m
                if u == 0 and m == 0:
                    pe.wait_ge(K.src_read.h, at(K.src_read, i, S0, pi * n_src + n_src - 1))
                    if rel_bias:
                        pe.wait_ge(K.g_ready.h, at(K.g_ready, i, 4 * pairs, 4 * pi + 3))
                pe.wait_ge(K.p_done.h, at(K.p_done, i, X, x - 2))
                rows = slice(m * HEAD_DIM, (m + 1) * HEAD_DIM)
                qcols = slice(un.tile * P, (un.tile + 1) * P)
                for j, n in un.segments():
                    q = K.headsT[2] if unrotated and j < un.unrotated else K.headsT[0]
                    o = S[m][:, j * P:(j + n) * P]
                    kt = un.keys[j]
                    masked = j in un.masks or (rel_bias and j == 0)
                    mm = pe.matmul(o, q[rows, qcols], K.headsT[1][rows, kt * P:(kt + n) * P], start=True, stop=not masked)
                    if j in un.masks:
                        mm = pe.matmul(o, K.ident[:, :], un.masks[j], start=False, stop=True)
                    elif masked:
                        first = N_ROWS - 1 - 2 * un.tile
                        g = K.G[:, :, m, first:first + N_ROWS].rearrange("p c r -> p r c")
                        mm = pe.matmul(o, K.ident[:, :], g, start=False, stop=True)
                mm.then_inc(K.s_done.h, 1)

            def turn(i, pi, u, m):
                un = units[u]
                x = pi * nu + u if diff else (pi * nu + u) * 2 + m
                src = K.w_mat if diff else K.p_mat[m]
                if diff:
                    pe.wait_ge(K.w_done.h, at(K.w_done, i, U, x))
                else:
                    pe.wait_ge(K.p_done.h, at(K.p_done, i, X, x))
                pe.wait_ge(K.pt_read[m].h, at(K.pt_read[m], i, U, pi * nu + u - (2 if diff else 1)))
                pe.wait_ge(K.o_read.h, at(K.o_read, i, U, pi * nu + u - (2 if diff else 1)))
                for j in range(len(un.keys)):
                    mm = pe.transpose(PT[x % 2][:, j * P:(j + 1) * P], src[:, j * P:(j + 1) * P], K.ident[:, :])
                mm.then_inc(K.pt_done.h, 1)

            def weighted(i, pi, u, m):
                un = units[u]
                x = pi * nu + u if diff else (pi * nu + u) * 2 + m
                pe.wait_ge(K.pt_read[m].h, at(K.pt_read[m], i, U, pi * nu + u))
                w = P if diff else HEAD_DIM
                o = o_bank(x)[:, 0:w]
                for j, kt in enumerate(un.keys):
                    mm = pe.matmul(o, K.pT_mat[x % 2][:, j * P:(j + 1) * P], values(i, pi, m, kt), start=j == 0,
                                   stop=j == len(un.keys) - 1)
                if diff or m == 1:
                    mm.then_inc(K.o_done.h, 1)

            with pe.Fori(0, steps) as i:
                for pi in range(pairs):
                    turn_sources(i, pi)
                    if rel_bias:
                        bias_tiles(i, pi)
                    for m in range(2):
                        scores(i, pi, 0, m)
                    for u in range(nu):
                        if u + 1 < nu:
                            for m in range(2):
                                scores(i, pi, u + 1, m)
                        for m in ms:
                            turn(i, pi, u, m)
                        for m in ms:
                            weighted(i, pi, u, m)

        @block.scalar
        def _(act):
            def probabilities(i, pi, u, m):
                un, x = units[u], (pi * nu + u) * 2 + m
                act.wait_ge(K.nm_done.h, at(K.nm_done, i, X, x))
                if diff:
                    act.wait_ge(K.w_done.h, at(K.w_done, i, U, pi * nu + u - 1))
                else:
                    act.wait_ge(K.pt_done.h, at(K.pt_done, i, T, x - 2))
                if sink is not None:
                    act.activation(K.sink_exp[:, u % 2, m:m + 1], K.sink_pair[:, m:m + 1], ACT.Exp,
                                   bias=K.neg_max[:, u % 2, m:m + 1])
                act.activation(K.p_mat[m][:, 0:un.width], S[m][:, 0:un.width], ACT.Exp, bias=K.neg_max[:, u % 2, m:m + 1],
                               scale=SCALE, accum_out=K.p_sum[:, u % 2, m:m + 1]).then_inc(K.p_done.h, 1)

            def read_turned(i, pi, u):
                x = pi * nu + u if diff else (pi * nu + u) * 2
                w = units[u].width
                act.wait_ge(K.pt_done.h, at(K.pt_done, i, T, x))
                act.activation(K.pT_mat[x % 2][:, 0:w], PT[x % 2][:, 0:w], ACT.Copy).then_inc(K.pt_read[0].h, 1)

            with act.Fori(0, steps) as i:
                for pi in range(pairs):
                    for q in range(n_src):
                        act.wait_ge(K.src_turned.h, at(K.src_turned, i, S0, pi * n_src + q))
                        act.activation(K.headsT[q][:, :], PT[q % 2][:, 0:TOK], ACT.Copy).then_inc(K.src_read.h, 1)
                    for m in range(2):
                        probabilities(i, pi, 0, m)
                    for u in range(nu):
                        read_turned(i, pi, u)
                        if u + 1 < nu:
                            for m in range(2):
                                probabilities(i, pi, u + 1, m)

        @block.vector
        def _(dve):
            per_step = pairs * (nu * ATT_LINKS[diff, sink is not None] + (sink is not None))

            def maxima(link, i, pi, u, m):
                un, x = units[u], (pi * nu + u) * 2 + m
                dve.wait_ge(K.s_done.h, at(K.s_done, i, X, x))
                nm = K.neg_max[:, u % 2, m:m + 1]
                link(dve.tensor_reduce(nm, S[m][:, 0:un.width], AX.X, ALU.max))
                if sink is not None:
                    link(dve.tensor_scalar(nm, nm, SCALE, K.sink_pair[:, m:m + 1], ALU.mult, ALU.max))
                    dve.tensor_scalar(nm, nm, -1.0, None, ALU.mult).then_inc(K.nm_done.h, 1)
                else:
                    dve.tensor_scalar(nm, nm, -SCALE, None, ALU.mult).then_inc(K.nm_done.h, 1)

            def inverse_sums(link, i, pi, u):
                x = (pi * nu + u) * 2 + 1
                dve.wait_ge(K.p_done.h, at(K.p_done, i, X, x))
                r = K.p_inv[:, u % 2, :]
                if sink is not None:
                    link(dve.tensor_tensor(K.p_sum[:, u % 2, :], K.p_sum[:, u % 2, :], K.sink_exp[:, u % 2, :], ALU.add))
                link(dve.reciprocal(r, K.p_sum[:, u % 2, :]))

            def combine(link, i, pi, u):
                un = units[u]
                inverse_sums(link, i, pi, u)
                link(dve.tensor_scalar(K.p_inv[:, u % 2, 1:2], K.p_inv[:, u % 2, 1:2], K.neg_lam[:, 0:1], None, ALU.mult))
                dve.wait_ge(K.pt_done.h, at(K.pt_done, i, T, pi * nu + u - 1))
                w = K.w_mat[:, 0:un.width]
                link(dve.tensor_scalar(w, K.p_mat[0][:, 0:un.width], K.p_inv[:, u % 2, 0:1], None, ALU.mult))
                dve.scalar_tensor_tensor(w, K.p_mat[1][:, 0:un.width], K.p_inv[:, u % 2, 1:2], w, ALU.mult, ALU.add)\
                   .then_inc(K.w_done.h, 1)

            def read_turned(i, pi, u):
                x = (pi * nu + u) * 2 + 1
                w = units[u].width
                dve.wait_ge(K.pt_done.h, at(K.pt_done, i, T, x))
                dve.tensor_copy(K.pT_mat[1][:, 0:w], PT[1][:, 0:w]).then_inc(K.pt_read[1].h, 1)

            def finish(i, pi, u):
                x = pi * nu + u
                dve.wait_ge(K.o_done.h, at(K.o_done, i, U, x))
                o = out(i, pi, units[u].tile)
                if diff:
                    dve.tensor_copy(o, o_bank(x)).then_inc(K.o_read.h, 1)
                else:
                    for m in range(2):
                        ins = dve.tensor_scalar(o[:, m * HEAD_DIM:(m + 1) * HEAD_DIM], o_bank(m)[:, 0:HEAD_DIM],
                                                K.p_inv[:, u % 2, m:m + 1], None, ALU.mult)
                    ins.then_inc(K.o_read.h, 1)

            with dve.Fori(0, steps) as i:
                link = Chain(dve, K.dve_chain, i * per_step)
                for pi in range(pairs):
                    if rel_bias:
                        flat = K.psum[:, 0:4, :].rearrange("p a b -> p (a b)")
                        dve.wait_ge(K.s_done.h, at(K.s_done, i, X, pi * nu * 2 - 1))
                        for b in range(4):
                            dve.wait_ge(K.g_done.h, at(K.g_done, i, 4 * pairs, 4 * pi + b))
                            g = K.G[:, :, :, :].rearrange("p c h r -> p c (h r)")[:, 16 * b:16 * b + 16, :]
                            mask = K.col_mask[:, 16 * b:16 * b + 16].unsqueeze(2).to_broadcast([P, 16, 32])
                            dve.scalar_tensor_tensor(g, flat[:, b * 512:(b + 1) * 512].rearrange("p (c x) -> p c x", x=32),
                                                     1.0 / SCALE, mask, ALU.mult, ALU.add).then_inc(K.g_ready.h, 1)
                    if sink is not None:
                        dve.wait_ge(K.p_done.h, at(K.p_done, i, X, pi * nu * 2 - 1))
                        link(dve.tensor_copy(K.sink_pair[:, :], K.sink_b[:, ds(2 * (pairs * i + pi), 2)]))
                    for m in range(2):
                        maxima(link, i, pi, 0, m)
                    for u in range(nu):
                        if diff:
                            combine(link, i, pi, u)
                        else:
                            inverse_sums(link, i, pi, u)
                        if u + 1 < nu:
                            for m in range(2):
                                maxima(link, i, pi, u + 1, m)
                        if not diff:
                            read_turned(i, pi, u)
                        finish(i, pi, u)
                assert link.k == per_step, (link.k, per_step)
            K.dve_chain.n += steps * link.k
    for s, per in ((K.staged, pairs), (K.src_turned, S0), (K.src_read, S0), (K.s_done, X), (K.nm_done, X), (K.p_done, X),
                   (K.pt_done, T), (K.pt_read[0], U), (K.o_done, U), (K.o_read, U)):
        s.n += per * steps
    if not diff:
        K.pt_read[1].n += U * steps
    if diff:
        K.w_done.n += U * steps
    if rel_bias:
        K.g_done.n += 4 * pairs * steps
        K.g_ready.n += 4 * pairs * steps


ATT_LINKS = {(True, False): 5, (False, False): 3, (False, True): 6}


def layer_norm_stage(K, gain, bias, tiles, store=None):
    nc = K.nc
    n = len(tiles)
    sm0, st0, nm0, rs0, ga0 = K.small_loaded.n, K.sums_done.n, K.normed.n, K.rstd_done.n, K.gained.n
    with nc.Block() as block:
        @block.sync
        def _(sp):
            sp.dma_start(K.ln_gain[:, :], gain.partition_broadcast(P)).then_inc(K.small_loaded.h, 16)
            sp.dma_start(K.ln_bias[:, :], bias.partition_broadcast(P)).then_inc(K.small_loaded.h, 16)
            if store is not None:
                for i, t in enumerate(tiles):
                    sp.wait_ge(K.gained.h, ga0 + i + 1)
                    sp.dma_start(store[t * P:(t + 1) * P, :], K.x[:, t, :]).then_inc(K.stored.h, 16)
                sp.wait_ge(K.stored.h, K.stored.n + 16 * n)

        @block.vector
        def _(dve):
            link = Chain(dve, K.dve_chain)
            for i, t in enumerate(tiles):
                for h in range(2):
                    ins = dve.bn_stats(K.ln_stats[:, t, h, :], K.x[:, t, h * 512:(h + 1) * 512])
                    link(ins)
                dve.bn_aggr(K.ln_mv[:, t, :], K.ln_stats[:, t, :, :]).then_inc(K.sums_done.h, 1)
            dve.wait_ge(K.rstd_done.h, rs0 + 1)
            for i, t in enumerate(tiles):
                dve.tensor_scalar(K.x[:, t, :], K.x[:, t, :], K.ln_mv[:, t, 0:1], K.rstd[:, t:t + 1], ALU.subtract, ALU.mult)\
                   .then_inc(K.normed.h, 1)
            K.dve_chain.n += link.k

        @block.scalar
        def _(act):
            act.wait_ge(K.sums_done.h, st0 + n)
            link = Chain(act, K.act_chain)
            link(act.activation(K.lnms[:, 0:n], K.ln_mv[:, 0:n, 1], ACT.Ln, bias=K.eps5[:, 0:1]))
            act.activation(K.rstd[:, 0:n], K.lnms[:, 0:n], ACT.Exp, scale=-0.5).then_inc(K.rstd_done.h, 1)
            K.act_chain.n += link.k

        @block.gpsimd
        def _(pool):
            link = Chain(pool, K.pool_chain)
            pool.wait_ge(K.small_loaded.h, sm0 + 32)
            for i, t in enumerate(tiles):
                pool.wait_ge(K.normed.h, nm0 + i + 1)
                link(pool.tensor_tensor(K.x[:, t, :], K.x[:, t, :], K.ln_gain[:, :], ALU.mult))
                pool.tensor_tensor(K.x[:, t, :], K.x[:, t, :], K.ln_bias[:, :], ALU.add).then_inc(K.gained.h, 1)
            K.pool_chain.n += link.k
    K.small_loaded.n += 32
    for s in (K.sums_done, K.normed, K.gained):
        s.n += n
    K.rstd_done.n += 1
    if store is not None:
        K.stored.n += 16 * n


TAPS = 5
SSM_INNER = 2 * D
SSM_STATE = 128
SSM_GROUPS = 4
GROUP_HEADS = 8
SSM_HEADS = SSM_GROUPS * GROUP_HEADS
GROUP_W = GROUP_HEADS * HEAD_DIM
PAD = TAPS // 2
LAT_AT, CTX_AT = 0, N_LAT + 2 * PAD
ROW = N_TOK + 4 * PAD
OUT = ROW - 2 * PAD


def dt_stage(K, w_dt, dt_bias, a_log, conv_w, conv_b, norm_g):
    nc = K.nc
    sm0, mm0, dv0, ac0, tr0 = K.small_loaded.n, K.mm_done.n, K.dve_chain.n, K.act_chain.n, K.turned.n
    H2 = 2 * SSM_HEADS
    with nc.Block() as block:
        @block.sync
        def _(sp):
            for out, src in ((K.dt_w[:, :, :], w_dt.rearrange("(k p) n -> p k n", p=P)),
                             (K.dt_bias[:, :], dt_bias.partition_broadcast(P)),
                             (K.a_neg[:, :], a_log.partition_broadcast(P)),
                             (K.conv_rows[0:TAPS * 24, :], conv_w.rearrange("j (b p) -> (j b) p", p=P)),
                             (K.vec_rows[0:24, :], conv_b.rearrange("(b p) -> b p", p=P)),
                             (K.vec_rows[32:48, :], norm_g.rearrange("(b p) -> b p", p=P))):
                sp.dma_start(out, src).then_inc(K.small_loaded.h, 16)

        @block.vector
        def _(dve):
            link = Chain(dve, K.dve_chain)
            dve.wait_ge(K.small_loaded.h, sm0 + 96)
            link(dve.tensor_copy(K.dt_w_hi[:, :, :], K.dt_w[:, :, :]))
            link(dve.tensor_tensor(K.dt_w_lo[:, :, :], K.dt_w[:, :, :], K.dt_w_hi[:, :, :].bitcast(F32), ALU.subtract))
            dve.wait_ge(K.mm_done.h, mm0 + 1)
            v, e = K.dt[:, :, :], K.a[:, :, :]
            link(dve.tensor_tensor(v, K.bank[0][:, 0:TOK_TILES * H2].rearrange("p (t h) -> p t h", h=H2),
                                   K.dt_bias[:, :].unsqueeze(1).to_broadcast([P, TOK_TILES, H2]), ALU.add))
            link(dve.scalar_tensor_tensor(e, v, -1.0, v, ALU.mult, ALU.max))
            dve.wait_ge(K.act_chain.h, ac0 + 3)
            link(dve.scalar_tensor_tensor(v.rearrange("p t h -> p (t h)"), v.rearrange("p t h -> p (t h)"), 0.0,
                                          e.rearrange("p t h -> p (t h)"), ALU.max, ALU.add))
            dve.wait_ge(K.a_neg_done.h, K.a_neg_done.n + 1)
            link(dve.tensor_tensor(e, v, K.a_neg[:, :].unsqueeze(1).to_broadcast([P, TOK_TILES, H2]), ALU.mult))
            dve.wait_ge(K.turned.h, tr0 + 1)
            dve.tensor_copy(K.conv_cols[:, :], K.bank[1][:, 0:TAPS * 24])
            dve.tensor_copy(K.vec_cols[:, :], K.bank[2][:, 0:48])
            K.dve_chain.n += link.k

        @block.scalar
        def _(act):
            act.wait_ge(K.small_loaded.h, sm0 + 96)
            link = Chain(act, K.act_chain)
            link(act.activation(K.a_neg[:, :], K.a_neg[:, :], ACT.Exp))
            act.wait_ge(K.dve_chain.h, dv0 + 4)
            e = K.a[:, :, :]
            link(act.activation(e, e, ACT.Exp, scale=-1.0))
            link(act.activation(e, e, ACT.Ln, bias=K.one[:, 0:1]))
            K.act_chain.n += link.k

        @block.gpsimd
        def _(pool):
            pool.wait_ge(K.act_chain.h, ac0 + 1)
            pool.tensor_scalar(K.a_neg[:, :], K.a_neg[:, :], -1.0, None, ALU.mult).then_inc(K.a_neg_done.h, 1)

        @block.tensor
        def _(pe):
            pe.wait_ge(K.dve_chain.h, dv0 + 2)
            for t in range(TOK_TILES):
                for k in range(KD):
                    mm = product(pe, K.bank[0][:, t * H2:(t + 1) * H2], K.hT_hi[:, k, t * P:(t + 1) * P],
                                 K.hT_lo[:, k, t * P:(t + 1) * P], K.dt_w_hi[:, k, :], K.dt_w_lo[:, k, :], k == 0, k == KD - 1)
            mm.then_inc(K.mm_done.h, 1)
            pe.wait_ge(K.small_loaded.h, sm0 + 96)
            pe.transpose(K.bank[1][:, 0:TAPS * 24], K.conv_rows[0:TAPS * 24, :], K.ident[0:TAPS * 24, 0:TAPS * 24])
            pe.transpose(K.bank[2][:, 0:48], K.vec_rows[0:48, :], K.ident[0:48, 0:48]).then_inc(K.turned.h, 1)
    K.small_loaded.n += 96
    K.mm_done.n += 1
    K.turned.n += 1


def conv_stage(K, stream, nxt, block0, back):
    nc = K.nc
    st = Stage(K, stream, nxt)
    nt = TOK_TILES
    ns = stream.count
    mm0, re0, tr0, xr0, cv0, si0, bt0, br0 = (s.n for s in (
        K.mm_done, K.relu_done, K.turned, K.xt_read, K.conv_done, K.silu_done, K.back_done, K.back_read))
    FB = SLAB_N // P

    def tile_done(eng, n, j):
        if j < nt - 1:
            eng.wait_ge(K.mm_done.h, mm0 + (nt - 1) * n + j + 1)
        else:
            eng.wait_ge(K.w_used.h, 2 * (st.g0 + n) + 2)

    with nc.Block() as block:
        @block.sync
        def _(sp):
            stream_loads(K, sp, st)

        @block.scalar
        def _(act):
            def silu(n):
                for fb in range(FB):
                    act.wait_ge(K.conv_done.h, cv0 + FB * n + fb + 1)
                    c = K.conv_out[fb // 2][:, fb % 2, :]
                    if back:
                        act.activation(c, c, ACT.Silu).then_inc(K.silu_done.h, 1)
                    else:
                        act.activation(K.BC[:, ds(n * FB + fb, 1), 0:N_LAT], c[:, 0:N_LAT].unsqueeze(1), ACT.Silu)
                        act.activation(K.BC[:, ds(n * FB + fb, 1), N_LAT:N_TOK], c[:, CTX_AT:CTX_AT + N_CTX].unsqueeze(1), ACT.Silu)\
                           .then_inc(K.silu_done.h, 1)

            def back_out(n):
                for t in range(nt):
                    act.wait_ge(K.back_done.h, bt0 + nt * n + t + 1)
                    act.activation(K.x_tok[:, t, ds(n * SLAB_N, SLAB_N)], K.bank[6 + t % 2][:, :], ACT.Copy)\
                       .then_inc(K.back_read.h, 1)

            def body(n, ahead):
                if ahead:
                    split_hi(K, act, st.g0 + n + 1, 0)
                for j in range(nt):
                    tile_done(act, n, j)
                    act.wait_ge(K.turned.h, tr0 + nt * n + j - 1)
                    act.activation(K.relu[:, j % 2, :], K.bank[j][:, :], ACT.Copy).then_inc(K.relu_done.h, 1)
                if ahead:
                    split_hi(K, act, st.g0 + n + 1, 1)
                silu(n)
                if back:
                    back_out(n)
            ahead_loop(act, st, body)

        @block.vector
        def _(dve):
            def body(n, ahead):
                if ahead:
                    split_lo(K, dve, st.g0 + n + 1, 0)
                for j in range(nt):
                    dve.wait_ge(K.turned.h, tr0 + nt * n + j + 1)
                    at = PAD + j * P if j < LAT_TILES else CTX_AT + PAD + (j - LAT_TILES) * P
                    dve.tensor_copy(K.xt[:, :, at:at + P], K.bank[6 + j % 2][:, :].rearrange("p (f t) -> p f t", f=FB))\
                       .then_inc(K.xt_read.h, 1)
                dve.wait_ge(K.xt_read.h, xr0 + nt * (n + 1))
                if ahead:
                    split_lo(K, dve, st.g0 + n + 1, 1)
                for fb in range(FB):
                    c = K.conv_out[fb // 2][:, fb % 2, :]
                    if back:
                        dve.wait_ge(K.back_read.h, br0 + nt * n)
                    else:
                        dve.wait_ge(K.silu_done.h, si0 + FB * n)
                    for j in range(TAPS):
                        x = K.xt[:, fb, j:j + OUT]
                        tap = K.conv_cols[:, ds(n * FB + (block0 + fb + 24 * j), 1)]
                        if j == 0:
                            ins = dve.tensor_scalar(c, x, tap, K.vec_cols[:, ds(n * FB + (block0 + fb), 1)], ALU.mult, ALU.add)
                        else:
                            ins = dve.scalar_tensor_tensor(c, x, tap, c, ALU.mult, ALU.add)
                        if j < TAPS - 1:
                            ins.then_inc(K.tap_done.h, 1)
                            dve.wait_ge(K.tap_done.h, K.tap_done.n + (TAPS - 1) * (FB * n + fb) + j + 1)
                    ins.then_inc(K.conv_done.h, 1)
            dve.memset(K.xt[:, :, :], 0.0).then_inc(K.dve_chain.h, 1)
            dve.wait_ge(K.dve_chain.h, K.dve_chain.n + 1)
            ahead_loop(dve, st, body)

        @block.tensor
        def _(pe):
            def turn(n, j):
                pe.wait_ge(K.relu_done.h, re0 + nt * n + j + 1)
                pe.wait_ge(K.xt_read.h, xr0 + nt * n + j - 1)
                if back:
                    pe.wait_ge(K.back_read.h, br0 + nt * n)
                if j == 0:
                    pe.wait_ge(K.conv_done.h, cv0 + FB * n)
                for k in range(FB):
                    mm = pe.transpose(K.bank[6 + j % 2][:, k * P:(k + 1) * P], K.relu[:, j % 2, k * P:(k + 1) * P], K.ident[:, :])
                mm.then_inc(K.turned.h, 1)

            def turn_back(n):
                pe.wait_ge(K.silu_done.h, si0 + FB * (n + 1))
                for t in range(nt):
                    pe.wait_ge(K.back_read.h, br0 + nt * n + t - 1)
                    pe.wait_ge(K.xt_read.h, xr0 + nt * (n + 1))
                    at = LAT_AT + t * P if t < LAT_TILES else CTX_AT + (t - LAT_TILES) * P
                    for fb in range(FB):
                        mm = pe.transpose(K.bank[6 + t % 2][:, fb * P:(fb + 1) * P], K.conv_out[fb // 2][:, fb % 2, at:at + P],
                                          K.ident[:, :])
                    mm.then_inc(K.back_done.h, 1)

            def gemm_half(n, h):
                pe.wait_ge(K.lo_done.h, 2 * (st.g0 + n) + h + 1)
                for j in range(nt):
                    if h == 0:
                        pe.wait_ge(K.relu_done.h, re0 + nt * (n - 1) + j + 1)
                    for k in range(SLAB_K):
                        kk = h * SLAB_K + k
                        mm = product(pe, K.bank[j][:, :], K.hT_hi[:, kk, j * P:(j + 1) * P], K.hT_lo[:, kk, j * P:(j + 1) * P],
                                     K.w_hi[h][:, k, :], K.w_lo[h][:, k, :], kk == 0, kk == KD - 1)
                    if j == nt - 1:
                        mm.then_inc(K.w_used.h, 1)
                    elif h == 1:
                        mm.then_inc(K.mm_done.h, 1)
                    if h == 1 and j:
                        turn(n, j - 1)
                if h == 1:
                    turn(n, nt - 1)

            gemm_half(0, 0)
            gemm_half(0, 1)
            with pe.Fori(1, ns) as n:
                gemm_half(n, 0)
                if back:
                    turn_back(n - 1)
                gemm_half(n, 1)
            if back:
                turn_back(ns - 1)
    K.mm_done.n += (nt - 1) * ns
    for s in (K.relu_done, K.turned, K.xt_read):
        s.n += nt * ns
    for s in (K.conv_done, K.silu_done):
        s.n += FB * ns
    K.tap_done.n += (TAPS - 1) * FB * ns
    K.dve_chain.n += 1
    if back:
        K.back_done.n += nt * ns
        K.back_read.n += nt * ns


def silu_store_out(K, act, count, n, t, bank, j):
    act.wait_ge(K.z_stored[j].h, K.z_stored[j].n + 16 * n)
    act.activation(K.z_buf[:, j, :], bank[:, :], ACT.Silu).then_inc(K.evacuated.h, 1)
    act.wait_ge(K.evacuated.h, K.evacuated.n + LAT_TILES * n + j + 1)
    act.dma_start(K.z_dram[t * P:(t + 1) * P, ds(n * SLAB_N, SLAB_N)], K.z_buf[:, j, :]).then_inc(K.z_stored[j].h, 16)


class Step:

    def __init__(self, direction, tile, first):
        self.d, self.tile, self.first = direction, tile, first
        self.lat = tile < LAT_TILES


def scan_steps():
    orders = ([4, 5, 0, 1, 2, 3], [5, 4, 3, 2, 1, 0])
    return [Step(d, t, i == 0) for d in range(2) for i, t in enumerate(orders[d])]


def scan_stage(K, d_skip):
    nc = K.nc
    steps = scan_steps()
    lat = [s for s in steps if s.lat]
    NL, NS = len(lat), len(steps)
    base = {}
    for s in (K.staged, K.turned, K.src_read, K.cs_done, K.cs_read, K.decay_done, K.bc_done, K.diff_done,
              K.l_done, K.m_done, K.yd_done, K.yo_done, K.y_read, K.st_done, K.state_done, K.xdt_done, K.z_loaded, K.cb_done,
              K.cb_read, K.y_done, K.yd_read, K.small_loaded, K.stored, K.ss_done, K.rstd_done, K.fin_done):
        base[s] = s.n
    at = lambda s, g, per, k: base[s] + g * per + k + 1
    GH = GROUP_HEADS
    H2 = 2 * SSM_HEADS
    view = lambda ap: ap.rearrange("p (h d) -> p h d", d=HEAD_DIM)
    bc8 = lambda ap: ap.unsqueeze(2).to_broadcast([P, GH, HEAD_DIM])
    tri = [K.tri[:, 0, :], K.tri[:, 1, :]]

    with nc.Block() as block:
        @block.sync
        def _(sp):
            sp.dma_start(K.d_skip[:, :], d_skip.partition_broadcast(P)).then_inc(K.small_loaded.h, 16)
            sp.dma_start(K.tri[:, :, :], K.c_tri).then_inc(K.small_loaded.h, 16)
            sp.dma_start(K.ones[:, :], K.c_ones).then_inc(K.small_loaded.h, 16)
            sp.dma_start(K.order_mask[:, :, :], K.c_order_mask).then_inc(K.small_loaded.h, 16)
            for j in range(LAT_TILES):
                sp.wait_ge(K.z_stored[j].h, K.z_stored[j].n)
            with sp.Fori(0, SSM_GROUPS) as g:
                sp.wait_ge(K.ss_done.h, base[K.ss_done] + g)
                sp.dma_start(K.z_g[:, :, :], K.z_dram.rearrange("(t p) n -> p t n", p=P)[:, :, ds(g * GROUP_W, GROUP_W)])\
                  .then_inc(K.z_loaded.h, 16)

        @block.gpsimd
        def _(pool):
            with pool.Fori(0, SSM_GROUPS) as g:
                pool.wait_ge(K.yd_done.h, at(K.yd_done, g, NL, -1))
                pool.wait_ge(K.yo_done.h, at(K.yo_done, g, NL, -1))
                pool.wait_ge(K.st_done.h, at(K.st_done, g, NS, -1))
                pool.wait_ge(K.xdt_done.h, at(K.xdt_done, g, 2, -1))
                pool.tensor_copy(K.BT_g[:, :].unsqueeze(1), K.BC[:, ds(g, 1), :])
                pool.tensor_copy(K.CT_g[:, :].unsqueeze(1), K.BC[:, ds(g + SSM_GROUPS, 1), :])
                for d in range(2):
                    pool.tensor_copy(K.dt_g[:, d, :, :], K.dt[:, :, ds(g * GH + d * SSM_HEADS, GH)])
                    ins = pool.tensor_copy(K.a_g[:, d, :, :], K.a[:, :, ds(g * GH + d * SSM_HEADS, GH)])
                ins.then_inc(K.staged.h, 1)

        @block.tensor
        def _(pe):
            def chunk(ap, t):
                return ap[:, t * P:(t + 1) * P]

            def decay_rows(g, i):
                s = lat[i]
                pe.wait_ge(K.diff_done.h, at(K.diff_done, g, NL, i - 1))
                for b in range(GH // 4):
                    pe.matmul(K.bank[b][:, :], K.ident[:, :], K.order_mask[:, s.d, :].unsqueeze(1).to_broadcast([P, 4, P]),
                              start=True, stop=False)
                for h in range(GH):
                    mm = pe.matmul(K.bank[h // 4][:, (h % 4) * P:(h % 4 + 1) * P],
                                   K.a_g[:, s.d, s.tile, h:h + 1].to_broadcast([P, P]), tri[s.d], start=False, stop=h % 4 == 3)
                mm.then_inc(K.bc_done.h, 1)

            def within(g, i):
                s = lat[i]
                pe.wait_ge(K.m_done.h, at(K.m_done, g, NL, i))
                pe.wait_ge(K.yd_read.h, at(K.yd_read, g, NL, i - 1))
                for h in range(GH):
                    mm = pe.matmul(K.bank[4][:, h * HEAD_DIM:(h + 1) * HEAD_DIM], K.decay[:, i % 2, h, :],
                                   K.xdt[:, s.tile, h * HEAD_DIM:(h + 1) * HEAD_DIM], start=True, stop=True)
                mm.then_inc(K.yd_done.h, 1)

            pe.wait_ge(K.small_loaded.h, base[K.small_loaded] + 64)
            with pe.Fori(0, SSM_GROUPS) as g:
                pe.wait_ge(K.staged.h, at(K.staged, g, 1, 0))
                pe.wait_ge(K.state_done.h, at(K.state_done, g, NS, -1))
                pe.wait_ge(K.yd_read.h, at(K.yd_read, g, NL, -1))
                pe.wait_ge(K.fin_done.h, at(K.fin_done, g, 1, -1))
                for t in range(TOK_TILES):
                    mm = pe.transpose(K.bank[6 + t // 4][:, (t % 4) * P:(t % 4 + 1) * P], chunk(K.BT_g, t), K.ident[:, :])
                mm.then_inc(K.turned.h, 1)
                for d in range(2):
                    pe.matmul(K.bank[5][:, d * 48:d * 48 + 48], tri[d], K.a_g[:, d, :, :], start=True, stop=True)
                mm = pe.matmul(K.bank[5][:, 96:192], K.ones[:, :], K.a_g[:, :, :, :], start=True, stop=True)
                mm.then_inc(K.cs_done.h, 1)
                for t in range(LAT_TILES):
                    mm = pe.matmul(K.bank[2][:, t * P:(t + 1) * P], chunk(K.BT_g, t), chunk(K.CT_g, t), start=True, stop=True)
                mm.then_inc(K.cb_done.h, 1)
                decay_rows(g, 0)
                i = 0
                for k, s in enumerate(steps):
                    if s.lat:
                        pe.wait_ge(K.state_done.h, at(K.state_done, g, NS, k - 1))
                        pe.wait_ge(K.y_read.h, at(K.y_read, g, NL, i - 1))
                        pe.wait_ge(K.cs_read.h, at(K.cs_read, g, 1, 0))
                        pe.matmul(K.bank[5][:, :], chunk(K.CT_g, s.tile), K.state[:, :], start=True, stop=True)\
                          .then_inc(K.yo_done.h, 1)
                    if s.first:
                        pe.wait_ge(K.xdt_done.h, at(K.xdt_done, g, 2, s.d))
                        pe.wait_ge(K.src_read.h, at(K.src_read, g, 1, 0))
                    pe.wait_ge(K.state_done.h, at(K.state_done, g, NS, k - 1))
                    pe.matmul(K.bank[6][:, :], K.B_tok[:, s.tile, :], K.xdts[:, s.tile, :], start=True, stop=True)\
                      .then_inc(K.st_done.h, 1)
                    if s.lat:
                        if i + 1 < NL:
                            decay_rows(g, i + 1)
                        within(g, i)
                        i += 1

        @block.scalar
        def _(act):
            link = Chain(act, K.act_chain)
            act.wait_ge(K.small_loaded.h, base[K.small_loaded] + 64)
            with act.Fori(0, SSM_GROUPS) as g:
                act.wait_ge(K.turned.h, at(K.turned, g, 1, 0))
                act.wait_ge(K.st_done.h, at(K.st_done, g, NS, -1))
                act.activation(K.B_tok[:, 0:4, :].rearrange("p t n -> p (t n)"), K.bank[6][:, :], ACT.Copy)
                act.activation(K.B_tok[:, 4:6, :].rearrange("p t n -> p (t n)"), K.bank[7][:, 0:256], ACT.Copy)\
                   .then_inc(K.src_read.h, 1)
                act.wait_ge(K.cs_read.h, at(K.cs_read, g, 1, 0))
                act.activation(K.cs_exp[:, :], K.cs[:, :], ACT.Exp).then_inc(K.decay_done.h, 1)
                for i, s in enumerate(lat):
                    act.wait_ge(K.diff_done.h, at(K.diff_done, g, NL, i))
                    m = K.decay[:, i % 2, :, :]
                    act.activation(m, m, ACT.Exp).then_inc(K.l_done.h, 1)
                act.wait_ge(K.y_done.h, at(K.y_done, g, 1, 0))
                for t in range(LAT_TILES):
                    ins = act.activation(K.z_g[:, t, :], K.y[:, t, :], ACT.Square, accum_out=K.y_ss[:, t:t + 1])
                ins.then_inc(K.ss_done.h, 1)
                act.wait_ge(K.ss_done.h, at(K.ss_done, g, 1, 0))
                act.activation(K.y_ln[:, :], K.y_ss[:, :], ACT.Ln, bias=K.eps5[:, 0:1], scale=1.0 / GROUP_W)\
                   .then_inc(K.act_chain.h, 1)
                act.wait_ge(K.act_chain.h, K.act_chain.n + g + 1)
                act.activation(K.y_rstd[:, :], K.y_ln[:, :], ACT.Exp, scale=-0.5).then_inc(K.rstd_done.h, 1)
            K.act_chain.n += SSM_GROUPS

        @block.vector
        def _(dve):
            links = SCAN_LINKS
            for j in range(LAT_TILES):
                dve.wait_ge(K.z_stored[j].h, K.z_stored[j].n)
            with dve.Fori(0, SSM_GROUPS) as g:
                link = Chain(dve, K.dve_chain, g * links)

                def differences(i):
                    s = lat[i]
                    dve.wait_ge(K.bc_done.h, at(K.bc_done, g, NL, i))
                    dve.wait_ge(K.yd_done.h, at(K.yd_done, g, NL, i - 2))
                    sums = K.cs[:, (s.d * TOK_TILES + s.tile) * GH:(s.d * TOK_TILES + s.tile + 1) * GH]
                    dve.tensor_tensor(K.decay[:, i % 2, :, :], K.psum[:, 0:2, :].rearrange("p a (h l) -> p (a h) l", l=P),
                                      sums.unsqueeze(2).to_broadcast([P, GH, P]), ALU.subtract).then_inc(K.diff_done.h, 1)

                def matrices(i):
                    s = lat[i]
                    dve.wait_ge(K.l_done.h, at(K.l_done, g, NL, i))
                    m = K.decay[:, i % 2, :, :]
                    dve.tensor_tensor(m, m, K.cbT[:, s.tile, :].unsqueeze(1).to_broadcast([P, GH, P]), ALU.mult)\
                       .then_inc(K.m_done.h, 1)

                def inputs(d):
                    k0 = d * TOK_TILES * GH
                    if d == 1:
                        dve.wait_ge(K.yd_done.h, at(K.yd_done, g, NL, LAT_TILES - 1))
                        dve.wait_ge(K.st_done.h, at(K.st_done, g, NS, TOK_TILES - 1))
                    for t in range(TOK_TILES):
                        x = view(K.xdt[:, t, :])
                        dve.tensor_tensor(x, K.x_tok[:, t, ds(g * GROUP_W, GROUP_W)].rearrange("p (h d) -> p h d", d=HEAD_DIM),
                                          bc8(K.dt_g[:, d, t, :]), ALU.mult).then_inc(K.xdt_part.h, 1)
                    dve.wait_ge(K.xdt_part.h, K.xdt_part.n + g * 2 * TOK_TILES + (d + 1) * TOK_TILES)
                    for t in range(TOK_TILES):
                        ins = dve.tensor_tensor(view(K.xdts[:, t, :]), view(K.xdt[:, t, :]),
                                                bc8(K.cs_exp[:, 192 + k0 + t * GH:192 + k0 + (t + 1) * GH]), ALU.mult)
                    ins.then_inc(K.xdt_done.h, 1)

                dve.wait_ge(K.cs_done.h, at(K.cs_done, g, 1, 0))
                link(dve.tensor_copy(K.cs[:, 0:192], K.bank[5][:, 0:192]))
                dve.tensor_tensor(K.cs[:, 192:288], K.cs[:, 96:192], K.cs[:, 0:96], ALU.subtract).then_inc(K.cs_read.h, 1)
                dve.wait_ge(K.cb_done.h, at(K.cb_done, g, 1, 0))
                link(dve.tensor_copy(K.cbT[:, :, :].rearrange("p t n -> p (t n)"), K.bank[2][:, :]))
                if True:
                    dve.wait_ge(K.small_loaded.h, base[K.small_loaded] + 64)
                    for t in range(LAT_TILES):
                        ins = dve.tensor_tensor(view(K.y[:, t, :]),
                                                K.x_tok[:, t, ds(g * GROUP_W, GROUP_W)].rearrange("p (h d) -> p h d", d=HEAD_DIM),
                                                bc8(K.d_skip[:, ds(g * GH, GH)]), ALU.mult)
                    link(ins)
                dve.wait_ge(K.decay_done.h, at(K.decay_done, g, 1, 0))
                differences(0)
                i = 0
                for k, s in enumerate(steps):
                    if s.first:
                        inputs(s.d)
                    c8 = (s.d * TOK_TILES + s.tile) * GH
                    if s.lat:
                        y = K.y[:, s.tile, :]
                        dve.wait_ge(K.yo_done.h, at(K.yo_done, g, NL, i))
                        link(dve.tensor_tensor(view(K.y_tmp[:, :]), view(K.bank[5][:, :]), bc8(K.cs_exp[:, c8:c8 + GH]), ALU.mult))
                        dve.tensor_tensor(y, y, K.y_tmp[:, :], ALU.add).then_inc(K.y_read.h, 1)
                        dve.wait_ge(K.y_read.h, at(K.y_read, g, NL, i))
                        matrices(i)
                    dve.wait_ge(K.st_done.h, at(K.st_done, g, NS, k))
                    if s.first:
                        dve.tensor_copy(K.state[:, :], K.bank[6][:, :]).then_inc(K.state_done.h, 1)
                    else:
                        if s.lat:
                            dve.wait_ge(K.yo_done.h, at(K.yo_done, g, NL, i))
                        else:
                            dve.wait_ge(K.state_done.h, at(K.state_done, g, NS, k - 1))
                        link(dve.tensor_tensor(view(K.state[:, :]), view(K.state[:, :]), bc8(K.cs_exp[:, 96 + c8:96 + c8 + GH]),
                                               ALU.mult))
                        dve.tensor_tensor(K.state[:, :], K.state[:, :], K.bank[6][:, :], ALU.add).then_inc(K.state_done.h, 1)
                    if s.lat:
                        if i + 1 < NL:
                            differences(i + 1)
                        dve.wait_ge(K.yd_done.h, at(K.yd_done, g, NL, i))
                        dve.tensor_tensor(y, y, K.bank[4][:, :], ALU.add).then_inc(K.yd_read.h, 1)
                        dve.wait_ge(K.yd_read.h, at(K.yd_read, g, NL, i))
                        i += 1
                dve.wait_ge(K.z_loaded.h, base[K.z_loaded] + 16 * (g + 1))
                dve.tensor_tensor(K.y[:, :, :], K.y[:, :, :], K.z_g[:, :, :], ALU.mult).then_inc(K.y_done.h, 1)
                dve.wait_ge(K.rstd_done.h, at(K.rstd_done, g, 1, 0))
                for t in range(LAT_TILES):
                    ins = dve.tensor_scalar(K.x_tok[:, t, ds(g * GROUP_W, GROUP_W)], K.y[:, t, :], K.y_rstd[:, t:t + 1], None, ALU.mult)
                ins.then_inc(K.fin_done.h, 1)
                dve.wait_ge(K.fin_done.h, at(K.fin_done, g, 1, 0))
                assert link.k == links, link.k
            K.dve_chain.n += SSM_GROUPS * links
    for s, per in ((K.staged, 1), (K.turned, 1), (K.src_read, 1), (K.cs_done, 1), (K.cs_read, 1), (K.decay_done, 1),
                   (K.bc_done, NL), (K.diff_done, NL), (K.l_done, NL), (K.m_done, NL), (K.yd_done, NL),
                   (K.yd_read, NL), (K.yo_done, NL), (K.y_read, NL), (K.st_done, NS), (K.state_done, NS), (K.xdt_done, 2),
                   (K.cb_done, 1), (K.y_done, 1), (K.z_loaded, 16), (K.ss_done, 1), (K.rstd_done, 1), (K.fin_done, 1),
                   (K.xdt_part, 2 * TOK_TILES)):
        s.n += per * SSM_GROUPS
    K.small_loaded.n += 64


SCAN_LINKS = 3 + 8 + 10


def spill_stage(K):
    with K.nc.Block() as block:
        @block.sync
        def _(sp):
            sp.dma_start(K.x_dram.rearrange("(t p) n -> p t n", p=P), K.x[:, 0:LAT_TILES, :]).then_inc(K.x_stored.h, 16)
            sp.wait_ge(K.x_stored.h, 16)


def reload_stage(K):
    with K.nc.Block() as block:
        @block.sync
        def _(sp):
            sp.dma_start(K.x[:, 0:LAT_TILES, :], K.x_dram.rearrange("(t p) n -> p t n", p=P)).then_inc(K.x_stored.h, 16)
            sp.wait_ge(K.x_stored.h, 32)


def start_stage(K, x, ctx, first):
    nc = K.nc
    with nc.Block() as block:
        @block.sync
        def _(sp):
            for n in range(2):
                for h in range(2):
                    load_half(K, sp, n, h, first.half(n, h), first=n == 0)

        @block.gpsimd
        def _(pool):
            for s in K.credited:
                pool.sem_inc(s.h, CREDIT)
            pool.memset(K.eps6[:, :], NORM_EPS)
            pool.memset(K.eps5[:, :], LN_EPS)
            pool.memset(K.one[:, :], 1.0)

        @block.scalar
        def _(act):
            act.dma_start(K.x[:, 0:LAT_TILES, :], x.rearrange("(t p) n -> p t n", p=P)).then_inc(K.inputs_loaded.h, 16)
            act.dma_start(K.x[:, LAT_TILES:TOK_TILES, :], ctx.rearrange("(t p) n -> p t n", p=P)).then_inc(K.inputs_loaded.h, 16)
            act.dma_start(K.ident[:, :], K.c_ident).then_inc(K.inputs_loaded.h, 16)
            for h in range(2):
                act.wait_ge(K.raw_loaded[h].h, 16)
                act.activation(K.w_hi[h][:, :, :], K.raw[h][:, :, :], ACT.Copy).then_inc(K.hi_done.h, 1)
            act.wait_ge(K.inputs_loaded.h, 48)

        @block.vector
        def _(dve):
            for h in range(2):
                split_lo(K, dve, 0, h)


def load_stage(K, pairs):
    sm0 = K.small_loaded.n
    with K.nc.Block() as block:
        @block.sync
        def _(sp):
            for out, src in pairs:
                sp.dma_start(out, src).then_inc(K.small_loaded.h, 16)
            sp.wait_ge(K.small_loaded.h, sm0 + 16 * len(pairs))
    K.small_loaded.n += 16 * len(pairs)


def lambda_stage(K, lq1, lk1, lq2, lk2):
    load_stage(K, [(K.lam_in[:, i, :], v.partition_broadcast(P)) for i, v in enumerate((lq1, lk1, lq2, lk2))])
    ac0 = K.act_chain.n
    dv0 = K.dve_chain.n
    with K.nc.Block() as block:
        @block.vector
        def _(dve):
            link = Chain(dve, K.dve_chain)
            v = K.lam_in[:, :, :].rearrange("p (a b) d -> p a b d", b=2)
            link(dve.tensor_tensor(v[:, :, 0, :], v[:, :, 0, :], v[:, :, 1, :], ALU.mult))
            link(dve.tensor_reduce(K.lam_sum[:, :], v[:, :, 0, :], AX.X, ALU.add))
            dve.wait_ge(K.act_chain.h, ac0 + 1)
            link(dve.tensor_scalar(K.neg_lam[:, :], K.lam_sum[:, 1:2], K.lam_sum[:, 0:1], LAM_INIT, ALU.subtract, ALU.subtract))
            dve.tensor_scalar(K.sub_gain[:, :], K.vecs[:, SUBLN_AT:SUBLN_AT + 1], 1.0 - LAM_INIT, None, ALU.mult)
            K.dve_chain.n += link.k

        @block.scalar
        def _(act):
            act.wait_ge(K.dve_chain.h, dv0 + 2)
            act.activation(K.lam_sum[:, :], K.lam_sum[:, :], ACT.Exp).then_inc(K.act_chain.h, 1)
    K.act_chain.n += 1


def bias_table_stage(K, rpb):
    half = 8 * REL_ROWS
    tr0 = K.turned.n
    load_stage(K, [(K.rpb_rows[0:half, :, :], rpb.rearrange("(a h) o j -> (h o) a j", a=2)), (K.shift[:, :], K.c_shift),
                   (K.col_mask[:, :], K.c_col_mask)])
    with K.nc.Block() as block:
        @block.tensor
        def _(pe):
            for a in range(2):
                mm = pe.transpose(K.bank[a][0:REL_COLS, 0:half], K.rpb_rows[0:half, a, :], K.ident[0:half, 0:half])
            mm.then_inc(K.turned.h, 1)

        @block.vector
        def _(dve):
            dve.memset(K.rpbT[:, :, :], 0.0).then_inc(K.dve_chain.h, 1)
            dve.wait_ge(K.dve_chain.h, K.dve_chain.n + 1)
            dve.wait_ge(K.turned.h, tr0 + 1)
            for a in range(2):
                src = K.bank[a][0:REL_COLS, 0:half].rearrange("j (h o) -> j h o", o=REL_ROWS)
                for r in range(2):
                    dve.tensor_copy(K.rpbT[32 * r:32 * r + REL_COLS, 8 * a:8 * a + 8, r:r + REL_ROWS], src)
    K.turned.n += 1
    K.dve_chain.n += 1


CREDIT = 8
NORM1_AT, NORM2_AT, SUBLN_AT = 8 * KD, 9 * KD, 10 * KD


def program(nc, A, out):
    K = Kernel()
    K.nc = nc
    with ExitStack() as ctx:

        def place(name, shape, offset, dtype=F32):
            return nc.alloc_sbuf_tensor_at(name, shape, dtype, offset=offset)

        top = -(-nc.sbuf_base // 32) * 32
        end = nc.sbuf_usable_end

        class Cursor:

            def __init__(self, at):
                self.at = at

            def put(self, name, shape, dtype=F32):
                tensor = place(name, shape, self.at, dtype)
                self.at += -(-4 * int(np.prod(shape[1:])) // 32) * 32
                assert self.at <= end, (name, self.at, end)
                return tensor

        kept = Cursor(top)
        keep = kept.put

        def region(size):
            at = kept.at
            kept.at += size
            return at

        tile_bytes = TOK_TILES * D * 4
        X = region(tile_bytes)
        H = region(2 * tile_bytes)
        K.x = place("x", [P, TOK_TILES, D], X)
        c = Cursor(H)
        K.hT_hi = c.put("hT_hi", [P, KD, N_TOK], F32R)
        K.hT_lo = c.put("hT_lo", [P, KD, N_TOK], F32R)
        K.raw = [keep(f"raw{h}", [P, SLAB_K, SLAB_N]) for h in range(2)]
        K.w_hi = [keep(f"w_hi{h}", [P, SLAB_K, SLAB_N], F32R) for h in range(2)]
        K.w_lo = [keep(f"w_lo{h}", [P, SLAB_K, SLAB_N], F32R) for h in range(2)]
        K.ident = keep("ident", [P, P])
        K.modT = keep("modT", [P, 6 * KD, 2])
        K.vecs = keep("vecs", [P, 88])
        K.cexp = keep("cexp", [P, 2 * KD])
        K.cT = keep("cT", [P, KD, 2])
        K.eps6 = keep("eps6", [P, 1])
        K.eps5 = keep("eps5", [P, 1])
        K.one = keep("one", [P, 1])
        K.ssum = keep("ssum", [P, 8])
        K.lnms = keep("lnms", [P, 8])
        K.rstd = keep("rstd", [P, 8])
        K.mod_scale = keep("mod_scale", [P, KD, 2])
        K.head_ss = keep("head_ss", [P, 2, 32])
        K.head_ln = keep("head_ln", [P, 2, 32])
        K.head_rstd = keep("head_rstd", [P, 2, 32])
        K.neg_max = keep("neg_max", [P, 2, 2])
        K.p_sum = keep("p_sum", [P, 2, 2])
        K.p_inv = keep("p_inv", [P, 2, 2])
        K.sink_exp = keep("sink_exp", [P, 2, 2])
        K.sink_pair = keep("sink_pair", [P, 2])
        K.lam_sum = keep("lam_sum", [P, 2])
        K.neg_lam = keep("neg_lam", [P, 1])
        K.sub_gain = keep("sub_gain", [P, 1])
        K.ln_stats = keep("ln_stats", [P, TOK_TILES, 2, 6])
        K.ln_mv = keep("ln_mv", [P, TOK_TILES, 2])
        K.y_ss = keep("y_ss", [P, 4])
        K.y_ln = keep("y_ln", [P, 4])
        K.y_rstd = keep("y_rstd", [P, 4])
        K.d_skip = keep("d_skip", [P, SSM_HEADS])
        R = kept.at
        qkv_end = R + TOK_TILES * 3 * D * 4
        c = Cursor(R)
        K.mod_raw = [c.put(f"mod_raw{s}", [P, SLAB_K, SLAB_N]) for s in range(6)]
        K.mod_row = c.put("mod_row", [2, SLAB_N])
        K.vec_in = c.put("vec_in", [P, P])
        K.xhat = place("xhat", [P, TOK_TILES, D], R)
        K.feat = place("feat", [P, 2, N_TOK], qkv_end)
        c = Cursor(R)
        K.gate = c.put("gate", [P, 2, D])
        K.scaled_buf = c.put("scaled_buf", [P, 2, SLAB_N])
        K.uT_hi = c.put("uT_hi", [P, SLAB_K, N_TOK], F32R)
        K.uT_lo = c.put("uT_lo", [P, SLAB_K, N_TOK], F32R)
        K.relu_mlp = c.put("relu_mlp", [P, 2, SLAB_N])
        K.sq = c.put("sq", [P, 2, SLAB_N])
        c = Cursor(R)
        K.ln_gain = c.put("ln_gain", [P, D])
        K.ln_bias = c.put("ln_bias", [P, D])
        K.lam_in = place("lam_in", [P, 4, HEAD_DIM], R)
        K.qkv = place("qkv", [P, TOK_TILES, 3 * D], R)
        c = Cursor(qkv_end)
        K.head_gain = c.put("head_gain", [P, 2, HEAD_DIM])
        K.rope_cos = c.put("rope_cos", [P, LAT_TILES, HEAD_DIM])
        K.rope_sin = c.put("rope_sin", [P, LAT_TILES, HEAD_DIM])
        K.sink_b = c.put("sink_b", [P, 16])
        K.col_mask = c.put("col_mask", [P, GRID_W])
        K.shift = c.put("shift", [HEAD_DIM, 3 * GRID_W - 1])
        K.rpbT = c.put("rpbT", [HEAD_DIM, 16, 16])
        K.near_mask = c.put("near_mask", [P, 2, P])
        K.rpb_rows = c.put("rpb_rows", [P, 2, REL_COLS])
        c = Cursor(R)
        K.qkv2 = c.put("qkv2", [P, TOK_TILES, 3 * SLAB_N])
        K.roped = c.put("roped", [P, LAT_TILES, 20 * HEAD_DIM])
        c = Cursor(H)
        K.head_sq = c.put("head_sq", [P, 2, 2 * D])
        K.head_swap = c.put("head_swap", [P, 2, 2 * D])
        c = Cursor(H)
        K.heads = [c.put(f"heads{q}", [P, TOK_TILES, P]) for q in range(3)]
        K.headsT = [c.put(f"headsT{q}", [P, N_TOK]) for q in range(3)]
        K.p_mat = [c.put(f"p_mat{m}", [P, N_TOK]) for m in range(2)]
        K.pT_mat = [c.put(f"pT_mat{m}", [P, N_TOK]) for m in range(2)]
        K.w_mat = place("w_mat", [P, N_TOK], c.at)
        K.G = place("G", [P, GRID_W, 2, 16], c.at)
        c = Cursor(R)
        K.x_tok = c.put("x_tok", [P, TOK_TILES, SSM_INNER])
        K.BC = c.put("BC", [P, 2 * SSM_GROUPS, N_TOK])
        tail = c.at
        K.relu_conv = c.put("relu_conv", [P, 2, SLAB_N])
        conv_out1 = c.put("conv_out1", [P, 2, OUT])
        c = Cursor(tail)
        K.tri = c.put("tri", [P, 2, P])
        K.order_mask = c.put("order_mask", [P, 2, P])
        K.ones = c.put("ones", [P, P])
        c = Cursor(X)
        K.xt = c.put("xt", [P, 4, ROW])
        K.conv_out = [c.put("conv_out0", [P, 2, OUT]), conv_out1]
        K.dt = c.put("dt", [P, TOK_TILES, 2 * SSM_HEADS])
        K.a = c.put("a", [P, TOK_TILES, 2 * SSM_HEADS])
        K.conv_cols = c.put("conv_cols", [P, TAPS * 24])
        K.vec_cols = c.put("vec_cols", [P, 48])
        assert c.at <= H
        K.z_buf = place("z_buf", [P, LAT_TILES, SLAB_N], X)
        c = Cursor(X)
        K.decay = c.put("decay", [P, 2, GROUP_HEADS, P])
        K.z_g = c.put("z_g", [P, LAT_TILES, GROUP_W])
        K.cbT = c.put("cbT", [P, LAT_TILES, P])
        c = Cursor(H)
        K.BT_g = c.put("BT_g", [P, N_TOK])
        K.CT_g = c.put("CT_g", [P, N_TOK])
        K.B_tok = c.put("B_tok", [P, TOK_TILES, SSM_STATE])
        K.xdt = c.put("xdt", [P, TOK_TILES, GROUP_W])
        K.xdts = c.put("xdts", [P, TOK_TILES, GROUP_W])
        K.y = c.put("y", [P, LAT_TILES, GROUP_W])
        K.state = c.put("state", [P, GROUP_W])
        K.y_tmp = c.put("y_tmp", [P, GROUP_W])
        K.cs = c.put("cs", [P, 288])
        K.cs_exp = c.put("cs_exp", [P, 288])
        K.dt_g = c.put("dt_g", [P, 2, TOK_TILES, GROUP_HEADS])
        K.a_g = c.put("a_g", [P, 2, TOK_TILES, GROUP_HEADS])
        assert c.at <= H + 2 * tile_bytes
        c = Cursor(R)
        K.dt_w = c.put("dt_w", [P, KD, 2 * SSM_HEADS])
        K.dt_w_hi = c.put("dt_w_hi", [P, KD, 2 * SSM_HEADS], F32R)
        K.dt_w_lo = c.put("dt_w_lo", [P, KD, 2 * SSM_HEADS], F32R)
        K.dt_bias = c.put("dt_bias", [P, 2 * SSM_HEADS])
        K.a_neg = c.put("a_neg", [P, 2 * SSM_HEADS])
        K.conv_rows = c.put("conv_rows", [P, P])
        K.vec_rows = c.put("vec_rows", [P, P])
        c = Cursor(H)
        K.yT_hi = c.put("yT_hi", [P, 16, N_LAT], F32R)
        K.y_feat = c.put("y_feat", [P, 2, N_TOK])
        K.yT_lo = place("yT_lo", [P, 16, N_LAT], R + TOK_TILES * SSM_INNER * 4, F32R)

        K.psum = ctx.enter_context(nc.psum_tensor("psum", [P, 8, 512], F32))
        K.bank = [K.psum[:, b, :] for b in range(8)]
        K.x_dram = nc.dram_tensor("x_rest", [N_LAT, D], F32).ap()
        K.z_dram = nc.dram_tensor("z_rest", [N_LAT, SSM_INNER], F32).ap()

        K.credited = []

        def sem(name, credit=CREDIT):
            s = Sem(ctx.enter_context(nc.semaphore(name)), credit)
            if credit:
                K.credited.append(s)
            return s

        K.hi_done = sem("hi_done", 0)
        K.lo_done = sem("lo_done", 0)
        K.w_used = sem("w_used", 0)
        K.small_loaded = sem("small_loaded", 0)
        K.inputs_loaded = sem("inputs_loaded", 0)
        K.stored = sem("stored", 0)
        K.x_stored = sem("x_stored", 0)
        K.z_loaded = sem("z_loaded", 0)
        K.raw_loaded = [sem(f"raw_loaded{h}", 0) for h in range(2)]
        K.mod_loaded = [sem(f"mod_loaded{s}", 0) for s in range(6)]
        K.z_stored = [sem(f"z_stored{j}") for j in range(LAT_TILES)]
        K.mm_done = sem("mm_done")
        K.evacuated = sem("evacuated")
        K.scaled = sem("scaled")
        K.added = sem("added")
        K.turned = sem("turned")
        K.relu_done = sem("relu_done")
        K.sq_done = sem("sq_done")
        K.u_hi_done = sem("u_hi_done")
        K.u_lo_done = sem("u_lo_done")
        K.normed = sem("normed")
        K.feat_done = sem("feat_done")
        K.feat_hi = sem("feat_hi")
        K.feat_lo = sem("feat_lo")
        K.rstd_done = sem("rstd_done")
        K.act_chain = sem("act_chain")
        K.dve_chain = sem("dve_chain")
        K.pool_chain = sem("pool_chain")
        K.mod_used = sem("mod_used")
        K.mod_rows = sem("mod_rows")
        K.row_out = sem("row_out")
        K.mod_cols = sem("mod_cols")
        K.c_done = sem("c_done")
        K.sums_done = sem("sums_done")
        K.gained = sem("gained")
        K.swapped = sem("swapped")
        K.rotated = sem("rotated")
        K.staged = sem("staged")
        K.src_turned = sem("src_turned")
        K.src_read = sem("src_read")
        K.s_done = sem("s_done")
        K.nm_done = sem("nm_done")
        K.p_done = sem("p_done")
        K.w_done = sem("w_done")
        K.pt_done = sem("pt_done")
        K.o_done = sem("o_done")
        K.o_read = sem("o_read")
        K.g_done = sem("g_done")
        K.g_ready = sem("g_ready")
        K.xt_read = sem("xt_read")
        K.conv_done = sem("conv_done")
        K.silu_done = sem("silu_done")
        K.back_done = sem("back_done")
        K.back_read = sem("back_read")
        K.tap_done = sem("tap_done")
        K.a_neg_done = sem("a_neg_done")
        K.cs_done = sem("cs_done")
        K.cs_read = sem("cs_read")
        K.decay_done = sem("decay_done")
        K.bc_done = sem("bc_done")
        K.diff_done = sem("diff_done")
        K.l_done = sem("l_done")
        K.m_done = sem("m_done")
        K.yd_done = sem("yd_done")
        K.yd_read = sem("yd_read")
        K.yo_done = sem("yo_done")
        K.y_read = sem("y_read")
        K.st_done = sem("st_done")
        K.state_done = sem("state_done")
        K.xdt_done = sem("xdt_done")
        K.xdt_part = sem("xdt_part")
        K.cb_done = sem("cb_done")
        K.cb_read = sem("cb_read")
        K.y_done = sem("y_done")
        K.ss_done = sem("ss_done")
        K.fin_done = sem("fin_done")
        K.pt_read = [sem(f"pt_read{m}") for m in range(2)]
        K.slabs = 0
        K.c_ident, K.c_shift, K.c_col_mask = A["const_ident"], A["const_shift"], A["const_col_mask"]
        K.c_tri, K.c_order_mask, K.c_ones = A["const_tri"], A["const_order_mask"], A["const_ones"]

        every, latent = list(range(TOK_TILES)), list(range(LAT_TILES))
        w_in = A["ssm_w_in_2"][0]
        streams = [
            columns_stream(A["a_w_qkv"][0], 6), columns_stream(A["a_w_o"][0], 2), mlp_stream(A["w_mlp1"][0], A["w_mlp2"][0]),
            columns_stream(A["b_w_qkv"][0], 6), columns_stream(A["b_w_o"][0], 2), mlp_stream(A["w_mlp1"][1], A["w_mlp2"][1]),
            columns_stream(A["att_w_in_2"][0], 3), columns_stream(A["att_w_out_2"][0], 2), mlp_stream(A["ff_w1_2"][0], A["ff_w2_2"][0]),
            columns_stream(w_in, 4, SSM_INNER), columns_stream(w_in, 2, 2 * SSM_INNER), columns_stream(w_in, 4),
            rows_stream(A["ssm_w_out_2"][0]), mlp_stream(A["ff_w1_2"][1], A["ff_w2_2"][1])]
        following = iter(zip(streams, streams[1:] + [None]))

        def next_streams():
            s, n = next(following)
            return dict(stream=s, nxt=n)

        def modulated(first_shift):
            return dict(scale=lambda k, cls: K.mod_scale[:, k, cls:cls + 1],
                        bias=lambda k, cls: K.modT[:, first_shift * KD + k, cls:cls + 1])

        x_at = lambda t, k: K.x[:, t, k * P:(k + 1) * P]
        xhat_at = lambda t, k: K.xhat[:, t, k * P:(k + 1) * P]
        qkv_at = lambda t, k: K.qkv[:, t, k * P:(k + 1) * P]
        qkv2_at = lambda t, k: K.qkv2[:, t, k * P:(k + 1) * P]

        def to(dst):
            return lambda act, count, n, t, bank, j: copy_out(K, dst, act, count, n, t, bank, j)

        def gated(dve, count, n, t, bank, j):
            gate_out(K, dve, count, n, t, bank, j)

        def mlp(tiles):
            K.relu = K.relu_mlp
            mlp_stage(K, **next_streams(), tiles=tiles)

        start_stage(K, A["x"][0], A["ctx"][0], streams[0])

        mod_stage(K, A["w_mod"][0], A["b_mod"][0], A["c"][0], A["c_ctx"], A["norm1_g"][0], A["norm2_g"][0], A["a_subln_g"][0])
        scale_stage(K, 1, NORM1_AT)
        operand_stage(K, xhat_at, KD, True, K.hT_hi, K.hT_lo, **modulated(0), rms_of=K.x)
        lambda_stage(K, *(A[f"a_lambda_{n}"][0] for n in ("q1", "k1", "q2", "k2")))
        gemm_stage(K, **next_streams(), k_tiles=KD, tiles=every, evacuate=to(K.qkv), evac_on="act")
        head_norm_stage(K, K.qkv, 32, HEAD_DIM, every, gains=(A["a_q_norm_g"][0], A["a_k_norm_g"][0]),
                        rope=(A["const_cos_pairs"], A["const_sin_pairs"]))

        def stage_qk(pool, i, pi):
            pool.tensor_copy(K.heads[0][:, :, :], K.qkv[:, :, ds(i * P, P)])
            pool.tensor_copy(K.heads[1][:, :, :], K.qkv[:, :, ds(i * P + D, P)]).then_inc(K.staged.h, 1)

        full = [0, 1, 2, 3, 4, 5]
        attention_stage(K, [Unit(t, full) for t in latent] + [Unit(t, [4, 5]) for t in (4, 5)], PAIRS, 1, stage_qk,
                        lambda i, pi, m, kt: K.qkv[:, kt, ds(i * P + 2 * D, P)],
                        lambda i, pi, t: K.qkv[:, t, ds(i * P, P)], diff=True)
        head_norm_stage(K, K.qkv, PAIRS, P, every)
        operand_stage(K, qkv_at, KD, True, K.hT_hi, K.hT_lo, scale=lambda k, cls: K.sub_gain[:, 0:1])
        gate_stage(K, 2)
        gemm_stage(K, **next_streams(), k_tiles=KD, tiles=every, evacuate=gated, evac_on="dve")
        scale_stage(K, 4, NORM2_AT)
        operand_stage(K, xhat_at, KD, True, K.hT_hi, K.hT_lo, **modulated(3), rms_of=K.x)
        gate_stage(K, 5)
        mlp(every)

        mod_stage(K, A["w_mod"][1], A["b_mod"][1], A["c"][0], A["c_ctx"], A["norm1_g"][1], A["norm2_g"][1])
        scale_stage(K, 1, NORM1_AT)
        operand_stage(K, xhat_at, KD, True, K.hT_hi, K.hT_lo, **modulated(0), rms_of=K.x)
        gemm_stage(K, **next_streams(), k_tiles=KD, tiles=every, evacuate=to(K.qkv), evac_on="act")
        head_norm_stage(K, K.qkv, 32, HEAD_DIM, every, gains=(A["b_q_norm_g"][0], A["b_k_norm_g"][0]))
        bias_table_stage(K, A["b_rpb"][0])
        attention_stage(K, [Unit(t, full) for t in latent], PAIRS, 1, stage_qk,
                        lambda i, pi, m, kt: K.qkv[:, kt, ds(i * P + (2 * D + m * HEAD_DIM), HEAD_DIM)],
                        lambda i, pi, t: K.qkv[:, t, ds(i * P, P)], rel_bias=True)
        operand_stage(K, qkv_at, KD, False, K.hT_hi, K.hT_lo)
        gate_stage(K, 2, 1)
        gemm_stage(K, **next_streams(), k_tiles=KD, tiles=latent, evacuate=gated, evac_on="dve")
        scale_stage(K, 4, NORM2_AT)
        operand_stage(K, xhat_at, KD, False, K.hT_hi, K.hT_lo, **modulated(3), rms_of=K.x)
        gate_stage(K, 5, 1)
        mlp(latent)

        mod_stage(K, A["w_mod_2"][0], A["b_mod_2"][0], A["c_2"][0], A["c_ctx_2"])
        load_stage(K, [(K.x[:, LAT_TILES:TOK_TILES, :], A["ctx_2"][0].rearrange("(t p) n -> p t n", p=P))])
        scale_stage(K, 1)
        operand_stage(K, x_at, KD, True, K.hT_hi, K.hT_lo, **modulated(0))
        gemm_stage(K, **next_streams(), k_tiles=KD, tiles=every, evacuate=to(K.qkv2), evac_on="act")
        rope_stage(K, 20, (A["const_cos_axes"], A["const_sin_axes"]))
        load_stage(K, [(K.sink_b[:, :], A["att_sink_2"][0].partition_broadcast(P)), (K.near_mask[:, :, :], A["const_near_mask"])])

        def stage_grouped(pool, i, pi):
            q, k = i * (2 * P) + pi * P, i * HEAD_DIM + D
            pool.tensor_copy(K.heads[0][:, 0:LAT_TILES, :], K.roped[:, :, ds(q, P)])
            pool.tensor_copy(K.heads[0][:, LAT_TILES:TOK_TILES, :], K.qkv2[:, LAT_TILES:TOK_TILES, ds(q, P)])
            for m in range(2):
                half = slice(m * HEAD_DIM, (m + 1) * HEAD_DIM)
                pool.tensor_copy(K.heads[1][:, 0:LAT_TILES, half], K.roped[:, :, ds(k, HEAD_DIM)])
                pool.tensor_copy(K.heads[1][:, LAT_TILES:TOK_TILES, half], K.qkv2[:, LAT_TILES:TOK_TILES, ds(k, HEAD_DIM)])
            pool.tensor_copy(K.heads[2][:, :, :], K.qkv2[:, :, ds(q, P)]).then_inc(K.staged.h, 1)

        units = []
        for t in latent:
            near = [s for s in (t - 1, t, t + 1) if 0 <= s < LAT_TILES]
            masks = {2 + i: K.near_mask[:, 0 if s < t else 1, :] for i, s in enumerate(near) if s != t}
            units.append(Unit(t, [4, 5] + near, masks, unrotated=2))
        units += [Unit(t, [4, 5], unrotated=2) for t in (4, 5)]
        attention_stage(K, units, 4, 2, stage_grouped, lambda i, pi, m, kt: K.qkv2[:, kt, ds(i * HEAD_DIM + (D + 4 * HEAD_DIM), HEAD_DIM)],
                        lambda i, pi, t: K.qkv2[:, t, ds(i * (2 * P) + pi * P, P)], sink=True, unrotated=True)
        operand_stage(K, qkv2_at, KD, True, K.hT_hi, K.hT_lo)
        gate_stage(K, 2, alpha=ALPHA)
        gemm_stage(K, **next_streams(), k_tiles=KD, tiles=every, evacuate=gated, evac_on="dve")
        layer_norm_stage(K, A["ln_mix_g_2"][0], A["ln_mix_b_2"][0], every)
        scale_stage(K, 4)
        operand_stage(K, x_at, KD, True, K.hT_hi, K.hT_lo, **modulated(3))
        gate_stage(K, 5, alpha=ALPHA)
        mlp(every)
        layer_norm_stage(K, A["ln_ff_g_2"][0], A["ln_ff_b_2"][0], every)

        mod_stage(K, A["w_mod_2"][1], A["b_mod_2"][1], A["c_2"][0], A["c_ctx_2"])
        scale_stage(K, 1)
        operand_stage(K, x_at, KD, True, K.hT_hi, K.hT_lo, **modulated(0))
        spill_stage(K)
        dt_stage(K, w_in[:, SSM_INNER + 6 * SLAB_N:SSM_INNER + 6 * SLAB_N + 2 * SSM_HEADS],
                 A["ssm_dt_bias_2"][0].rearrange("d h -> (d h)"), A["ssm_a_log_2"][0].rearrange("d h -> (d h)"),
                 A["ssm_conv_w_2"][0], A["ssm_conv_b_2"][0], A["ssm_norm_g_2"][0])
        K.relu = K.relu_conv
        conv_stage(K, **next_streams(), block0=0, back=True)
        conv_stage(K, **next_streams(), block0=16, back=False)
        gemm_stage(K, **next_streams(), k_tiles=KD, tiles=latent, evac_on="act",
                   evacuate=lambda act, count, n, t, bank, j: silu_store_out(K, act, count, n, t, bank, j))
        for s in K.z_stored:
            s.n += 16 * 4
        scan_stage(K, A["ssm_d_2"][0])
        operand_stage(K, lambda t, k: K.x_tok[:, t, k * P:(k + 1) * P], 16, False, K.yT_hi, K.yT_lo,
                      scale=lambda k, cls: K.vec_cols[:, 32 + k:33 + k], feat=K.y_feat)
        reload_stage(K)
        gate_stage(K, 2, 1, alpha=ALPHA)
        gemm_stage(K, **next_streams(), k_tiles=16, tiles=latent, evacuate=gated, evac_on="dve", hi_t=K.yT_hi, lo_t=K.yT_lo)
        layer_norm_stage(K, A["ln_mix_g_2"][1], A["ln_mix_b_2"][1], latent)
        scale_stage(K, 4)
        operand_stage(K, x_at, KD, False, K.hT_hi, K.hT_lo, **modulated(3))
        gate_stage(K, 5, 1, alpha=ALPHA)
        mlp(latent)
        layer_norm_stage(K, A["ln_ff_g_2"][1], A["ln_ff_b_2"][1], latent, store=out)


def constants():
    t = np.arange(N_LAT)
    row, col = (t // GRID_W).astype(np.float32), (t % GRID_W).astype(np.float32)
    lay = lambda a: np.ascontiguousarray(a.reshape(LAT_TILES, P, -1).transpose(1, 0, 2), np.float32)
    c = {"ident": np.eye(P, dtype=np.float32), "ones": np.ones((P, P), np.float32)}
    nf = HEAD_DIM // 4
    inv = (10000.0 ** (-np.arange(nf, dtype=np.float32) / nf)).astype(np.float32)
    ang = np.concatenate([row[:, None] * inv, col[:, None] * inv], axis=-1)
    c["cos_pairs"] = lay(np.repeat(np.cos(ang), 2, axis=-1))
    c["sin_pairs"] = lay(np.stack([-np.sin(ang), np.sin(ang)], axis=-1).reshape(N_LAT, HEAD_DIM))
    ar, ac = row[:, None] * inv, col[:, None] * inv
    c["cos_axes"] = lay(np.concatenate([np.cos(ar), np.cos(ar), np.cos(ac), np.cos(ac)], axis=-1))
    c["sin_axes"] = lay(np.concatenate([-np.sin(ar), np.sin(ar), -np.sin(ac), np.sin(ac)], axis=-1))
    shift = np.zeros((HEAD_DIM, 3 * GRID_W - 1), np.float32)
    for r in range(2):
        for j in range(REL_COLS):
            shift[32 * r + j, GRID_W * r + GRID_W - 1 + WINDOW_COLS - 1 - j] = 1
    c["shift"] = shift
    q, k = np.arange(GRID_W)[:, None], np.arange(GRID_W)[None, :]
    start = np.clip(q - WINDOW_COLS // 2, 0, GRID_W - WINDOW_COLS)
    inside = (k >= start) & (k < start + WINDOW_COLS)
    c["col_mask"] = np.tile(np.where(inside, 0, NEG).astype(np.float32), (2, 1))
    q, k = np.arange(P)[:, None], np.arange(P)[None, :]
    c["near_mask"] = np.stack([np.where(k >= q, 0, NEG), np.where(k <= q, 0, NEG)], axis=1).astype(np.float32)
    c["tri"] = np.stack([q <= k, q >= k], axis=1).astype(np.float32)
    c["order_mask"] = np.where(c["tri"] > 0, 0, NEG).astype(np.float32)
    return c


_INS = ["x", "c", "ctx", "c_ctx", "norm1_g", "norm2_g", "w_mod", "b_mod", "w_mlp1", "w_mlp2", "a_w_qkv", "a_q_norm_g", "a_k_norm_g",
        "a_lambda_q1", "a_lambda_k1", "a_lambda_q2", "a_lambda_k2", "a_subln_g", "a_w_o", "b_w_qkv", "b_q_norm_g", "b_k_norm_g",
        "b_rpb", "b_w_o", "c_2", "ctx_2", "c_ctx_2", "w_mod_2", "b_mod_2", "ln_mix_g_2", "ln_mix_b_2", "ln_ff_g_2", "ln_ff_b_2",
        "att_w_in_2", "att_w_out_2", "att_sink_2", "ssm_w_in_2", "ssm_conv_w_2", "ssm_conv_b_2", "ssm_dt_bias_2", "ssm_a_log_2",
        "ssm_d_2", "ssm_norm_g_2", "ssm_w_out_2", "ff_w1_2", "ff_w2_2"]


def kernel(**inputs):
    import numpy as _np
    import concourse.bacc as _bacc
    from concourse import mybir as _mybir
    from concourse.bass_utils import run_bass_kernel_spmd as _run

    nc = _bacc.Bacc("TRN2", target_bir_lowering=False, num_devices=1)
    arrays, A = {}, {}
    for name in _INS:
        a = _np.ascontiguousarray(inputs[name])
        arrays[f"in_{name}"] = a
        A[name] = nc.dram_tensor(f"in_{name}", a.shape, _mybir.dt.from_np(a.dtype), kind="ExternalInput").ap()
    for name, a in constants().items():
        arrays[f"const_{name}"] = a
        A[f"const_{name}"] = nc.dram_tensor(f"const_{name}", a.shape, _mybir.dt.from_np(a.dtype), kind="ExternalInput").ap()
    out = nc.dram_tensor("out", (1, N_LAT, D), _mybir.dt.float32, kind="ExternalOutput").ap()
    program(nc, A, out[0])
    r = _run(nc, [arrays], core_ids=[0])
    return r.results[0]["out"]
```

```python
from contextlib import ExitStack

import numpy as np

import concourse.bass as bass
from concourse import mybir

P = 128
D = 1024
KD = D // P
LAT_TILES, CTX_TILES = 4, 2
TOK_TILES = LAT_TILES + CTX_TILES
N_LAT, N_CTX = LAT_TILES * P, CTX_TILES * P
N_TOK = N_LAT + N_CTX
GRID_W = 64
HEAD_DIM = 64
PAIRS = D // (2 * HEAD_DIM)
SLAB_K, SLAB_N = 4, 512
D_FF = 4 * D
FF_CHUNK = 512
LAM_INIT = 0.8 - 0.6 * float(np.exp(-0.3 * 0))
SCALE = HEAD_DIM ** -0.5
ALPHA = (2.0 * 2) ** 0.25
NORM_EPS = 1e-6
LN_EPS = 1e-5
NEG = -1e30
WINDOW_COLS = 16
N_ROWS = N_LAT // GRID_W
REL_ROWS, REL_COLS = 15, 31

F32 = mybir.dt.float32
F32R = mybir.dt.float32r
ALU = mybir.AluOpType
ACT = mybir.ActivationFunctionType
AX = mybir.AxisListType
ds = bass.ds


class Sem:

    def __init__(self, handle, credit=0):
        self.h = handle
        self.n = credit


class Chain:

    def __init__(self, eng, sem, start=0):
        self.eng, self.sem, self.start, self.k = eng, sem, start, 0

    def __call__(self, ins):
        self.k += 1
        ins.then_inc(self.sem.h, 1)
        self.eng.wait_ge(self.sem.h, self.sem.n + self.start + self.k)


class Kernel:
    pass


class Stream:

    def __init__(self, count, half):
        self.count, self.half = count, half


def columns_stream(w, n_slabs, col0=0):
    rows = w.rearrange("(k p) n -> p k n", p=P)
    return Stream(n_slabs, lambda n, h: rows[:, h * SLAB_K:(h + 1) * SLAB_K, ds(col0 + n * SLAB_N, SLAB_N)])


def rows_stream(w):
    rows = w.rearrange("(k p) n -> p k n", p=P)
    return Stream(4, lambda n, h: rows[:, (n % 2) * 8 + h * SLAB_K:(n % 2) * 8 + (h + 1) * SLAB_K,
                                       (n // 2) * SLAB_N:(n // 2 + 1) * SLAB_N])


def mlp_stream(w1, w2):
    up = w1.rearrange("(k p) n -> p k n", p=P)
    down = w2.rearrange("(k p) n -> p k n", p=P)

    def half(chunk, part, h):
        if part == 0:
            return up[:, h * SLAB_K:(h + 1) * SLAB_K, ds(chunk * FF_CHUNK, FF_CHUNK)]
        return down[:, ds(chunk * SLAB_K, SLAB_K), h * SLAB_N:(h + 1) * SLAB_N]

    s = Stream(2 * (D_FF // FF_CHUNK), lambda n, h: half(n // 2, n % 2, h))
    s.chunk_half = half
    return s


def load_half(K, sp, g, h, src, first=False):
    if not first:
        sp.wait_ge(K.lo_done.h, 2 * (g - 1) + h + 1)
    sp.dma_start(K.raw[h][:, :, :], src).then_inc(K.raw_loaded[h].h, 16)


def split_hi(K, act, g, h):
    act.wait_ge(K.raw_loaded[h].h, 16 * (g + 1))
    act.wait_ge(K.w_used.h, 2 * (g - 1) + h + 1)
    act.activation(K.w_hi[h][:, :, :], K.raw[h][:, :, :], ACT.Copy).then_inc(K.hi_done.h, 1)


def split_lo(K, dve, g, h):
    dve.wait_ge(K.hi_done.h, 2 * g + h + 1)
    dve.tensor_tensor(K.w_lo[h][:, :, :], K.raw[h][:, :, :], K.w_hi[h][:, :, :].bitcast(F32),
                      ALU.subtract).then_inc(K.lo_done.h, 1)


def stream_loads(K, sp, stage):
    g0, s, nxt = stage.g0, stage.stream, stage.next_stream
    if s.count > 2:
        if stage.chunked:
            with sp.Fori(1, s.count // 2) as c:
                for part in range(2):
                    for h in range(2):
                        load_half(K, sp, g0 + 2 * c + part, h, s.chunk_half(c, part, h))
        elif stage.unrolled:
            for n in range(2, s.count):
                for h in range(2):
                    load_half(K, sp, g0 + n, h, s.half(n, h))
        else:
            with sp.Fori(2, s.count) as n:
                for h in range(2):
                    load_half(K, sp, g0 + n, h, s.half(n, h))
    if nxt is not None:
        for n in range(2):
            for h in range(2):
                load_half(K, sp, g0 + s.count + n, h, nxt.half(n, h))


def product(pe, out, hi_a, lo_a, hi_w, lo_w, first, last):
    pe.matmul(out, hi_a, hi_w, start=first, stop=False)
    pe.matmul(out, hi_a, lo_w, start=False, stop=False)
    return pe.matmul(out, lo_a, hi_w, start=False, stop=last)


class Stage:
    def __init__(self, K, stream, next_stream, chunked=False, unrolled=False):
        self.g0, self.stream, self.next_stream = K.slabs, stream, next_stream
        self.chunked, self.unrolled = chunked, unrolled
        K.slabs += stream.count
        self.last = next_stream is None


def ahead_loop(eng, stage, body):
    n = stage.stream.count // (2 if stage.chunked else 1)
    if stage.unrolled:
        for i in range(n):
            body(i, not (stage.last and i == n - 1))
        return
    loops = n - 1 if stage.last else n
    if loops > 0:
        with eng.Fori(0, loops) as i:
            body(i, True)
    if stage.last:
        body(n - 1, False)


def gemm_stage(K, stream, nxt, k_tiles, tiles, evacuate, evac_on, hi_t=None, lo_t=None):
    nc = K.nc
    hi_t = hi_t or K.hT_hi
    lo_t = lo_t or K.hT_lo
    unrolled = k_tiles > 2 * SLAB_K
    st = Stage(K, stream, nxt, unrolled=unrolled)
    per = k_tiles // (2 * SLAB_K)
    nt = len(tiles)
    freed = K.scaled if evac_on == "dve" else K.evacuated
    mm0, ev0 = K.mm_done.n, freed.n

    def tile_done(eng, n, block_n, j):
        if j < nt - 1:
            eng.wait_ge(K.mm_done.h, mm0 + (nt - 1) * block_n + j + 1)
        else:
            eng.wait_ge(K.w_used.h, 2 * (st.g0 + n) + 2)

    def pe_body(n, _):
        part = n % per if unrolled else 0
        block_n = n // per if unrolled else n
        for h in range(2):
            pe = nc.tensor
            pe.wait_ge(K.lo_done.h, 2 * (st.g0 + n) + h + 1)
            for j, t in enumerate(tiles):
                first, last = part == 0 and h == 0, part == per - 1 and h == 1
                if first:
                    pe.wait_ge(freed.h, ev0 + nt * (block_n - 1) + j + 1)
                for k in range(SLAB_K):
                    kk = part * 2 * SLAB_K + h * SLAB_K + k
                    mm = product(pe, K.bank[j][:, :], hi_t[:, kk, t * P:(t + 1) * P], lo_t[:, kk, t * P:(t + 1) * P],
                                 K.w_hi[h][:, k, :], K.w_lo[h][:, k, :], first and k == 0, last and k == SLAB_K - 1)
                if last and j < nt - 1:
                    mm.then_inc(K.mm_done.h, 1)
            mm.then_inc(K.w_used.h, 1)

    def reads(eng, n, who):
        if who != evac_on:
            return
        part = n % per if unrolled else per - 1
        block_n = n // per if unrolled else n
        if part != per - 1:
            return
        for j, t in enumerate(tiles):
            tile_done(eng, n, block_n, j)
            evacuate(eng, K.scaled.n + nt * block_n + j, block_n, t, K.bank[j], j)

    with nc.Block() as block:
        @block.sync
        def _(sp):
            stream_loads(K, sp, st)

        @block.scalar
        def _(act):
            def body(n, ahead):
                if ahead:
                    split_hi(K, act, st.g0 + n + 1, 0)
                reads(act, n, "act")
                if ahead:
                    split_hi(K, act, st.g0 + n + 1, 1)
            ahead_loop(act, st, body)

        @block.vector
        def _(dve):
            def body(n, ahead):
                if ahead:
                    split_lo(K, dve, st.g0 + n + 1, 0)
                reads(dve, n, "dve")
                if ahead:
                    split_lo(K, dve, st.g0 + n + 1, 1)
            ahead_loop(dve, st, body)

        if evac_on == "dve":
            @block.gpsimd
            def _(pool):
                blocks = stream.count // per
                with pool.Fori(0, blocks) as n:
                    for j, t in enumerate(tiles):
                        residual_add(K, pool, K.scaled.n + nt * n + j, t, n, j)

        @block.tensor
        def _(pe):
            if unrolled:
                for n in range(stream.count):
                    pe_body(n, None)
            else:
                with pe.Fori(0, stream.count) as n:
                    pe_body(n, None)
    K.mm_done.n += (nt - 1) * (stream.count // per)
    freed.n += nt * (stream.count // per)


def copy_out(K, dst, act, _, n, t, bank, j):
    act.activation(dst[:, t, ds(n * SLAB_N, SLAB_N)], bank[:, :], ACT.Copy).then_inc(K.evacuated.h, 1)


def gate_out(K, dve, count, n, t, bank, j):
    dve.wait_ge(K.added.h, count - 1)
    cls = 0 if t < LAT_TILES else 1
    dve.tensor_tensor(K.scaled_buf[:, j % 2, :], bank[:, :], K.gate[:, cls, ds(n * SLAB_N, SLAB_N)], ALU.mult)\
       .then_inc(K.scaled.h, 1)


def residual_add(K, pool, count, t, n, j):
    pool.wait_ge(K.scaled.h, count + 1)
    x = K.x[:, t, ds(n * SLAB_N, SLAB_N)]
    pool.tensor_tensor(x, x, K.scaled_buf[:, j % 2, :], ALU.add).then_inc(K.added.h, 1)


def mlp_stage(K, stream, nxt, tiles):
    nc = K.nc
    st = Stage(K, stream, nxt, chunked=True)
    nt = len(tiles)
    mm0, tr0, re0, sq0, uh0, ul0, sc0 = (s.n for s in (
        K.mm_done, K.turned, K.relu_done, K.sq_done, K.u_hi_done, K.u_lo_done, K.scaled))
    chunks = D_FF // FF_CHUNK

    def tile_done(eng, c, which, j):
        if j < nt - 1:
            eng.wait_ge(K.mm_done.h, mm0 + (nt - 1) * (3 * c + which) + j + 1)
        else:
            eng.wait_ge(K.w_used.h, 2 * (st.g0 + 2 * c) + 2 + which)

    with nc.Block() as block:
        @block.sync
        def _(sp):
            stream_loads(K, sp, st)

        @block.scalar
        def _(act):
            def square(c, j):
                act.wait_ge(K.turned.h, tr0 + nt * c + j + 1)
                act.wait_ge(K.u_lo_done.h, ul0 + nt * c + j - 1)
                act.activation(K.sq[:, j % 2, :], K.bank[6 + j % 2][:, :], ACT.Square).then_inc(K.sq_done.h, 1)

            def body(c, ahead):
                g = st.g0 + 2 * c
                split_hi(K, act, g + 1, 0)
                for j in range(nt):
                    tile_done(act, c, 0, j)
                    act.wait_ge(K.turned.h, tr0 + nt * c + j - 1)
                    act.activation(K.relu[:, j % 2, :], K.bank[j][:, :], ACT.Relu).then_inc(K.relu_done.h, 1)
                    if j:
                        square(c, j - 1)
                square(c, nt - 1)
                split_hi(K, act, g + 1, 1)
                if ahead:
                    split_hi(K, act, g + 2, 0)
                    split_hi(K, act, g + 2, 1)
            ahead_loop(act, st, body)

        @block.vector
        def _(dve):
            def parts(c, j):
                t = tiles[j]
                view = lambda u: u[:, :, t * P:(t + 1) * P]
                square = K.sq[:, j % 2, :].rearrange("p (k t) -> p k t", k=SLAB_K)
                dve.wait_ge(K.sq_done.h, sq0 + nt * c + j + 1)
                dve.wait_ge(K.w_used.h, 2 * (st.g0 + 2 * c) - 1 + 1)
                dve.tensor_copy(view(K.uT_hi), square).then_inc(K.u_hi_done.h, 1)
                dve.wait_ge(K.u_hi_done.h, uh0 + nt * c + j + 1)
                dve.tensor_tensor(view(K.uT_lo), square, view(K.uT_hi).bitcast(F32), ALU.subtract)\
                   .then_inc(K.u_lo_done.h, 1)

            def body(c, ahead):
                g = st.g0 + 2 * c
                split_lo(K, dve, g + 1, 0)
                for j in range(nt):
                    parts(c, j)
                split_lo(K, dve, g + 1, 1)
                for h in range(2):
                    for j, t in enumerate(tiles):
                        tile_done(dve, c, 1 + h, j)
                        gate_out(K, dve, sc0 + 2 * nt * c + h * nt + j, h, t, K.bank[j], j)
                    if ahead:
                        split_lo(K, dve, g + 2, h)
            ahead_loop(dve, st, body)

        @block.gpsimd
        def _(pool):
            with pool.Fori(0, chunks) as c:
                for h in range(2):
                    for j, t in enumerate(tiles):
                        residual_add(K, pool, sc0 + 2 * nt * c + h * nt + j, t, h, j)

        @block.tensor
        def _(pe):
            def turn(c, j):
                pe.wait_ge(K.relu_done.h, re0 + nt * c + j + 1)
                pe.wait_ge(K.sq_done.h, sq0 + nt * c + j - 1)
                for k in range(SLAB_K):
                    mm = pe.transpose(K.bank[6 + j % 2][:, k * P:(k + 1) * P], K.relu[:, j % 2, k * P:(k + 1) * P], K.ident[:, :])
                mm.then_inc(K.turned.h, 1)

            with pe.Fori(0, chunks) as c:
                g = st.g0 + 2 * c
                for h in range(2):
                    pe.wait_ge(K.lo_done.h, 2 * g + h + 1)
                    for j, t in enumerate(tiles):
                        if h == 0:
                            pe.wait_ge(K.scaled.h, sc0 + 2 * nt * (c - 1) + nt + j + 1)
                        for k in range(SLAB_K):
                            kk = h * SLAB_K + k
                            mm = product(pe, K.bank[j][:, :], K.hT_hi[:, kk, t * P:(t + 1) * P],
                                         K.hT_lo[:, kk, t * P:(t + 1) * P], K.w_hi[h][:, k, :], K.w_lo[h][:, k, :],
                                         kk == 0, kk == KD - 1)
                        if j == nt - 1:
                            mm.then_inc(K.w_used.h, 1)
                        elif h == 1:
                            mm.then_inc(K.mm_done.h, 1)
                        if h == 1 and j:
                            turn(c, j - 1)
                for h in range(2):
                    pe.wait_ge(K.lo_done.h, 2 * (g + 1) + h + 1)
                    for j, t in enumerate(tiles):
                        if h == 0:
                            pe.wait_ge(K.u_lo_done.h, ul0 + nt * c + j + 1)
                            pe.wait_ge(K.relu_done.h, re0 + nt * c + j + 1)
                        else:
                            pe.wait_ge(K.scaled.h, sc0 + 2 * nt * c + j + 1)
                        for k in range(SLAB_K):
                            mm = product(pe, K.bank[j][:, :], K.uT_hi[:, k, t * P:(t + 1) * P],
                                         K.uT_lo[:, k, t * P:(t + 1) * P], K.w_hi[h][:, k, :], K.w_lo[h][:, k, :],
                                         k == 0, k == SLAB_K - 1)
                        mm.then_inc((K.w_used if j == nt - 1 else K.mm_done).h, 1)
                        if h == 0 and j == 0:
                            turn(c, nt - 1)
    K.mm_done.n += 3 * (nt - 1) * chunks
    K.scaled.n += 2 * nt * chunks
    for s in (K.turned, K.relu_done, K.sq_done, K.u_hi_done, K.u_lo_done):
        s.n += nt * chunks


def operand_stage(K, src, k_tiles, ctx, dst_hi, dst_lo, scale=None, bias=None, rms_of=None, feat=None, gate=None, gate_scale=1.0):
    nc = K.nc
    classes = [(0, 0, LAT_TILES)] + ([(1, LAT_TILES, CTX_TILES)] if ctx else [])
    tiles = TOK_TILES if ctx else LAT_TILES
    cols = tiles * P
    feat = feat or K.feat
    nr0, tr0, ft0, fh0, fl0, rs0, mm0 = (s.n for s in (K.normed, K.turned, K.feat_done, K.feat_hi, K.feat_lo, K.rstd_done, K.mm_done))

    def lo_parts(dve):
        for k in range(k_tiles):
            dve.wait_ge(K.feat_done.h, ft0 + len(classes) * (k + 1))
            dve.tensor_copy(dst_hi[:, k, 0:cols], feat[:, k % 2, 0:cols]).then_inc(K.feat_hi.h, 1)
            dve.wait_ge(K.feat_hi.h, fh0 + k + 1)
            dve.tensor_tensor(dst_lo[:, k, 0:cols], feat[:, k % 2, 0:cols], dst_hi[:, k, 0:cols].bitcast(F32),
                              ALU.subtract).then_inc(K.feat_lo.h, 1)

    with nc.Block() as block:
        if rms_of is not None:
            @block.vector
            def _(dve):
                for t in range(tiles):
                    dve.wait_ge(K.rstd_done.h, rs0 + 1)
                    dve.tensor_scalar(K.xhat[:, t, :], K.x[:, t, :], K.rstd[:, t:t + 1], None, ALU.mult)\
                       .then_inc(K.normed.h, 1)
                lo_parts(dve)
        else:
            @block.vector
            def _(dve):
                lo_parts(dve)

        @block.scalar
        def _(act):
            if rms_of is not None:
                link = Chain(act, K.act_chain)
                for t in range(tiles):
                    ins = act.activation(feat[:, :, :].rearrange("p a b -> p (a b)")[:, 0:D], K.x[:, t, :], ACT.Square,
                                         accum_out=K.ssum[:, t:t + 1])
                    link(ins)
                link(act.activation(K.lnms[:, 0:tiles], K.ssum[:, 0:tiles], ACT.Ln, bias=K.eps6[:, 0:1], scale=1.0 / D))
                act.activation(K.rstd[:, 0:tiles], K.lnms[:, 0:tiles], ACT.Exp, scale=-0.5).then_inc(K.rstd_done.h, 1)
                act.wait_ge(K.rstd_done.h, rs0 + 1)
                K.act_chain.n += link.k
            for k in range(k_tiles):
                for c, (cls, t0, n) in enumerate(classes):
                    act.wait_ge(K.turned.h, tr0 + len(classes) * k + c + 1)
                    if k >= 2:
                        act.wait_ge(K.feat_lo.h, fl0 + k - 1)
                    bank = K.bank[2 * (k % 4) + c]
                    out = feat[:, k % 2, t0 * P:(t0 + n) * P]
                    if scale is None:
                        ins = act.activation(out, bank[:, 0:n * P], ACT.Copy)
                    else:
                        b = {} if bias is None else {"bias": bias(k, cls)}
                        ins = act.activation(out, bank[:, 0:n * P], ACT.Identity, scale=scale(k, cls), **b)
                    ins.then_inc(K.feat_done.h, 1)
            if gate is not None:
                for cls in range(len(classes)):
                    act.wait_ge(K.mm_done.h, mm0 + cls + 1)
                    for half in range(2):
                        act.activation(K.gate[:, cls, half * 512:(half + 1) * 512], K.bank[2 * cls + half][:, :], ACT.Copy,
                                       scale=gate_scale)

        @block.tensor
        def _(pe):
            if rms_of is not None:
                pe.wait_ge(K.normed.h, nr0 + tiles)
            for k in range(k_tiles):
                for c, (cls, t0, n) in enumerate(classes):
                    if k >= 4:
                        pe.wait_ge(K.feat_done.h, ft0 + len(classes) * (k - 4) + c + 1)
                    for t in range(n):
                        mm = pe.transpose(K.bank[2 * (k % 4) + c][:, t * P:(t + 1) * P], src(t0 + t, k), K.ident[:, :])
                    mm.then_inc(K.turned.h, 1)
            if gate is not None:
                for cls in range(len(classes)):
                    pe.wait_ge(K.feat_done.h, ft0 + len(classes) * (k_tiles - 3 + cls))
                    gate_rows(K, pe, gate, cls)
    if rms_of is not None:
        K.normed.n += tiles
        K.rstd_done.n += 1
    if gate is not None:
        K.mm_done.n += len(classes)
    K.turned.n += len(classes) * k_tiles
    K.feat_done.n += len(classes) * k_tiles
    K.feat_hi.n += k_tiles
    K.feat_lo.n += k_tiles


class Modulation:

    def __init__(self, layer, w, first, per):
        self.layer, self.w, self.first, self.per = layer, w.rearrange("(k p) n -> p k n", p=P), first, per


def mod_rows(K, pe, out, layer, slab):
    for k in range(KD):
        mm = pe.matmul(out, K.cT[:, layer // 2, k, :], slab[:, k, :], start=k == 0, stop=k == KD - 1)
    return mm


def mod_turn(K, pe, out, row):
    return pe.matmul(out, row, K.ident[0:2, 0:2], start=True, stop=True)


def mod_add(K, dve, layer, n0, count, psum):
    b_at = (1 + layer // 2) * P + (layer % 2) * 6 * KD
    return dve.tensor_tensor(K.modT_all[:, ds(n0 + layer * 6 * KD, count), :], psum.rearrange("p (j c) -> p j c", c=2),
                             K.vecs[:, ds(n0 + b_at, count)].unsqueeze(2).to_broadcast([P, count, 2]), ALU.add)


def start_stage(K, x, ctx, first, w_mod, groups):
    nc = K.nc
    blocks = 4
    rows = w_mod.rearrange("(k p) n -> p k n", p=P)
    ld0 = [s.n for s in K.mod_loaded]
    us0, tr0, cn0, sm0, ro0, mt0 = (s.n for s in (K.mod_used, K.turned, K.c_done, K.small_loaded, K.row_out, K.mod_turned))
    n_vectors = sum(len(g) for g in groups)
    with nc.Block() as block:
        @block.gpsimd
        def _(pool):
            for s in K.credited:
                pool.sem_inc(s.h, CREDIT)
            pool.memset(K.eps6[:, :], NORM_EPS)
            pool.memset(K.eps5[:, :], LN_EPS)
            pool.memset(K.eps_ln[:, :], LN_EPS / ALPHA ** 2)
            pool.memset(K.one[:, :], 1.0)

    with nc.Block() as block:
        @block.sync
        def _(sp):
            sp.dma_start(K.ident[:, :], K.c_ident).then_inc(K.ident_loaded.h, 16)
            for g, vectors in enumerate(groups):
                row = 0
                for v in vectors:
                    n = v.shape[0] // P
                    sp.dma_start(K.vec_in[row:row + n, g, :], v.rearrange("(k p) -> k p", p=P)).then_inc(K.small_loaded.h, 16)
                    row += n
            for b in range(blocks):
                sp.dma_start(K.mod_first[b][:, :, :], rows[:, :, b * SLAB_N:(b + 1) * SLAB_N]).then_inc(K.mod_loaded[b].h, 16)
            sp.dma_start(K.x[:, 0:LAT_TILES, :], x.rearrange("(t p) n -> p t n", p=P)).then_inc(K.inputs_loaded.h, 16)
            sp.dma_start(K.x[:, LAT_TILES:TOK_TILES, :], ctx.rearrange("(t p) n -> p t n", p=P)).then_inc(K.inputs_loaded.h, 16)
            for n in range(2):
                for h in range(2):
                    load_half(K, sp, n, h, first.half(n, h), first=n == 0)

        @block.scalar
        def _(act):
            act.wait_ge(K.c_done.h, cn0 + 1)
            act.activation(K.cexp[:, :], K.vecs[:, 0:4 * KD], ACT.Exp, scale=-1.0).then_inc(K.c_done.h, 1)
            for h in range(2):
                act.wait_ge(K.raw_loaded[h].h, 16)
                act.activation(K.w_hi[h][:, :, :], K.raw[h][:, :, :], ACT.Copy).then_inc(K.hi_done.h, 1)
            act.wait_ge(K.inputs_loaded.h, 32)

        @block.vector
        def _(dve):
            link = Chain(dve, K.dve_chain)
            dve.wait_ge(K.turned.h, tr0 + 1)
            for g, vectors in enumerate(groups):
                n = sum(v.shape[0] for v in vectors) // P
                ins = dve.tensor_copy(K.vecs[:, g * P:g * P + n], K.bank[7][:, g * P:g * P + n])
            ins.then_inc(K.c_done.h, 1)
            dve.wait_ge(K.c_done.h, cn0 + 2)
            link(dve.tensor_scalar(K.cexp[:, :], K.cexp[:, :], 1.0, None, ALU.add))
            link(dve.reciprocal(K.cexp[:, :], K.cexp[:, :]))
            for block_i in range(2):
                at = slice(block_i * 2 * KD, (block_i + 1) * 2 * KD)
                ins = dve.tensor_tensor(K.cT[:, block_i, :, :].rearrange("p k c -> p c k"),
                                        K.vecs[:, at].rearrange("p (c k) -> p c k", c=2),
                                        K.cexp[:, at].rearrange("p (c k) -> p c k", c=2), ALU.mult)
            ins.then_inc(K.c_done.h, 1)
            for b in range(blocks):
                dve.wait_ge(K.mod_used.h, us0 + b + 1)
                dve.tensor_copy(K.first_rows[:, b, :], K.bank[b][0:2, :]).then_inc(K.row_out.h, 1)
            for b in range(blocks):
                dve.wait_ge(K.mod_turned.h, mt0 + b + 1)
                mod_add(K, dve, 0, 4 * b, 4, K.bank[b][:, 0:8])
            for h in range(2):
                split_lo(K, dve, 0, h)
            K.dve_chain.n += link.k

        @block.tensor
        def _(pe):
            pe.wait_ge(K.small_loaded.h, sm0 + 16 * n_vectors)
            pe.wait_ge(K.ident_loaded.h, 16)
            for g, vectors in enumerate(groups):
                n = sum(v.shape[0] for v in vectors) // P
                mm = pe.transpose(K.bank[7][:, g * P:g * P + n], K.vec_in[0:n, g, :], K.ident[0:n, 0:n])
            mm.then_inc(K.turned.h, 1)
            pe.wait_ge(K.c_done.h, cn0 + 3)
            for b in range(blocks):
                pe.wait_ge(K.mod_loaded[b].h, ld0[b] + 16)
                mod_rows(K, pe, K.bank[b][0:2, :], 0, K.mod_first[b]).then_inc(K.mod_used.h, 1)
            for b in range(blocks):
                pe.wait_ge(K.row_out.h, ro0 + b + 1)
                for j in range(4):
                    mm = mod_turn(K, pe, K.bank[b][:, 2 * j:2 * j + 2], K.first_rows[:, b, j * P:(j + 1) * P])
                mm.then_inc(K.mod_turned.h, 1)
    for s in K.mod_loaded:
        s.n += 16
    K.mod_used.n += blocks
    K.row_out.n += blocks
    K.mod_turned.n += blocks
    K.turned.n += 1
    K.c_done.n += 3
    K.small_loaded.n += 16 * n_vectors


def gate_rows(K, pe, part, cls):
    for k in range(KD):
        mm = pe.matmul(K.bank[2 * cls + k // 4][:, (k % 4) * P:(k % 4 + 1) * P],
                       K.modT[:, part * KD + k, cls:cls + 1].to_broadcast([P, P]), K.ident[:, :], start=True, stop=True)
    mm.then_inc(K.mm_done.h, 1)


def gate_stage(K, part, gate_scale):
    mm0 = K.mm_done.n
    with K.nc.Block() as block:
        @block.tensor
        def _(pe):
            gate_rows(K, pe, part, 0)

        @block.scalar
        def _(act):
            act.wait_ge(K.mm_done.h, mm0 + 1)
            for half in range(2):
                act.activation(K.gate[:, 0, half * 512:(half + 1) * 512], K.bank[half][:, :], ACT.Copy, scale=gate_scale)
    K.mm_done.n += 1


def scale_stage(K, part, gain_at=None):
    with K.nc.Block() as block:
        @block.vector
        def _(dve):
            link = Chain(dve, K.dve_chain)
            link(dve.tensor_scalar(K.mod_scale[:, :, :], K.modT[:, part * KD:(part + 1) * KD, :], 1.0, None, ALU.add))
            if gain_at is not None:
                dve.tensor_tensor(K.mod_scale[:, :, :], K.mod_scale[:, :, :],
                                  K.vecs[:, gain_at:gain_at + KD].unsqueeze(2).to_broadcast([P, KD, 2]), ALU.mult)
            K.dve_chain.n += link.k


def head_norm_stage(K, src, heads, dim, tiles, gains=None, rope=None):
    nc = K.nc
    width = heads * dim
    sq0, ss0, rs0, nm0, ga0, t20, sm0 = (s.n for s in (
        K.sq_done, K.sums_done, K.rstd_done, K.normed, K.gained, K.swapped, K.small_loaded))
    cols = lambda t: src[:, t, 0:width]
    by_head = lambda ap: ap.rearrange("p (h d) -> p h d", d=dim)
    loads = (2 if gains else 0) + (2 if rope else 0)
    def rotate(dve, i, t):
        x = by_head(cols(t))
        cos = K.rope_cos[:, t, :].unsqueeze(1).to_broadcast([P, heads, dim])
        if i == 0:
            dve.wait_ge(K.small_loaded.h, sm0 + 16 * loads)
        dve.wait_ge(K.swapped.h, t20 + i + 1)
        dve.tensor_tensor(x, x, cos, ALU.mult).then_inc(K.dve_chain.h, 1)
        dve.wait_ge(K.dve_chain.h, K.dve_chain.n + i + 1)
        dve.tensor_tensor(cols(t), cols(t), K.head_swap[:, i % 2, 0:width], ALU.add).then_inc(K.rotated.h, 1)

    with nc.Block() as block:
        if loads:
            @block.sync
            def _(sp):
                if gains:
                    for i, g in enumerate(gains):
                        sp.dma_start(K.head_gain[:, i, :], g.partition_broadcast(P)).then_inc(K.small_loaded.h, 16)
                if rope:
                    sp.dma_start(K.rope_cos[:, :, :], rope[0]).then_inc(K.small_loaded.h, 16)
                    sp.dma_start(K.rope_sin[:, :, :], rope[1]).then_inc(K.small_loaded.h, 16)

        @block.scalar
        def _(act):
            link = Chain(act, K.act_chain)

            def rstd(i):
                act.wait_ge(K.sums_done.h, ss0 + i + 1)
                link(act.activation(K.head_ln[:, i % 2, 0:heads], K.head_ss[:, i % 2, 0:heads], ACT.Ln,
                                    bias=K.eps6[:, 0:1], scale=1.0 / dim))
                act.activation(K.head_rstd[:, i % 2, 0:heads], K.head_ln[:, i % 2, 0:heads], ACT.Exp, scale=-0.5)\
                   .then_inc(K.rstd_done.h, 1)

            for i, t in enumerate(tiles):
                if i >= 2:
                    act.wait_ge(K.sums_done.h, ss0 + i - 1)
                act.activation(K.head_sq[:, i % 2, 0:width], cols(t), ACT.Square).then_inc(K.sq_done.h, 1)
                if i:
                    rstd(i - 1)
            rstd(len(tiles) - 1)
            K.act_chain.n += link.k

        @block.vector
        def _(dve):
            def sums(i):
                dve.wait_ge(K.sq_done.h, sq0 + i + 1)
                if i >= 2:
                    dve.wait_ge(K.rstd_done.h, rs0 + i - 1)
                dve.tensor_reduce(K.head_ss[:, i % 2, 0:heads], by_head(K.head_sq[:, i % 2, 0:width]), AX.X, ALU.add)\
                   .then_inc(K.sums_done.h, 1)

            sums(0)
            for i, t in enumerate(tiles):
                if i + 1 < len(tiles):
                    sums(i + 1)
                dve.wait_ge(K.rstd_done.h, rs0 + i + 1)
                x = by_head(cols(t))
                dve.tensor_tensor(x, x, K.head_rstd[:, i % 2, 0:heads].unsqueeze(2).to_broadcast([P, heads, dim]), ALU.mult)\
                   .then_inc(K.normed.h, 1)
                if rope and t < LAT_TILES:
                    rotate(dve, i, t)

        if gains:
            @block.gpsimd
            def _(pool):
                link = Chain(pool, K.pool_chain)
                pool.wait_ge(K.small_loaded.h, sm0 + 16 * loads)
                for i, t in enumerate(tiles):
                    pool.wait_ge(K.normed.h, nm0 + i + 1)
                    x = cols(t).rearrange("p (a h d) -> p a h d", a=2, d=dim)
                    gain = K.head_gain[:, :, :].unsqueeze(2).to_broadcast([P, 2, heads // 2, dim])
                    link(pool.tensor_tensor(x, x, gain, ALU.mult))
                    if rope and t < LAT_TILES:
                        if i >= 2:
                            pool.wait_ge(K.rotated.h, K.rotated.n + i - 1)
                        swap_products(K, pool, by_head(cols(t)), by_head(K.head_swap[:, i % 2, 0:width]), t, heads, "pairs")
                K.pool_chain.n += link.k
    n = len(tiles)
    for s in (K.sq_done, K.sums_done, K.rstd_done, K.normed):
        s.n += n
    if rope:
        for s in (K.swapped, K.rotated, K.dve_chain):
            s.n += LAT_TILES
    K.small_loaded.n += 16 * loads


def swap_products(K, pool, x, out, t, heads, kind):
    if kind == "pairs":
        a = lambda ap: (ap[:, :, 0::2], ap[:, :, 1::2])
        sin = K.rope_sin[:, t, :]
        s = [sin[:, i::2].unsqueeze(1).to_broadcast([P, heads, HEAD_DIM // 2]) for i in range(2)]
    else:
        q = HEAD_DIM // 4
        halves = lambda ap: ap.rearrange("p h (a b d) -> p h a b d", a=2, b=2)
        a = lambda ap: (halves(ap)[:, :, :, 0, :], halves(ap)[:, :, :, 1, :])
        sin = K.rope_sin[:, t, :].rearrange("p (a b d) -> p a b d", a=2, b=2)
        s = [sin[:, :, i, :].unsqueeze(1).to_broadcast([P, heads, 2, q]) for i in range(2)]
    (x0, x1), (o0, o1) = a(x), a(out)
    pool.tensor_tensor(o0, x1, s[0], ALU.mult)
    pool.tensor_tensor(o1, x0, s[1], ALU.mult).then_inc(K.swapped.h, 1)


def heads_gemm_stage(K, stream, nxt, parts, gains, rope=None):
    nc = K.nc
    st = Stage(K, stream, nxt)
    heads = SLAB_N // HEAD_DIM
    loads = 2 + (2 if rope else 0)
    by_head = lambda ap: ap.rearrange("p (h d) -> p h d", d=HEAD_DIM)
    sm0 = K.small_loaded.n

    class Part:

        def __init__(self, n0, n1, tiles, gain):
            self.n0, self.n1, self.tiles, self.gain, self.nt = n0, n1, tiles, gain, len(tiles)
            self.rotated = [t for t in tiles if rope and gain is not None and t < LAT_TILES]
            self.mm, self.ev = K.mm_done.n, K.evacuated.n
            self.sq, self.ss, self.rs, self.nm = K.sq_done.n, K.sums_done.n, K.rstd_done.n, K.normed.n
            self.sw, self.ro, self.dc, self.pc, self.ac = K.swapped.n, K.rotated.n, K.dve_chain.n, K.pool_chain.n, K.act_chain.n
            slabs = n1 - n0
            K.mm_done.n += (self.nt - 1) * slabs
            K.evacuated.n += self.nt * slabs
            if gain is not None:
                for s in (K.sq_done, K.sums_done, K.rstd_done, K.normed, K.pool_chain, K.act_chain):
                    s.n += self.nt * slabs
                for s in (K.swapped, K.rotated, K.dve_chain):
                    s.n += len(self.rotated) * slabs

    parts = [Part(*p) for p in parts]
    assert parts[-1].n1 == stream.count and not st.last

    with nc.Block() as block:
        @block.sync
        def _(sp):
            for i, g in enumerate(gains):
                sp.dma_start(K.head_gain[:, i, :], g.partition_broadcast(P)).then_inc(K.small_loaded.h, 16)
            if rope:
                sp.dma_start(K.rope_cos[:, :, :], rope[0]).then_inc(K.small_loaded.h, 16)
                sp.dma_start(K.rope_sin[:, :, :], rope[1]).then_inc(K.small_loaded.h, 16)
            stream_loads(K, sp, st)

        @block.tensor
        def _(pe):
            for p in parts:
                pe.wait_ge(K.evacuated.h, p.ev)
                with pe.Fori(p.n0, p.n1) as n:
                    for h in range(2):
                        pe.wait_ge(K.lo_done.h, 2 * (st.g0 + n) + h + 1)
                        for j, t in enumerate(p.tiles):
                            if h == 0:
                                pe.wait_ge(K.evacuated.h, (n - p.n0) * p.nt + (p.ev - p.nt + j + 1))
                            for k in range(SLAB_K):
                                kk = h * SLAB_K + k
                                mm = product(pe, K.bank[j][:, :], K.hT_hi[:, kk, t * P:(t + 1) * P], K.hT_lo[:, kk, t * P:(t + 1) * P],
                                             K.w_hi[h][:, k, :], K.w_lo[h][:, k, :], kk == 0, kk == KD - 1)
                            if h == 1 and j < p.nt - 1:
                                mm.then_inc(K.mm_done.h, 1)
                        mm.then_inc(K.w_used.h, 1)

        @block.scalar
        def _(act):
            def rstd(p, n, j):
                i = (n - p.n0) * p.nt + j
                act.wait_ge(K.sums_done.h, i + (p.ss + 1))
                act.activation(K.head_ln[:, j % 2, 0:heads], K.head_ss[:, j % 2, 0:heads], ACT.Ln, bias=K.eps6[:, 0:1],
                               scale=1.0 / HEAD_DIM).then_inc(K.act_chain.h, 1)
                act.wait_ge(K.act_chain.h, i + (p.ac + 1))
                act.activation(K.head_rstd[:, j % 2, 0:heads], K.head_ln[:, j % 2, 0:heads], ACT.Exp, scale=-0.5)\
                   .then_inc(K.rstd_done.h, 1)

            for p in parts:
                with act.Fori(p.n0, p.n1) as n:
                    split_hi(K, act, st.g0 + n + 1, 0)
                    for j, t in enumerate(p.tiles):
                        if j < p.nt - 1:
                            act.wait_ge(K.mm_done.h, (n - p.n0) * (p.nt - 1) + (p.mm + j + 1))
                        else:
                            act.wait_ge(K.w_used.h, 2 * (st.g0 + n) + 2)
                        if p.gain is not None:
                            act.wait_ge(K.sums_done.h, (n - p.n0) * p.nt + (p.ss + j - 1))
                            act.activation(K.slab_sq[:, j % 2, :], K.bank[j][:, :], ACT.Square).then_inc(K.sq_done.h, 1)
                        act.activation(K.qkv[:, t, ds(n * SLAB_N, SLAB_N)], K.bank[j][:, :], ACT.Copy).then_inc(K.evacuated.h, 1)
                        if p.gain is not None and j:
                            rstd(p, n, j - 1)
                    if p.gain is not None:
                        rstd(p, n, p.nt - 1)
                    split_hi(K, act, st.g0 + n + 1, 1)

        @block.vector
        def _(dve):
            def sums(p, n, j):
                i = (n - p.n0) * p.nt + j
                dve.wait_ge(K.sq_done.h, i + (p.sq + 1))
                dve.wait_ge(K.rstd_done.h, i + (p.rs - 1))
                dve.tensor_reduce(K.head_ss[:, j % 2, 0:heads], by_head(K.slab_sq[:, j % 2, :]), AX.X, ALU.add)\
                   .then_inc(K.sums_done.h, 1)

            def normalise(p, n, j):
                i = (n - p.n0) * p.nt + j
                dve.wait_ge(K.rstd_done.h, i + (p.rs + 1))
                dve.wait_ge(K.evacuated.h, i + (p.ev + 1))
                x = by_head(K.qkv[:, p.tiles[j], ds(n * SLAB_N, SLAB_N)])
                dve.tensor_tensor(x, x, K.head_rstd[:, j % 2, 0:heads].unsqueeze(2).to_broadcast([P, heads, HEAD_DIM]), ALU.mult)\
                   .then_inc(K.normed.h, 1)

            def rotate(p, n, j):
                t = p.tiles[j]
                i = (n - p.n0) * len(p.rotated) + j
                x = K.qkv[:, t, ds(n * SLAB_N, SLAB_N)]
                dve.wait_ge(K.swapped.h, i + (p.sw + 1))
                dve.tensor_tensor(by_head(x), by_head(x), K.rope_cos[:, t, :].unsqueeze(1).to_broadcast([P, heads, HEAD_DIM]), ALU.mult)\
                   .then_inc(K.dve_chain.h, 1)
                dve.wait_ge(K.dve_chain.h, i + (p.dc + 1))
                dve.tensor_tensor(x, x, K.slab_swap[:, j % 2, :], ALU.add).then_inc(K.rotated.h, 1)

            dve.wait_ge(K.small_loaded.h, sm0 + 16 * loads)
            for p in parts:
                with dve.Fori(p.n0, p.n1) as n:
                    split_lo(K, dve, st.g0 + n + 1, 0)
                    if p.gain is not None:
                        sums(p, n, 0)
                        for j in range(p.nt):
                            if j + 1 < p.nt:
                                sums(p, n, j + 1)
                            normalise(p, n, j)
                            if 0 < j <= len(p.rotated):
                                rotate(p, n, j - 1)
                        if len(p.rotated) == p.nt:
                            rotate(p, n, p.nt - 1)
                    split_lo(K, dve, st.g0 + n + 1, 1)

        @block.gpsimd
        def _(pool):
            pool.wait_ge(K.small_loaded.h, sm0 + 16 * loads)
            for p in parts:
                if p.gain is None:
                    continue
                with pool.Fori(p.n0, p.n1) as n:
                    for j, t in enumerate(p.tiles):
                        i = (n - p.n0) * p.nt + j
                        pool.wait_ge(K.normed.h, i + (p.nm + 1))
                        x = by_head(K.qkv[:, t, ds(n * SLAB_N, SLAB_N)])
                        pool.sem_inc(K.pool_go.h, 1)
                        pool.tensor_tensor(x, x, K.head_gain[:, p.gain, :].unsqueeze(1).to_broadcast([P, heads, HEAD_DIM]), ALU.mult)\
                            .then_inc(K.pool_chain.h, 1)
                        if t in p.rotated:
                            pool.wait_ge(K.pool_chain.h, i + (p.pc + 1))
                            pool.wait_ge(K.rotated.h, (n - p.n0) * len(p.rotated) + (p.ro + j - 1))
                            pool.sem_inc(K.pool_go.h, 1)
                            swap_products(K, pool, x, by_head(K.slab_swap[:, j % 2, :]), t, heads, "pairs")
    K.small_loaded.n += 16 * loads


def rope_stage(K, heads, rope):
    nc = K.nc
    width = heads * HEAD_DIM
    sm0, t20, ro0 = K.small_loaded.n, K.swapped.n, K.rotated.n
    by_head = lambda ap: ap.rearrange("p (h d) -> p h d", d=HEAD_DIM)
    with nc.Block() as block:
        @block.sync
        def _(sp):
            sp.dma_start(K.rope_cos[:, :, :], rope[0]).then_inc(K.small_loaded.h, 16)
            sp.dma_start(K.rope_sin[:, :, :], rope[1]).then_inc(K.small_loaded.h, 16)

        @block.gpsimd
        def _(pool):
            pool.memset(K.roped[:, :, width:width + HEAD_DIM], 0.0)
            pool.memset(K.sink_b[:, 16:18], 0.0)
            pool.wait_ge(K.small_loaded.h, sm0 + 32)
            for t in range(LAT_TILES):
                if t >= 2:
                    pool.wait_ge(K.rotated.h, ro0 + t - 1)
                swap_products(K, pool, by_head(K.qkv2[:, t, 0:width]), by_head(K.head_swap[:, t % 2, 0:width]), t, heads, "halves")

        @block.vector
        def _(dve):
            link = Chain(dve, K.dve_chain)
            dve.wait_ge(K.small_loaded.h, sm0 + 32)
            for t in range(LAT_TILES):
                cos = K.rope_cos[:, t, :].unsqueeze(1).to_broadcast([P, heads, HEAD_DIM])
                link(dve.tensor_tensor(by_head(K.roped[:, t, 0:width]), by_head(K.qkv2[:, t, 0:width]), cos, ALU.mult))
                dve.wait_ge(K.swapped.h, t20 + t + 1)
                dve.tensor_tensor(K.roped[:, t, 0:width], K.roped[:, t, 0:width], K.head_swap[:, t % 2, 0:width], ALU.add)\
                   .then_inc(K.rotated.h, 1)
            K.dve_chain.n += link.k
    K.small_loaded.n += 32
    K.swapped.n += LAT_TILES
    K.rotated.n += LAT_TILES


class Unit:

    def __init__(self, tile, keys, masks=None, unrotated=0):
        self.tile, self.keys, self.masks, self.unrotated = tile, keys, masks or {}, unrotated
        self.width = len(keys) * P

    def segments(self):
        runs = []
        for i, kt in enumerate(self.keys):
            if runs and i % 4 and self.keys[i - 1] == kt - 1 and i not in self.masks and i - 1 not in self.masks \
                    and i != self.unrotated:
                runs[-1][1] += 1
            else:
                runs.append([i, 1])
        return runs


def attention_stage(K, units, steps, stage_heads, values, out, mods, mods_at, diff=False, rel_bias=False, sink=None,
                    unrotated=False, q_tiles=TOK_TILES):
    nc = K.nc
    pairs = 2
    nu = len(units)
    X = pairs * nu * 2
    U = pairs * nu
    T = U if diff else X
    n_src = 3 if unrotated else 2
    S0 = pairs * n_src
    src_at = nu // 2
    base = {s: s.n for s in (K.staged, K.src_turned, K.src_read, K.s_done, K.nm_done, K.p_done, K.w_done, K.pt_done,
                             K.pt_read[0], K.pt_read[1], K.o_done, K.o_read, K.g_done, K.g_ready, K.mod_used)}
    slabs = [(m, j) for m in mods for j in range(m.per)]
    M = len(slabs)
    assert M == sum(mods_at) and M % 2 == 0 and nu % 2 == 0
    ml0 = [s.n for s in K.mod_loaded]
    at = lambda s, i, per, k: base[s] + i * per + k + 1
    S = [K.psum[:, 0:2, :].rearrange("p a b -> p (a b)"), K.psum[:, 2:4, :].rearrange("p a b -> p (a b)")]
    PT = [K.psum[:, 4:6, :].rearrange("p a b -> p (a b)"), K.psum[:, 6:8, :].rearrange("p a b -> p (a b)")]
    TOK = N_TOK
    row_psum, col_psum = K.bank[1][0:2, 256:512], K.bank[3][:, 256:260]
    assert mods_at[0] == 0 and max(mods_at) <= 2
    ms = (0,) if diff else (0, 1)

    def unit(v):
        return units[v % nu], v // nu, v % nu

    def turned_at(v, m):
        return v if diff else 2 * v + m

    def o_bank(x):
        return PT[x % 2][:, TOK:TOK + P]

    with nc.Block() as block:
        @block.sync
        def _(sp):
            with sp.Fori(0, steps) as i:
                for pi in range(pairs):
                    for k, (m, j) in enumerate(slabs):
                        sp.wait_ge(K.mod_used.h, at(K.mod_used, i, pairs * M, pi * M + k - 2))
                        sp.dma_start(K.mod_slab[k % 2][:, :, :], m.w[:, :, ds(i * (pairs * m.per * P) + (pi * m.per + m.first + j) * P, P)])\
                          .then_inc(K.mod_loaded[k % 2].h, 16)

        @block.gpsimd
        def _(pool):
            stage_heads(pool, 0, 0)
            with pool.Fori(0, steps) as i:
                for pi in range(pairs):
                    pool.wait_ge(K.src_turned.h, at(K.src_turned, i, S0, (pi + 1) * n_src - 1))
                    stage_heads(pool, i, pi + 1)

        @block.tensor
        def _(pe):
            def modulate(i, v):
                _, pi, u = unit(v)
                k0 = sum(mods_at[:u])
                for j in range(mods_at[u]):
                    k = k0 + j
                    pe.wait_ge(K.mod_loaded[k % 2].h, i * (pairs * 16 * M // 2) + (ml0[k % 2] + 16 * (pi * M // 2 + k // 2 + 1)))
                    mod_rows(K, pe, row_psum[:, j * P:(j + 1) * P], slabs[k][0].layer, K.mod_slab[k % 2]).then_inc(K.mod_used.h, 1)

            def turn_sources(i, pi):
                pe.wait_ge(K.staged.h, at(K.staged, i, pairs, pi))
                for q in range(n_src):
                    if q == 2:
                        pe.wait_ge(K.src_read.h, at(K.src_read, i, S0, pi * n_src))
                    for t in range(TOK_TILES if q == 1 else q_tiles):
                        mm = pe.transpose(PT[q % 2][:, t * P:(t + 1) * P], K.heads[q][:, t, :], K.ident[:, :])
                    mm.then_inc(K.src_turned.h, 1)

            def bias_tiles(i, step):
                pe.wait_ge(K.p_done.h, at(K.p_done, i, X, step * X - 1))
                flat = K.psum[:, 0:4, :].rearrange("p a b -> p (a b)")
                for kc in range(GRID_W):
                    half, c = kc // 32, kc % 32
                    if half and c % 8 == 0:
                        pe.wait_ge(K.g_ready.h, at(K.g_ready, i, 8, 8 * step + c // 8))
                    mm = pe.matmul(flat[:, c * 64:c * 64 + 64], K.shift_r[:, GRID_W - 1 - kc:3 * GRID_W - 1 - kc],
                                   K.rpbT[:, ds(i * (2 * pairs) + 2 * pairs * step, 2 * pairs), :], start=True, stop=True)
                    if c % 8 == 7:
                        mm.then_inc(K.g_done.h, 1)

            def scores(i, v, m, first=False):
                un, pi, u = unit(v)
                if u == 0 and m == 0:
                    pe.wait_ge(K.src_read.h, at(K.src_read, i, S0, pi * n_src + n_src - 1))
                    if rel_bias:
                        pe.wait_ge(K.g_ready.h, at(K.g_ready, i, 8, 8 * (pi // pairs) + 7))
                pe.wait_ge(K.p_done.h, at(K.p_done, i, X, 2 * v + m - 2))
                if m == 0:
                    modulate(i, v)
                elif not first:
                    for j in range(mods_at[u - 1]):
                        mod_turn(K, pe, col_psum[:, 2 * j:2 * j + 2], K.mod_row[:, (u - 1) % 2, j * P:(j + 1) * P])
                rows = slice(m * HEAD_DIM, (m + 1) * HEAD_DIM)
                qcols = slice(un.tile * P, (un.tile + 1) * P)
                heads = K.headsT[pi % 2]
                for j, n in un.segments():
                    q = heads[2] if unrotated and j < un.unrotated else heads[0]
                    o = S[m][:, j * P:(j + n) * P]
                    kt = un.keys[j]
                    masked = j in un.masks or (rel_bias and j == 0)
                    mm = pe.matmul(o, q[rows, qcols], heads[1][rows, kt * P:(kt + n) * P], start=True, stop=not masked)
                    if j in un.masks:
                        mm = pe.matmul(o, K.ident[:, :], un.masks[j], start=False, stop=True)
                    elif masked:
                        first_row = N_ROWS - 1 - 2 * un.tile
                        g = K.G[pi % 2][:, :, m, first_row:first_row + N_ROWS].rearrange("p c r -> p r c")
                        mm = pe.matmul(o, K.ident[:, :], g, start=False, stop=True)
                mm.then_inc(K.s_done.h, 1)

            def turn(i, v, m):
                un, pi, u = unit(v)
                x = turned_at(v, m)
                src = K.w_mat if diff else K.p_mat[m]
                if diff:
                    pe.wait_ge(K.w_done.h, at(K.w_done, i, U, v))
                else:
                    pe.wait_ge(K.p_done.h, at(K.p_done, i, X, x))
                pe.wait_ge(K.o_read.h, at(K.o_read, i, U, v - (2 if diff else 1)))
                if u == src_at:
                    pe.wait_ge(K.src_read.h, at(K.src_read, i, S0, (pi + 1) * n_src + n_src - 1))
                for j in range(len(un.keys)):
                    mm = pe.transpose(PT[x % 2][:, j * P:(j + 1) * P], src[:, j * P:(j + 1) * P], K.ident[:, :])
                mm.then_inc(K.pt_done.h, 1)

            def weighted(i, v, m):
                un, pi, u = unit(v)
                x = turned_at(v, m)
                pe.wait_ge(K.pt_read[m].h, at(K.pt_read[m], i, U, v))
                o = o_bank(x)[:, 0:P if diff else HEAD_DIM]
                for j, kt in enumerate(un.keys):
                    mm = pe.matmul(o, K.pT_mat[x % 2][:, j * P:(j + 1) * P], values(i, pi, m, kt), start=j == 0,
                                   stop=j == len(un.keys) - 1)
                if diff or m == 1:
                    mm.then_inc(K.o_done.h, 1)

            turn_sources(0, 0)
            if rel_bias:
                bias_tiles(0, 0)
            for m in range(2):
                scores(0, 0, m, first=True)
            with pe.Fori(0, steps) as i:
                for v in range(U):
                    _, pi, u = unit(v)
                    if rel_bias and v == U - 1:
                        for m in ms:
                            turn(i, v, m)
                        bias_tiles(i, 1)
                        for m in ms:
                            weighted(i, v, m)
                        for m in range(2):
                            scores(i, v + 1, m)
                        continue
                    scores(i, v + 1, 0)
                    if u == src_at:
                        pe.wait_ge(K.o_read.h, at(K.o_read, i, U, v - 1))
                        turn_sources(i, pi + 1)
                        scores(i, v + 1, 1)
                    for m in ms:
                        turn(i, v, m)
                    if u != src_at:
                        scores(i, v + 1, 1)
                    for m in ms:
                        weighted(i, v, m)

        @block.scalar
        def _(act):
            def probabilities(i, v, m):
                un, pi, u = unit(v)
                act.wait_ge(K.nm_done.h, at(K.nm_done, i, X, 2 * v + m))
                if diff:
                    act.wait_ge(K.w_done.h, at(K.w_done, i, U, v - 1))
                else:
                    act.wait_ge(K.pt_done.h, at(K.pt_done, i, T, 2 * v + m - 2))
                if sink is not None:
                    act.activation(K.sink_exp[:, v % 2, m:m + 1], K.sink_pair[:, m:m + 1], ACT.Exp,
                                   bias=K.neg_max[:, v % 2, m:m + 1])
                act.activation(K.p_mat[m][:, 0:un.width], S[m][:, 0:un.width], ACT.Exp, bias=K.neg_max[:, v % 2, m:m + 1],
                               scale=SCALE, accum_out=K.p_sum[:, v % 2, m:m + 1]).then_inc(K.p_done.h, 1)

            def read_turned(i, v):
                x = turned_at(v, 0)
                w = unit(v)[0].width
                act.wait_ge(K.pt_done.h, at(K.pt_done, i, T, x))
                act.activation(K.pT_mat[x % 2][:, 0:w], PT[x % 2][:, 0:w], ACT.Copy).then_inc(K.pt_read[0].h, 1)

            def read_sources(i, pi):
                for q in range(n_src):
                    act.wait_ge(K.src_turned.h, at(K.src_turned, i, S0, pi * n_src + q))
                    w = TOK if q == 1 else q_tiles * P
                    act.activation(K.headsT[pi % 2][q][:, 0:w], PT[q % 2][:, 0:w], ACT.Copy).then_inc(K.src_read.h, 1)

            read_sources(0, 0)
            for m in range(2):
                probabilities(0, 0, m)
            with act.Fori(0, steps) as i:
                for v in range(U):
                    _, pi, u = unit(v)
                    if u == src_at:
                        read_sources(i, pi + 1)
                        probabilities(i, v + 1, 0)
                        read_turned(i, v)
                        probabilities(i, v + 1, 1)
                    else:
                        read_turned(i, v)
                        probabilities(i, v + 1, 0)
                        probabilities(i, v + 1, 1)

        @block.vector
        def _(dve):
            per_step = pairs * (nu * ATT_LINKS[diff, sink is not None] + (sink is not None))

            def maxima(link, i, v, m, first=False):
                un, pi, u = unit(v)
                dve.wait_ge(K.s_done.h, at(K.s_done, i, X, 2 * v + m))
                if m == 0 and mods_at[u]:
                    w = mods_at[u] * P
                    dve.tensor_copy(K.mod_row[:, u % 2, 0:w], row_psum[:, 0:w])
                if m == 1 and not first:
                    before = unit(v - 1)
                    k0 = sum(mods_at[:before[2]])
                    for j in range(mods_at[before[2]]):
                        mod, n = slabs[k0 + j]
                        mod_add(K, dve, mod.layer, i * (pairs * mod.per) + (before[1] * mod.per + mod.first + n), 1,
                                col_psum[:, 2 * j:2 * j + 2])
                nm = K.neg_max[:, v % 2, m:m + 1]
                link(dve.tensor_reduce(nm, S[m][:, 0:un.width], AX.X, ALU.max))
                if sink is not None:
                    link(dve.tensor_scalar(nm, nm, SCALE, K.sink_pair[:, m:m + 1], ALU.mult, ALU.max))
                    dve.tensor_scalar(nm, nm, -1.0, None, ALU.mult).then_inc(K.nm_done.h, 1)
                else:
                    dve.tensor_scalar(nm, nm, -SCALE, None, ALU.mult).then_inc(K.nm_done.h, 1)

            def inverse_sums(link, i, v):
                dve.wait_ge(K.p_done.h, at(K.p_done, i, X, 2 * v + 1))
                r = K.p_inv[:, v % 2, :]
                if sink is not None:
                    link(dve.tensor_tensor(K.p_sum[:, v % 2, :], K.p_sum[:, v % 2, :], K.sink_exp[:, v % 2, :], ALU.add))
                link(dve.reciprocal(r, K.p_sum[:, v % 2, :]))

            def combine(link, i, v):
                un = unit(v)[0]
                inverse_sums(link, i, v)
                link(dve.tensor_scalar(K.p_inv[:, v % 2, 1:2], K.p_inv[:, v % 2, 1:2], K.neg_lam[:, 0:1], None, ALU.mult))
                dve.wait_ge(K.pt_done.h, at(K.pt_done, i, T, v - 1))
                w = K.w_mat[:, 0:un.width]
                link(dve.tensor_scalar(w, K.p_mat[0][:, 0:un.width], K.p_inv[:, v % 2, 0:1], None, ALU.mult))
                dve.scalar_tensor_tensor(w, K.p_mat[1][:, 0:un.width], K.p_inv[:, v % 2, 1:2], w, ALU.mult, ALU.add)\
                   .then_inc(K.w_done.h, 1)

            def read_turned(i, v):
                w = unit(v)[0].width
                dve.wait_ge(K.pt_done.h, at(K.pt_done, i, T, 2 * v + 1))
                dve.tensor_copy(K.pT_mat[1][:, 0:w], PT[1][:, 0:w]).then_inc(K.pt_read[1].h, 1)

            def finish(i, v):
                un, pi, u = unit(v)
                dve.wait_ge(K.o_done.h, at(K.o_done, i, U, v))
                o = out(i, pi, un.tile)
                if diff:
                    dve.tensor_copy(o, o_bank(v)).then_inc(K.o_read.h, 1)
                else:
                    for m in range(2):
                        ins = dve.tensor_scalar(o[:, m * HEAD_DIM:(m + 1) * HEAD_DIM], o_bank(m)[:, 0:HEAD_DIM],
                                                K.p_inv[:, v % 2, m:m + 1], None, ALU.mult)
                    ins.then_inc(K.o_read.h, 1)

            def read_bias_tiles(i, step):
                flat = K.psum[:, 0:4, :].rearrange("p a b -> p (a b)")
                for q in range(8):
                    dve.wait_ge(K.g_done.h, at(K.g_done, i, 8, 8 * step + q))
                    bank = flat[:, (q % 4) * 512:(q % 4 + 1) * 512].rearrange("p (c x) -> p c x", x=64)
                    mask = K.col_mask[:, 8 * q:8 * q + 8].unsqueeze(2).to_broadcast([P, 8, 32])
                    for pi in range(pairs):
                        g = K.G[pi][:, :, :, :].rearrange("p c h r -> p c (h r)")[:, 8 * q:8 * q + 8, :]
                        ins = dve.scalar_tensor_tensor(g, bank[:, :, 32 * pi:32 * pi + 32], 1.0 / SCALE, mask, ALU.mult, ALU.add)
                    ins.then_inc(K.g_ready.h, 1)

            def load_sinks(link, i, pi):
                link(dve.tensor_copy(K.sink_pair[:, :], K.sink_b[:, ds(2 * (pairs * i + pi), 2)]))

            link = Chain(dve, K.dve_chain)
            if rel_bias:
                read_bias_tiles(0, 0)
            if sink is not None:
                load_sinks(link, 0, 0)
            for m in range(2):
                maxima(link, 0, 0, m, first=True)
            before = link.k
            with dve.Fori(0, steps) as i:
                link = Chain(dve, K.dve_chain, before + i * per_step)
                for v in range(U):
                    _, pi, u = unit(v)
                    if diff:
                        combine(link, i, v)
                    else:
                        inverse_sums(link, i, v)
                    if sink is not None and u == nu - 1:
                        load_sinks(link, i, pi + 1)
                    if rel_bias and v == U - 1:
                        read_turned(i, v)
                        read_bias_tiles(i, 1)
                        finish(i, v)
                        for m in range(2):
                            maxima(link, i, v + 1, m)
                        continue
                    maxima(link, i, v + 1, 0)
                    if not diff and u != src_at:
                        read_turned(i, v)
                    maxima(link, i, v + 1, 1)
                    if not diff and u == src_at:
                        read_turned(i, v)
                    finish(i, v)
                assert link.k == per_step, (link.k, per_step)
            K.dve_chain.n += before + steps * per_step
    for s, per, more in ((K.staged, pairs, 1), (K.src_turned, S0, n_src), (K.src_read, S0, n_src), (K.s_done, X, 2), (K.nm_done, X, 2),
                         (K.p_done, X, 2), (K.pt_done, T, 0), (K.pt_read[0], U, 0), (K.o_done, U, 0), (K.o_read, U, 0),
                         (K.mod_used, pairs * M, 0)):
        s.n += per * steps + more
    for s in K.mod_loaded[0:2]:
        s.n += 16 * (M // 2) * pairs * steps
    if not diff:
        K.pt_read[1].n += U * steps
    if diff:
        K.w_done.n += U * steps
    if rel_bias:
        K.g_done.n += 8 * steps + 8
        K.g_ready.n += 8 * steps + 8


ATT_LINKS = {(True, False): 5, (False, False): 3, (False, True): 6}


def layer_norm_stage(K, gain, bias, tiles, store=None):
    nc = K.nc
    n = len(tiles)
    sm0, st0, rs0, ga0 = K.small_loaded.n, K.sums_done.n, K.rstd_done.n, K.gained.n
    with nc.Block() as block:
        @block.sync
        def _(sp):
            sp.dma_start(K.ln_gain[:, :], gain.partition_broadcast(P)).then_inc(K.small_loaded.h, 16)
            sp.dma_start(K.ln_bias[:, :], bias.partition_broadcast(P)).then_inc(K.small_loaded.h, 16)
            if store is not None:
                for i, t in enumerate(tiles):
                    sp.wait_ge(K.gained.h, ga0 + i + 1)
                    sp.dma_start(store[t * P:(t + 1) * P, :], K.x[:, t, :]).then_inc(K.stored.h, 16)
                sp.wait_ge(K.stored.h, K.stored.n + 16 * n)

        @block.vector
        def _(dve):
            link = Chain(dve, K.dve_chain)
            for i, t in enumerate(tiles):
                for h in range(2):
                    ins = dve.bn_stats(K.ln_stats[:, t, h, :], K.x[:, t, h * 512:(h + 1) * 512])
                    link(ins)
                dve.bn_aggr(K.ln_mv[:, t, :], K.ln_stats[:, t, :, :]).then_inc(K.sums_done.h, 1)
            dve.wait_ge(K.small_loaded.h, sm0 + 32)
            for i, t in enumerate(tiles):
                link(dve.scalar_tensor_tensor(K.x[:, t, :], K.x[:, t, :], K.ln_mv[:, t, 0:1], K.ln_gain[:, :],
                                              ALU.subtract, ALU.mult))
                if i == 0:
                    dve.wait_ge(K.rstd_done.h, rs0 + 1)
                dve.scalar_tensor_tensor(K.x[:, t, :], K.x[:, t, :], K.rstd[:, t:t + 1], K.ln_bias[:, :], ALU.mult, ALU.add)\
                   .then_inc(K.gained.h, 1)
            K.dve_chain.n += link.k

        @block.scalar
        def _(act):
            act.wait_ge(K.sums_done.h, st0 + n)
            link = Chain(act, K.act_chain)
            link(act.activation(K.lnms[:, 0:n], K.ln_mv[:, 0:n, 1], ACT.Ln, bias=K.eps_ln[:, 0:1]))
            act.activation(K.rstd[:, 0:n], K.lnms[:, 0:n], ACT.Exp, scale=-0.5).then_inc(K.rstd_done.h, 1)
            K.act_chain.n += link.k
    K.small_loaded.n += 32
    for s in (K.sums_done, K.gained):
        s.n += n
    K.rstd_done.n += 1
    if store is not None:
        K.stored.n += 16 * n


TAPS = 5
SSM_INNER = 2 * D
SSM_STATE = 128
SSM_GROUPS = 4
GROUP_HEADS = 8
SSM_HEADS = SSM_GROUPS * GROUP_HEADS
GROUP_W = GROUP_HEADS * HEAD_DIM
PAD = TAPS // 2
LAT_AT, CTX_AT = 0, N_LAT + 2 * PAD
ROW = N_TOK + 4 * PAD
OUT = ROW - 2 * PAD


TURN_AFTER = ((), (), (), (0,), (1, 2), (3, 4, 5))


def dt_stage(K, w_dt, dt_bias, a_log, conv_w, conv_b, norm_g):
    nc = K.nc
    sm0, mm0, dv0, ac0, tr0, re0 = (s.n for s in (K.small_loaded, K.mm_done, K.dve_chain, K.act_chain, K.turned, K.relu_done))
    H2 = 2 * SSM_HEADS
    with nc.Block() as block:
        @block.sync
        def _(sp):
            for out, src in ((K.dt_w[:, :, :], w_dt.rearrange("(k p) n -> p k n", p=P)),
                             (K.dt_bias[:, :], dt_bias.partition_broadcast(P)),
                             (K.a_neg[:, :], a_log.partition_broadcast(P)),
                             (K.conv_rows[0:TAPS * 24, :], conv_w.rearrange("j (b p) -> (j b) p", p=P)),
                             (K.vec_rows[0:24, :], conv_b.rearrange("(b p) -> b p", p=P)),
                             (K.vec_rows[32:48, :], norm_g.rearrange("(b p) -> b p", p=P))):
                sp.dma_start(out, src).then_inc(K.small_loaded.h, 16)

        @block.vector
        def _(dve):
            link = Chain(dve, K.dve_chain)
            dve.wait_ge(K.small_loaded.h, sm0 + 96)
            link(dve.tensor_copy(K.dt_w_hi[:, :, :], K.dt_w[:, :, :]))
            link(dve.tensor_tensor(K.dt_w_lo[:, :, :], K.dt_w[:, :, :], K.dt_w_hi[:, :, :].bitcast(F32), ALU.subtract))
            dve.wait_ge(K.mm_done.h, mm0 + 2)
            v, e = K.dt[:, :, :], K.a[:, :, :]
            link(dve.tensor_tensor(v, K.bank[3][:, 0:TOK_TILES * H2].rearrange("p (t h) -> p t h", h=H2),
                                   K.dt_bias[:, :].unsqueeze(1).to_broadcast([P, TOK_TILES, H2]), ALU.add))
            link(dve.scalar_tensor_tensor(e, v, -1.0, v, ALU.mult, ALU.max))
            dve.wait_ge(K.act_chain.h, ac0 + 3)
            link(dve.scalar_tensor_tensor(v.rearrange("p t h -> p (t h)"), v.rearrange("p t h -> p (t h)"), 0.0,
                                          e.rearrange("p t h -> p (t h)"), ALU.max, ALU.add))
            dve.wait_ge(K.a_neg_done.h, K.a_neg_done.n + 1)
            link(dve.tensor_tensor(e, v, K.a_neg[:, :].unsqueeze(1).to_broadcast([P, TOK_TILES, H2]), ALU.mult))
            dve.wait_ge(K.turned.h, tr0 + 1)
            dve.tensor_copy(K.conv_cols[:, :], K.bank[4][:, 0:TAPS * 24])
            dve.tensor_copy(K.vec_cols[:, :], K.bank[5][:, 0:48])
            K.dve_chain.n += link.k

        @block.scalar
        def _(act):
            act.wait_ge(K.small_loaded.h, sm0 + 96)
            link = Chain(act, K.act_chain)
            link(act.activation(K.a_neg[:, :], K.a_neg[:, :], ACT.Exp))
            act.wait_ge(K.mm_done.h, mm0 + 1)
            act.activation(K.dtT[:, 0:N_LAT], K.bank[0][0:H2, :], ACT.Copy)
            act.activation(K.dtT[:, N_LAT:N_TOK], K.bank[1][0:H2, 0:N_CTX], ACT.Copy).then_inc(K.relu_done.h, 1)
            act.wait_ge(K.dve_chain.h, dv0 + 4)
            e = K.a[:, :, :]
            link(act.activation(e, e, ACT.Exp, scale=-1.0))
            link(act.activation(e, e, ACT.Ln, bias=K.one[:, 0:1]))
            K.act_chain.n += link.k

        @block.gpsimd
        def _(pool):
            pool.wait_ge(K.act_chain.h, ac0 + 1)
            pool.tensor_scalar(K.a_neg[:, :], K.a_neg[:, :], -1.0, None, ALU.mult).then_inc(K.a_neg_done.h, 1)

        @block.tensor
        def _(pe):
            pe.wait_ge(K.dve_chain.h, dv0 + 2)
            for b, t0, t1 in ((0, 0, N_LAT), (1, N_LAT, N_TOK)):
                for k in range(KD):
                    mm = product(pe, K.bank[b][0:H2, 0:t1 - t0], K.dt_w_hi[:, k, :], K.dt_w_lo[:, k, :], K.hT_hi[:, k, t0:t1],
                                 K.hT_lo[:, k, t0:t1], k == 0, k == KD - 1)
            mm.then_inc(K.mm_done.h, 1)
            pe.wait_ge(K.relu_done.h, re0 + 1)
            for t in range(TOK_TILES):
                mm = pe.transpose(K.bank[3][:, t * H2:(t + 1) * H2], K.dtT[:, t * P:(t + 1) * P], K.ident[0:H2, 0:H2])
            mm.then_inc(K.mm_done.h, 1)
            pe.wait_ge(K.small_loaded.h, sm0 + 96)
            pe.transpose(K.bank[4][:, 0:TAPS * 24], K.conv_rows[0:TAPS * 24, :], K.ident[0:TAPS * 24, 0:TAPS * 24])
            pe.transpose(K.bank[5][:, 0:48], K.vec_rows[0:48, :], K.ident[0:48, 0:48]).then_inc(K.turned.h, 1)
    K.small_loaded.n += 96
    K.relu_done.n += 1
    K.mm_done.n += 2
    K.turned.n += 1


def conv_stage(K, stream, nxt):
    nc = K.nc
    st = Stage(K, stream, nxt)
    nt = TOK_TILES
    ns, nb = stream.count, SSM_INNER // SLAB_N
    mm0, re0, tr0, xr0, cv0, si0, bt0, br0 = (s.n for s in (
        K.mm_done, K.relu_done, K.turned, K.xt_read, K.conv_done, K.silu_done, K.back_done, K.back_read))
    FB = SLAB_N // P

    def tile_done(eng, n, j):
        if j < nt - 1:
            eng.wait_ge(K.mm_done.h, mm0 + (nt - 1) * n + j + 1)
        else:
            eng.wait_ge(K.w_used.h, 2 * (st.g0 + n) + 2)

    with nc.Block() as block:
        @block.sync
        def _(sp):
            stream_loads(K, sp, st)

        @block.scalar
        def _(act):
            def silu(n, back):
                for fb in range(FB):
                    act.wait_ge(K.conv_done.h, cv0 + FB * n + fb + 1)
                    c = K.conv_out[fb // 2][:, fb % 2, :]
                    if back:
                        act.activation(c, c, ACT.Silu).then_inc(K.silu_done.h, 1)
                    else:
                        act.activation(K.BC[:, ds(n * FB + (fb - nb * FB), 1), 0:N_LAT], c[:, 0:N_LAT].unsqueeze(1), ACT.Silu)
                        act.activation(K.BC[:, ds(n * FB + (fb - nb * FB), 1), N_LAT:N_TOK], c[:, CTX_AT:CTX_AT + N_CTX].unsqueeze(1), ACT.Silu)\
                           .then_inc(K.silu_done.h, 1)

            def back_out(n):
                for t in range(nt):
                    act.wait_ge(K.back_done.h, bt0 + nt * n + t + 1)
                    act.activation(K.x_tok[:, t, ds(n * SLAB_N, SLAB_N)], K.bank[6 + t % 2][:, :], ACT.Copy)\
                       .then_inc(K.back_read.h, 1)

            def body(n, back):
                split_hi(K, act, st.g0 + n + 1, 0)
                for j in range(nt):
                    tile_done(act, n, j)
                    act.wait_ge(K.turned.h, tr0 + nt * n + j - 1)
                    act.activation(K.relu[:, j % 2, :], K.bank[j][:, :], ACT.Copy).then_inc(K.relu_done.h, 1)
                split_hi(K, act, st.g0 + n + 1, 1)
                silu(n, back)
                if back:
                    back_out(n)
            with act.Fori(0, nb) as n:
                body(n, True)
            with act.Fori(nb, ns) as n:
                body(n, False)

        @block.vector
        def _(dve):
            def body(n, back):
                split_lo(K, dve, st.g0 + n + 1, 0)
                for j in range(nt):
                    dve.wait_ge(K.turned.h, tr0 + nt * n + j + 1)
                    at = PAD + j * P if j < LAT_TILES else CTX_AT + PAD + (j - LAT_TILES) * P
                    dve.tensor_copy(K.xt[:, :, at:at + P], K.bank[6 + j % 2][:, :].rearrange("p (f t) -> p f t", f=FB))\
                       .then_inc(K.xt_read.h, 1)
                dve.wait_ge(K.xt_read.h, xr0 + nt * (n + 1))
                split_lo(K, dve, st.g0 + n + 1, 1)
                for fb in range(FB):
                    c = K.conv_out[fb // 2][:, fb % 2, :]
                    dve.wait_ge(K.back_read.h, br0 + nt * (n if back else nb))
                    if not back:
                        dve.wait_ge(K.silu_done.h, si0 + FB * n)
                    for j in range(TAPS):
                        x = K.xt[:, fb, j:j + OUT]
                        tap = K.conv_cols[:, ds(n * FB + (fb + 24 * j), 1)]
                        if j == 0:
                            ins = dve.tensor_scalar(c, x, tap, K.vec_cols[:, ds(n * FB + fb, 1)], ALU.mult, ALU.add)
                        else:
                            ins = dve.scalar_tensor_tensor(c, x, tap, c, ALU.mult, ALU.add)
                        if j < TAPS - 1:
                            ins.then_inc(K.tap_done.h, 1)
                            dve.wait_ge(K.tap_done.h, K.tap_done.n + (TAPS - 1) * (FB * n + fb) + j + 1)
                    ins.then_inc(K.conv_done.h, 1)
            dve.memset(K.xt[:, :, :], 0.0).then_inc(K.dve_chain.h, 1)
            dve.wait_ge(K.dve_chain.h, K.dve_chain.n + 1)
            with dve.Fori(0, nb) as n:
                body(n, True)
            with dve.Fori(nb, ns) as n:
                body(n, False)

        @block.tensor
        def _(pe):
            def turn(n, j, back):
                pe.wait_ge(K.relu_done.h, re0 + nt * n + j + 1)
                pe.wait_ge(K.xt_read.h, xr0 + nt * n + j - 1)
                pe.wait_ge(K.back_read.h, br0 + nt * (n if back else nb))
                if j == 0:
                    pe.wait_ge(K.conv_done.h, cv0 + FB * n)
                for k in range(FB):
                    mm = pe.transpose(K.bank[6 + j % 2][:, k * P:(k + 1) * P], K.relu[:, j % 2, k * P:(k + 1) * P], K.ident[:, :])
                mm.then_inc(K.turned.h, 1)

            def turn_back(n):
                pe.wait_ge(K.silu_done.h, si0 + FB * (n + 1))
                for t in range(nt):
                    pe.wait_ge(K.back_read.h, br0 + nt * n + t - 1)
                    pe.wait_ge(K.xt_read.h, xr0 + nt * (n + 1))
                    at = LAT_AT + t * P if t < LAT_TILES else CTX_AT + (t - LAT_TILES) * P
                    for fb in range(FB):
                        mm = pe.transpose(K.bank[6 + t % 2][:, fb * P:(fb + 1) * P], K.conv_out[fb // 2][:, fb % 2, at:at + P],
                                          K.ident[:, :])
                    mm.then_inc(K.back_done.h, 1)

            def gemm_half(n, h, back=True, before=None):
                pe.wait_ge(K.lo_done.h, 2 * (st.g0 + n) + h + 1)
                for j in range(nt):
                    if h == 0:
                        pe.wait_ge(K.relu_done.h, re0 + nt * (n - 1) + j + 1)
                    for k in range(SLAB_K):
                        kk = h * SLAB_K + k
                        mm = product(pe, K.bank[j][:, :], K.hT_hi[:, kk, j * P:(j + 1) * P], K.hT_lo[:, kk, j * P:(j + 1) * P],
                                     K.w_hi[h][:, k, :], K.w_lo[h][:, k, :], kk == 0, kk == KD - 1)
                    if j == nt - 1:
                        mm.then_inc(K.w_used.h, 1)
                    elif h == 1:
                        mm.then_inc(K.mm_done.h, 1)
                    if h == 1:
                        if j == 3 and before is not None:
                            turn_back(before)
                        for i in TURN_AFTER[j]:
                            turn(n, i, back)

            gemm_half(0, 0)
            gemm_half(0, 1)
            with pe.Fori(1, nb) as n:
                gemm_half(n, 0)
                gemm_half(n, 1, before=n - 1)
            for n in range(nb, ns):
                gemm_half(n, 0, back=False)
                gemm_half(n, 1, back=False, before=n - 1 if n == nb else None)
    K.mm_done.n += (nt - 1) * ns
    for s in (K.relu_done, K.turned, K.xt_read):
        s.n += nt * ns
    for s in (K.conv_done, K.silu_done):
        s.n += FB * ns
    K.tap_done.n += (TAPS - 1) * FB * ns
    K.dve_chain.n += 1
    K.back_done.n += nt * nb
    K.back_read.n += nt * nb


def silu_store_out(K, act, count, n, t, bank, j):
    act.wait_ge(K.z_stored[j].h, K.z_stored[j].n + 16 * n)
    act.activation(K.z_buf[:, j, :], bank[:, :], ACT.Silu).then_inc(K.evacuated.h, 1)
    act.wait_ge(K.evacuated.h, K.evacuated.n + LAT_TILES * n + j + 1)
    act.dma_start(K.z_dram[t * P:(t + 1) * P, ds(n * SLAB_N, SLAB_N)], K.z_buf[:, j, :]).then_inc(K.z_stored[j].h, 16)


class Step:

    def __init__(self, direction, tile, first):
        self.d, self.tile, self.first = direction, tile, first
        self.lat = tile < LAT_TILES


def scan_steps():
    orders = ([4, 5, 0, 1, 2, 3], [5, 4, 3, 2, 1, 0])
    return [Step(d, t, i == 0) for d in range(2) for i, t in enumerate(orders[d])]


def scan_stage(K, d_skip):
    nc = K.nc
    steps = scan_steps()
    lat = [s for s in steps if s.lat]
    NL, NS = len(lat), len(steps)
    base = {}
    for s in (K.staged, K.turned, K.src_read, K.cs_done, K.cs_read, K.decay_done, K.bc_done, K.diff_done,
              K.l_done, K.m_done, K.yd_done, K.yo_done, K.y_read, K.st_done, K.state_done, K.xdt_done, K.z_loaded, K.cb_done,
              K.cb_read, K.y_done, K.yd_read, K.small_loaded, K.stored, K.ss_done, K.rstd_done, K.fin_done, K.xdt_part):
        base[s] = s.n
    at = lambda s, g, per, k: base[s] + g * per + k + 1
    GH = GROUP_HEADS
    H2 = 2 * SSM_HEADS
    view = lambda ap: ap.rearrange("p (h d) -> p h d", d=HEAD_DIM)
    bc8 = lambda ap: ap.unsqueeze(2).to_broadcast([P, GH, HEAD_DIM])
    tri = [K.tri[:, 0, :], K.tri[:, 1, :]]

    with nc.Block() as block:
        @block.sync
        def _(sp):
            sp.dma_start(K.d_skip[:, :], d_skip.partition_broadcast(P)).then_inc(K.small_loaded.h, 16)
            sp.dma_start(K.tri[:, :, :], K.c_tri).then_inc(K.small_loaded.h, 16)
            sp.dma_start(K.ones[:, :], K.c_ones).then_inc(K.small_loaded.h, 16)
            sp.dma_start(K.order_mask[:, :, :], K.c_order_mask).then_inc(K.small_loaded.h, 16)
            for j in range(LAT_TILES):
                sp.wait_ge(K.z_stored[j].h, K.z_stored[j].n)
            with sp.Fori(0, SSM_GROUPS) as g:
                sp.wait_ge(K.ss_done.h, base[K.ss_done] + g)
                sp.dma_start(K.z_g[:, :, :], K.z_dram.rearrange("(t p) n -> p t n", p=P)[:, :, ds(g * GROUP_W, GROUP_W)])\
                  .then_inc(K.z_loaded.h, 16)

        @block.gpsimd
        def _(pool):
            with pool.Fori(0, SSM_GROUPS) as g:
                pool.wait_ge(K.staged.h, at(K.staged, g, 1, 0))
                pool.wait_ge(K.decay_done.h, at(K.decay_done, g, 1, 0))
                for k, s in enumerate(steps):
                    t = s.tile
                    if s.d == 1:
                        other = [o.tile for o in steps[:TOK_TILES]].index(t)
                        pool.wait_ge(K.st_done.h, at(K.st_done, g, NS, other))
                        if s.lat:
                            pool.wait_ge(K.yd_done.h, at(K.yd_done, g, NL, [o.tile for o in lat].index(t)))
                    c8 = 192 + (s.d * TOK_TILES + t) * GH
                    pool.sem_inc(K.pool_go.h, 1)
                    pool.tensor_tensor(view(K.xdt[:, t, :]),
                                       K.x_tok[:, t, ds(g * GROUP_W, GROUP_W)].rearrange("p (h d) -> p h d", d=HEAD_DIM),
                                       bc8(K.dt_g[:, s.d, t, :]), ALU.mult).then_inc(K.xdt_part.h, 1)
                    pool.wait_ge(K.xdt_part.h, at(K.xdt_part, g, NS, k))
                    pool.tensor_tensor(view(K.xdts[:, t, :]), view(K.xdt[:, t, :]), bc8(K.cs_exp[:, c8:c8 + GH]), ALU.mult)\
                        .then_inc(K.xdt_done.h, 1)

        @block.tensor
        def _(pe):
            def chunk(ap, t):
                return ap[:, t * P:(t + 1) * P]

            def decay_rows(g, i):
                s = lat[i]
                pe.wait_ge(K.diff_done.h, at(K.diff_done, g, NL, i - 1))
                for b in range(GH // 4):
                    pe.matmul(K.bank[b][:, :], K.ident_r[:, :], K.order_mask_r[:, s.d, :].unsqueeze(1).to_broadcast([P, 4, P]),
                              start=True, stop=False)
                for h in range(GH):
                    mm = pe.matmul(K.bank[h // 4][:, (h % 4) * P:(h % 4 + 1) * P],
                                   K.a_g[:, s.d, s.tile, h:h + 1].to_broadcast([P, P]), tri[s.d], start=False, stop=h % 4 == 3)
                mm.then_inc(K.bc_done.h, 1)

            def within(g, i):
                s = lat[i]
                pe.wait_ge(K.m_done.h, at(K.m_done, g, NL, i))
                pe.wait_ge(K.yd_read.h, at(K.yd_read, g, NL, i - 1))
                for h in range(GH):
                    mm = pe.matmul(K.bank[4][:, h * HEAD_DIM:(h + 1) * HEAD_DIM], K.decay[:, i % 2, h, :],
                                   K.xdt[:, s.tile, h * HEAD_DIM:(h + 1) * HEAD_DIM], start=True, stop=True)
                mm.then_inc(K.yd_done.h, 1)

            pe.wait_ge(K.small_loaded.h, base[K.small_loaded] + 64)
            with pe.Fori(0, SSM_GROUPS) as g:
                pe.wait_ge(K.staged.h, at(K.staged, g, 1, 0))
                pe.wait_ge(K.state_done.h, at(K.state_done, g, NS, -1))
                pe.wait_ge(K.yd_read.h, at(K.yd_read, g, NL, -1))
                pe.wait_ge(K.fin_done.h, at(K.fin_done, g, 1, -1))
                for t in range(TOK_TILES):
                    mm = pe.transpose(K.bank[6 + t // 4][:, (t % 4) * P:(t % 4 + 1) * P], chunk(K.BT_g, t), K.ident[:, :])
                mm.then_inc(K.turned.h, 1)
                for d in range(2):
                    pe.matmul(K.bank[5][:, d * 48:d * 48 + 48], tri[d], K.a_g[:, d, :, :], start=True, stop=True)
                mm = pe.matmul(K.bank[5][:, 96:192], K.ones[:, :], K.a_g[:, :, :, :], start=True, stop=True)
                mm.then_inc(K.cs_done.h, 1)
                for t in range(LAT_TILES):
                    mm = pe.matmul(K.bank[2][:, t * P:(t + 1) * P], chunk(K.BT_g, t), chunk(K.CT_g, t), start=True, stop=True)
                mm.then_inc(K.cb_done.h, 1)
                decay_rows(g, 0)
                i = 0
                for k, s in enumerate(steps):
                    if s.lat:
                        pe.wait_ge(K.state_done.h, at(K.state_done, g, NS, k - 1))
                        pe.wait_ge(K.y_read.h, at(K.y_read, g, NL, i - 1))
                        pe.wait_ge(K.cs_read.h, at(K.cs_read, g, 1, 0))
                        pe.matmul(K.bank[5][:, :], chunk(K.CT_g, s.tile), K.state[:, :], start=True, stop=True)\
                          .then_inc(K.yo_done.h, 1)
                    pe.wait_ge(K.xdt_done.h, at(K.xdt_done, g, NS, k))
                    if s.first:
                        pe.wait_ge(K.src_read.h, at(K.src_read, g, 1, 0))
                    pe.wait_ge(K.state_done.h, at(K.state_done, g, NS, k - 1))
                    pe.matmul(K.bank[6][:, :], K.B_tok[:, s.tile, :], K.xdts[:, s.tile, :], start=True, stop=True)\
                      .then_inc(K.st_done.h, 1)
                    if s.lat:
                        if i + 1 < NL:
                            decay_rows(g, i + 1)
                        within(g, i)
                        i += 1

        @block.scalar
        def _(act):
            link = Chain(act, K.act_chain)
            act.wait_ge(K.small_loaded.h, base[K.small_loaded] + 64)
            with act.Fori(0, SSM_GROUPS) as g:
                act.wait_ge(K.turned.h, at(K.turned, g, 1, 0))
                act.wait_ge(K.st_done.h, at(K.st_done, g, NS, -1))
                act.activation(K.B_tok[:, 0:4, :].rearrange("p t n -> p (t n)"), K.bank[6][:, :], ACT.Copy)
                act.activation(K.B_tok[:, 4:6, :].rearrange("p t n -> p (t n)"), K.bank[7][:, 0:256], ACT.Copy)\
                   .then_inc(K.src_read.h, 1)
                act.wait_ge(K.cs_read.h, at(K.cs_read, g, 1, 0))
                act.activation(K.cs_exp[:, :], K.cs[:, :], ACT.Exp).then_inc(K.decay_done.h, 1)
                for i, s in enumerate(lat):
                    act.wait_ge(K.diff_done.h, at(K.diff_done, g, NL, i))
                    m = K.decay[:, i % 2, :, :]
                    act.activation(m, m, ACT.Exp).then_inc(K.l_done.h, 1)
                act.wait_ge(K.y_done.h, at(K.y_done, g, 1, 0))
                for t in range(LAT_TILES):
                    ins = act.activation(K.z_g[:, t, :], K.y[:, t, :], ACT.Square, accum_out=K.y_ss[:, t:t + 1])
                ins.then_inc(K.ss_done.h, 1)
                act.wait_ge(K.ss_done.h, at(K.ss_done, g, 1, 0))
                act.activation(K.y_ln[:, :], K.y_ss[:, :], ACT.Ln, bias=K.eps5[:, 0:1], scale=1.0 / GROUP_W)\
                   .then_inc(K.act_chain.h, 1)
                act.wait_ge(K.act_chain.h, K.act_chain.n + g + 1)
                act.activation(K.y_rstd[:, :], K.y_ln[:, :], ACT.Exp, scale=-0.5).then_inc(K.rstd_done.h, 1)
            K.act_chain.n += SSM_GROUPS

        @block.vector
        def _(dve):
            links = SCAN_LINKS
            for j in range(LAT_TILES):
                dve.wait_ge(K.z_stored[j].h, K.z_stored[j].n)
            dve.wait_ge(K.small_loaded.h, base[K.small_loaded] + 64)
            dve.tensor_copy(K.ident_r[:, :], K.ident[:, :])
            dve.tensor_copy(K.order_mask_r[:, :, :], K.order_mask[:, :, :])
            with dve.Fori(0, SSM_GROUPS) as g:
                link = Chain(dve, K.dve_chain, g * links)

                def differences(i):
                    s = lat[i]
                    dve.wait_ge(K.bc_done.h, at(K.bc_done, g, NL, i))
                    dve.wait_ge(K.yd_done.h, at(K.yd_done, g, NL, i - 2))
                    sums = K.cs[:, (s.d * TOK_TILES + s.tile) * GH:(s.d * TOK_TILES + s.tile + 1) * GH]
                    dve.tensor_tensor(K.decay[:, i % 2, :, :], K.psum[:, 0:2, :].rearrange("p a (h l) -> p (a h) l", l=P),
                                      sums.unsqueeze(2).to_broadcast([P, GH, P]), ALU.subtract).then_inc(K.diff_done.h, 1)

                def matrices(i):
                    s = lat[i]
                    dve.wait_ge(K.l_done.h, at(K.l_done, g, NL, i))
                    m = K.decay[:, i % 2, :, :]
                    dve.tensor_tensor(m, m, K.cbT[:, s.tile, :].unsqueeze(1).to_broadcast([P, GH, P]), ALU.mult)\
                       .then_inc(K.m_done.h, 1)

                dve.wait_ge(K.yd_done.h, at(K.yd_done, g, NL, -1))
                dve.wait_ge(K.yo_done.h, at(K.yo_done, g, NL, -1))
                dve.wait_ge(K.st_done.h, at(K.st_done, g, NS, -1))
                dve.tensor_copy(K.BT_g[:, :].unsqueeze(1), K.BC[:, ds(g, 1), :])
                dve.tensor_copy(K.CT_g[:, :].unsqueeze(1), K.BC[:, ds(g + SSM_GROUPS, 1), :])
                for d in range(2):
                    dve.tensor_copy(K.dt_g[:, d, :, :], K.dt[:, :, ds(g * GH + d * SSM_HEADS, GH)])
                    ins = dve.tensor_copy(K.a_g[:, d, :, :], K.a[:, :, ds(g * GH + d * SSM_HEADS, GH)])
                ins.then_inc(K.staged.h, 1)
                dve.wait_ge(K.cs_done.h, at(K.cs_done, g, 1, 0))
                link(dve.tensor_copy(K.cs[:, 0:192], K.bank[5][:, 0:192]))
                dve.tensor_tensor(K.cs[:, 192:288], K.cs[:, 96:192], K.cs[:, 0:96], ALU.subtract).then_inc(K.cs_read.h, 1)
                dve.wait_ge(K.cb_done.h, at(K.cb_done, g, 1, 0))
                link(dve.tensor_copy(K.cbT[:, :, :].rearrange("p t n -> p (t n)"), K.bank[2][:, :]))
                if True:
                    dve.wait_ge(K.small_loaded.h, base[K.small_loaded] + 64)
                    for t in range(LAT_TILES):
                        ins = dve.tensor_tensor(view(K.y[:, t, :]),
                                                K.x_tok[:, t, ds(g * GROUP_W, GROUP_W)].rearrange("p (h d) -> p h d", d=HEAD_DIM),
                                                bc8(K.d_skip[:, ds(g * GH, GH)]), ALU.mult)
                    link(ins)
                dve.wait_ge(K.decay_done.h, at(K.decay_done, g, 1, 0))
                differences(0)
                i = 0
                for k, s in enumerate(steps):
                    c8 = (s.d * TOK_TILES + s.tile) * GH
                    if s.lat:
                        y = K.y[:, s.tile, :]
                        dve.wait_ge(K.yo_done.h, at(K.yo_done, g, NL, i))
                        link(dve.tensor_tensor(view(K.y_tmp[:, :]), view(K.bank[5][:, :]), bc8(K.cs_exp[:, c8:c8 + GH]), ALU.mult))
                        dve.tensor_tensor(y, y, K.y_tmp[:, :], ALU.add).then_inc(K.y_read.h, 1)
                        dve.wait_ge(K.y_read.h, at(K.y_read, g, NL, i))
                        matrices(i)
                    dve.wait_ge(K.st_done.h, at(K.st_done, g, NS, k))
                    if s.first:
                        dve.tensor_copy(K.state[:, :], K.bank[6][:, :]).then_inc(K.state_done.h, 1)
                    else:
                        if s.lat:
                            dve.wait_ge(K.yo_done.h, at(K.yo_done, g, NL, i))
                        else:
                            dve.wait_ge(K.state_done.h, at(K.state_done, g, NS, k - 1))
                        link(dve.tensor_tensor(view(K.state[:, :]), view(K.state[:, :]), bc8(K.cs_exp[:, 96 + c8:96 + c8 + GH]),
                                               ALU.mult))
                        dve.tensor_tensor(K.state[:, :], K.state[:, :], K.bank[6][:, :], ALU.add).then_inc(K.state_done.h, 1)
                    if s.lat:
                        if i + 1 < NL:
                            differences(i + 1)
                        dve.wait_ge(K.yd_done.h, at(K.yd_done, g, NL, i))
                        dve.tensor_tensor(y, y, K.bank[4][:, :], ALU.add).then_inc(K.yd_read.h, 1)
                        dve.wait_ge(K.yd_read.h, at(K.yd_read, g, NL, i))
                        i += 1
                dve.wait_ge(K.z_loaded.h, base[K.z_loaded] + 16 * (g + 1))
                dve.tensor_tensor(K.y[:, :, :], K.y[:, :, :], K.z_g[:, :, :], ALU.mult).then_inc(K.y_done.h, 1)
                dve.wait_ge(K.rstd_done.h, at(K.rstd_done, g, 1, 0))
                for t in range(LAT_TILES):
                    ins = dve.tensor_scalar(K.x_tok[:, t, ds(g * GROUP_W, GROUP_W)], K.y[:, t, :], K.y_rstd[:, t:t + 1], None, ALU.mult)
                ins.then_inc(K.fin_done.h, 1)
                dve.wait_ge(K.fin_done.h, at(K.fin_done, g, 1, 0))
                assert link.k == links, link.k
            K.dve_chain.n += SSM_GROUPS * links
    for s, per in ((K.staged, 1), (K.turned, 1), (K.src_read, 1), (K.cs_done, 1), (K.cs_read, 1), (K.decay_done, 1),
                   (K.bc_done, NL), (K.diff_done, NL), (K.l_done, NL), (K.m_done, NL), (K.yd_done, NL),
                   (K.yd_read, NL), (K.yo_done, NL), (K.y_read, NL), (K.st_done, NS), (K.state_done, NS), (K.xdt_done, NS),
                   (K.cb_done, 1), (K.y_done, 1), (K.z_loaded, 16), (K.ss_done, 1), (K.rstd_done, 1), (K.fin_done, 1),
                   (K.xdt_part, 2 * TOK_TILES)):
        s.n += per * SSM_GROUPS
    K.small_loaded.n += 64


SCAN_LINKS = 3 + 8 + 10


def spill_stage(K):
    with K.nc.Block() as block:
        @block.sync
        def _(sp):
            sp.dma_start(K.x_dram.rearrange("(t p) n -> p t n", p=P), K.x[:, 0:LAT_TILES, :]).then_inc(K.x_stored.h, 16)
            sp.wait_ge(K.x_stored.h, 16)


def reload_stage(K):
    with K.nc.Block() as block:
        @block.sync
        def _(sp):
            sp.dma_start(K.x[:, 0:LAT_TILES, :], K.x_dram.rearrange("(t p) n -> p t n", p=P)).then_inc(K.x_stored.h, 16)
            sp.wait_ge(K.x_stored.h, 32)


def load_stage(K, pairs):
    sm0 = K.small_loaded.n
    with K.nc.Block() as block:
        @block.sync
        def _(sp):
            for out, src in pairs:
                sp.dma_start(out, src).then_inc(K.small_loaded.h, 16)
            sp.wait_ge(K.small_loaded.h, sm0 + 16 * len(pairs))
    K.small_loaded.n += 16 * len(pairs)


def lambda_stage(K, lq1, lk1, lq2, lk2):
    load_stage(K, [(K.lam_in[:, i, :], v.partition_broadcast(P)) for i, v in enumerate((lq1, lk1, lq2, lk2))])
    ac0 = K.act_chain.n
    dv0 = K.dve_chain.n
    with K.nc.Block() as block:
        @block.vector
        def _(dve):
            link = Chain(dve, K.dve_chain)
            v = K.lam_in[:, :, :].rearrange("p (a b) d -> p a b d", b=2)
            link(dve.tensor_tensor(v[:, :, 0, :], v[:, :, 0, :], v[:, :, 1, :], ALU.mult))
            link(dve.tensor_reduce(K.lam_sum[:, :], v[:, :, 0, :], AX.X, ALU.add))
            dve.wait_ge(K.act_chain.h, ac0 + 1)
            link(dve.tensor_scalar(K.neg_lam[:, :], K.lam_sum[:, 1:2], K.lam_sum[:, 0:1], LAM_INIT, ALU.subtract, ALU.subtract))
            dve.tensor_scalar(K.sub_gain[:, :], K.vecs[:, SUBLN_AT:SUBLN_AT + 1], 1.0 - LAM_INIT, None, ALU.mult)
            K.dve_chain.n += link.k

        @block.scalar
        def _(act):
            act.wait_ge(K.dve_chain.h, dv0 + 2)
            act.activation(K.lam_sum[:, :], K.lam_sum[:, :], ACT.Exp).then_inc(K.act_chain.h, 1)
    K.act_chain.n += 1


def bias_table_stage(K, rpb):
    half = 8 * REL_ROWS
    tr0 = K.turned.n
    load_stage(K, [(K.rpb_rows[0:half, :, :], rpb.rearrange("(a h) o j -> (h o) a j", a=2)), (K.shift[:, :], K.c_shift),
                   (K.col_mask[:, :], K.c_col_mask)])
    with K.nc.Block() as block:
        @block.tensor
        def _(pe):
            for a in range(2):
                mm = pe.transpose(K.bank[a][0:REL_COLS, 0:half], K.rpb_rows[0:half, a, :], K.ident[0:half, 0:half])
            mm.then_inc(K.turned.h, 1)

        @block.vector
        def _(dve):
            link = Chain(dve, K.dve_chain)
            link(dve.tensor_scalar(K.rpbT[:, :, :].rearrange("p h o -> p (h o)"), K.x[:, 0, 0:20 * 16], 0.0, None, ALU.mult))
            dve.tensor_copy(K.shift_r[:, :], K.shift[:, :])
            dve.wait_ge(K.turned.h, tr0 + 1)
            for a in range(2):
                src = K.bank[a][0:REL_COLS, 0:half].rearrange("j (h o) -> j h o", o=REL_ROWS)
                heads = slice(8 * a, 8 * a + 8)
                for r in range(2):
                    ins = dve.tensor_copy(K.rpbT[32 * r:32 * r + REL_COLS, heads, r:r + REL_ROWS], src)
                    if r == 0:
                        link(ins)
                hi = K.rpbT[0:REL_COLS, heads, 0:REL_ROWS].bitcast(F32)
                for r in range(2, 4):
                    dve.tensor_tensor(K.rpbT[32 * r:32 * r + REL_COLS, heads, r - 2:r - 2 + REL_ROWS], src, hi, ALU.subtract)
            assert link.k == 3
    K.turned.n += 1
    K.dve_chain.n += 3


CREDIT = 8
NORM1_AT, NORM2_AT, SUBLN_AT = 4 * KD, 6 * KD, 8 * KD


def program(nc, A, out):
    K = Kernel()
    K.nc = nc
    with ExitStack() as ctx:

        def place(name, shape, offset, dtype=F32):
            return nc.alloc_sbuf_tensor_at(name, shape, dtype, offset=offset)

        top = -(-nc.sbuf_base // 32) * 32
        end = nc.sbuf_usable_end

        class Cursor:

            def __init__(self, at):
                self.at = at

            def put(self, name, shape, dtype=F32):
                tensor = place(name, shape, self.at, dtype)
                self.at += -(-4 * int(np.prod(shape[1:])) // 32) * 32
                assert self.at <= end, (name, self.at, end)
                return tensor

        kept = Cursor(top)
        keep = kept.put

        def region(size):
            at = kept.at
            kept.at += size
            return at

        tile_bytes = TOK_TILES * D * 4
        X = region(tile_bytes)
        H = region(2 * tile_bytes)
        K.x = place("x", [P, TOK_TILES, D], X)
        c = Cursor(H)
        K.hT_hi = c.put("hT_hi", [P, KD, N_TOK], F32R)
        K.hT_lo = c.put("hT_lo", [P, KD, N_TOK], F32R)
        K.raw = [keep(f"raw{h}", [P, SLAB_K, SLAB_N]) for h in range(2)]
        K.w_hi = [keep(f"w_hi{h}", [P, SLAB_K, SLAB_N], F32R) for h in range(2)]
        K.w_lo = [keep(f"w_lo{h}", [P, SLAB_K, SLAB_N], F32R) for h in range(2)]
        K.ident = keep("ident", [P, P])
        K.modT_all = keep("modT_all", [P, 4 * 6 * KD, 2])
        K.vecs = keep("vecs", [P, 3 * P])
        K.cT = keep("cT", [P, 2, KD, 2])
        K.eps6 = keep("eps6", [P, 1])
        K.eps5 = keep("eps5", [P, 1])
        K.one = keep("one", [P, 1])
        K.eps_ln = keep("eps_ln", [P, 1])
        K.ssum = keep("ssum", [P, 8])
        K.lnms = keep("lnms", [P, 8])
        K.rstd = keep("rstd", [P, 8])
        K.mod_scale = keep("mod_scale", [P, KD, 2])
        K.head_ss = keep("head_ss", [P, 2, 32])
        K.head_ln = keep("head_ln", [P, 2, 32])
        K.head_rstd = keep("head_rstd", [P, 2, 32])
        K.neg_max = keep("neg_max", [P, 2, 2])
        K.p_sum = keep("p_sum", [P, 2, 2])
        K.p_inv = keep("p_inv", [P, 2, 2])
        K.sink_exp = keep("sink_exp", [P, 2, 2])
        K.sink_pair = keep("sink_pair", [P, 2])
        K.lam_sum = keep("lam_sum", [P, 2])
        K.neg_lam = keep("neg_lam", [P, 1])
        K.sub_gain = keep("sub_gain", [P, 1])
        K.ln_stats = keep("ln_stats", [P, TOK_TILES, 2, 6])
        K.ln_mv = keep("ln_mv", [P, TOK_TILES, 2])
        K.y_ss = keep("y_ss", [P, 4])
        K.y_ln = keep("y_ln", [P, 4])
        K.y_rstd = keep("y_rstd", [P, 4])
        R = kept.at
        qkv_end = R + TOK_TILES * 3 * D * 4
        c = Cursor(R)
        K.mod_first = [c.put(f"mod_first{b}", [P, KD, SLAB_N]) for b in range(4)]
        K.vec_in = c.put("vec_in", [P, 3, P])
        K.cexp = c.put("cexp", [P, 4 * KD])
        K.first_rows = c.put("first_rows", [2, 4, SLAB_N])
        K.xhat = place("xhat", [P, TOK_TILES, D], R)
        K.feat = place("feat", [P, 2, N_TOK], qkv_end)
        c = Cursor(R)
        K.scaled_buf = c.put("scaled_buf", [P, 2, SLAB_N])
        K.uT_hi = c.put("uT_hi", [P, SLAB_K, N_TOK], F32R)
        K.uT_lo = c.put("uT_lo", [P, SLAB_K, N_TOK], F32R)
        K.relu_mlp = c.put("relu_mlp", [P, 2, SLAB_N])
        K.sq = c.put("sq", [P, 2, SLAB_N])
        gate_at = R + 40 * 1024
        assert c.at <= gate_at
        K.gate = place("gate", [P, 2, D], gate_at)
        c = Cursor(R)
        K.ln_gain = c.put("ln_gain", [P, D])
        K.ln_bias = c.put("ln_bias", [P, D])
        K.lam_in = place("lam_in", [P, 4, HEAD_DIM], R)
        K.qkv = place("qkv", [P, TOK_TILES, 3 * D], R)
        c = Cursor(qkv_end)
        K.head_gain = c.put("head_gain", [P, 2, HEAD_DIM])
        K.rope_cos = c.put("rope_cos", [P, LAT_TILES, HEAD_DIM])
        K.rope_sin = c.put("rope_sin", [P, LAT_TILES, HEAD_DIM])
        tables_at = c.at
        K.sink_b = c.put("sink_b", [P, 18])
        K.col_mask = c.put("col_mask", [P, GRID_W])
        K.shift = c.put("shift", [P, 3 * GRID_W - 1])
        K.shift_r = c.put("shift_r", [P, 3 * GRID_W - 1], F32R)
        K.rpbT = c.put("rpbT", [P, 20, 16], F32R)
        K.near_mask = c.put("near_mask", [P, 2, P])
        K.rpb_rows = c.put("rpb_rows", [P, 2, REL_COLS])
        c = Cursor(H)
        K.head_sq = c.put("head_sq", [P, 2, 2 * D])
        K.head_swap = c.put("head_swap", [P, 2, 2 * D])
        c = Cursor(H)
        K.heads = [c.put(f"heads{q}", [P, TOK_TILES, P]) for q in range(2)]
        K.headsT = [[c.put(f"headsT{b}{q}", [P, N_TOK]) for q in range(2)] for b in range(2)]
        K.p_mat = [c.put(f"p_mat{m}", [P, N_TOK]) for m in range(2)]
        K.pT_mat = [c.put(f"pT_mat{m}", [P, N_TOK]) for m in range(2)]
        K.w_mat = place("w_mat", [P, N_TOK], c.at)
        K.G = [c.put("G0", [P, GRID_W, 2, 16]), place("G1", [P, GRID_W, 2, 16], X + LAT_TILES * D * 4)]
        K.mod_slab = [c.put(f"mod_slab{k}", [P, KD, P]) for k in range(2)]
        K.mod_row = c.put("mod_row", [2, 2, 2 * P])
        assert c.at <= H + 2 * tile_bytes
        c = Cursor(tables_at)
        K.slab_sq = c.put("slab_sq", [P, 2, SLAB_N])
        K.slab_swap = c.put("slab_swap", [P, 2, SLAB_N])
        c = Cursor(R)
        K.qkv2 = c.put("qkv2", [P, TOK_TILES, 3 * SLAB_N])
        K.roped = c.put("roped", [P, LAT_TILES, 21 * HEAD_DIM])
        K.heads.append(c.put("heads2", [P, TOK_TILES, P]))
        for b in range(2):
            K.headsT[b].append(c.put(f"headsT{b}2", [P, N_TOK]))
        c = Cursor(R)
        K.x_tok = c.put("x_tok", [P, TOK_TILES, SSM_INNER])
        K.BC = c.put("BC", [P, 2 * SSM_GROUPS, N_TOK])
        tail = c.at
        K.relu_conv = c.put("relu_conv", [P, 2, SLAB_N])
        conv_out1 = c.put("conv_out1", [P, 2, OUT])
        c = Cursor(tail)
        K.tri = c.put("tri", [P, 2, P])
        K.order_mask = c.put("order_mask", [P, 2, P])
        K.ones = c.put("ones", [P, P])
        K.ident_r = c.put("ident_r", [P, P], F32R)
        K.order_mask_r = c.put("order_mask_r", [P, 2, P], F32R)
        K.d_skip = c.put("d_skip", [P, SSM_HEADS])
        c = Cursor(X)
        K.xt = c.put("xt", [P, 4, ROW])
        K.conv_out = [c.put("conv_out0", [P, 2, OUT]), conv_out1]
        K.dt = c.put("dt", [P, TOK_TILES, 2 * SSM_HEADS])
        K.a = c.put("a", [P, TOK_TILES, 2 * SSM_HEADS])
        K.conv_cols = c.put("conv_cols", [P, TAPS * 24])
        K.vec_cols = c.put("vec_cols", [P, 48])
        assert c.at <= H
        K.z_buf = place("z_buf", [P, LAT_TILES, SLAB_N], X)
        c = Cursor(X)
        K.decay = c.put("decay", [P, 2, GROUP_HEADS, P])
        K.z_g = c.put("z_g", [P, LAT_TILES, GROUP_W])
        K.cbT = c.put("cbT", [P, LAT_TILES, P])
        c = Cursor(H)
        K.BT_g = c.put("BT_g", [P, N_TOK])
        K.CT_g = c.put("CT_g", [P, N_TOK])
        K.B_tok = c.put("B_tok", [P, TOK_TILES, SSM_STATE])
        K.xdt = c.put("xdt", [P, TOK_TILES, GROUP_W])
        K.xdts = c.put("xdts", [P, TOK_TILES, GROUP_W])
        K.y = c.put("y", [P, LAT_TILES, GROUP_W])
        K.state = c.put("state", [P, GROUP_W])
        K.y_tmp = c.put("y_tmp", [P, GROUP_W])
        K.cs = c.put("cs", [P, 288])
        K.cs_exp = c.put("cs_exp", [P, 288])
        K.dt_g = c.put("dt_g", [P, 2, TOK_TILES, GROUP_HEADS])
        K.a_g = c.put("a_g", [P, 2, TOK_TILES, GROUP_HEADS])
        assert c.at <= H + 2 * tile_bytes
        c = Cursor(R)
        K.dt_w = c.put("dt_w", [P, KD, 2 * SSM_HEADS])
        K.dt_w_hi = c.put("dt_w_hi", [P, KD, 2 * SSM_HEADS], F32R)
        K.dt_w_lo = c.put("dt_w_lo", [P, KD, 2 * SSM_HEADS], F32R)
        K.dt_bias = c.put("dt_bias", [P, 2 * SSM_HEADS])
        K.a_neg = c.put("a_neg", [P, 2 * SSM_HEADS])
        K.conv_rows = c.put("conv_rows", [P, P])
        K.vec_rows = c.put("vec_rows", [P, P])
        K.dtT = c.put("dtT", [2 * SSM_HEADS, N_TOK])
        c = Cursor(H)
        K.yT_hi = c.put("yT_hi", [P, 16, N_LAT], F32R)
        K.y_feat = c.put("y_feat", [P, 2, N_TOK])
        K.yT_lo = place("yT_lo", [P, 16, N_LAT], R + TOK_TILES * SSM_INNER * 4, F32R)

        K.psum = ctx.enter_context(nc.psum_tensor("psum", [P, 8, 512], F32))
        K.bank = [K.psum[:, b, :] for b in range(8)]
        K.x_dram = nc.dram_tensor("x_rest", [N_LAT, D], F32).ap()
        K.z_dram = nc.dram_tensor("z_rest", [N_LAT, SSM_INNER], F32).ap()

        K.credited = []

        def sem(name, credit=CREDIT):
            s = Sem(ctx.enter_context(nc.semaphore(name)), credit)
            if credit:
                K.credited.append(s)
            return s

        K.hi_done = sem("hi_done", 0)
        K.lo_done = sem("lo_done", 0)
        K.w_used = sem("w_used", 0)
        K.small_loaded = sem("small_loaded", 0)
        K.inputs_loaded = sem("inputs_loaded", 0)
        K.ident_loaded = sem("ident_loaded", 0)
        K.stored = sem("stored", 0)
        K.x_stored = sem("x_stored", 0)
        K.z_loaded = sem("z_loaded", 0)
        K.raw_loaded = [sem(f"raw_loaded{h}", 0) for h in range(2)]
        K.mod_loaded = [sem(f"mod_loaded{s}", 0) for s in range(4)]
        K.z_stored = [sem(f"z_stored{j}") for j in range(LAT_TILES)]
        K.mm_done = sem("mm_done")
        K.evacuated = sem("evacuated")
        K.scaled = sem("scaled")
        K.added = sem("added")
        K.turned = sem("turned")
        K.relu_done = sem("relu_done")
        K.sq_done = sem("sq_done")
        K.u_hi_done = sem("u_hi_done")
        K.u_lo_done = sem("u_lo_done")
        K.normed = sem("normed")
        K.feat_done = sem("feat_done")
        K.feat_hi = sem("feat_hi")
        K.feat_lo = sem("feat_lo")
        K.rstd_done = sem("rstd_done")
        K.act_chain = sem("act_chain")
        K.dve_chain = sem("dve_chain")
        K.pool_chain = sem("pool_chain")
        K.pool_go = sem("pool_go", 0)
        K.mod_used = sem("mod_used")
        K.row_out = sem("row_out")
        K.mod_turned = sem("mod_turned")
        K.c_done = sem("c_done")
        K.sums_done = sem("sums_done")
        K.gained = sem("gained")
        K.swapped = sem("swapped")
        K.rotated = sem("rotated")
        K.staged = sem("staged")
        K.src_turned = sem("src_turned")
        K.src_read = sem("src_read")
        K.s_done = sem("s_done")
        K.nm_done = sem("nm_done")
        K.p_done = sem("p_done")
        K.w_done = sem("w_done")
        K.pt_done = sem("pt_done")
        K.o_done = sem("o_done")
        K.o_read = sem("o_read")
        K.g_done = sem("g_done")
        K.g_ready = sem("g_ready")
        K.xt_read = sem("xt_read")
        K.conv_done = sem("conv_done")
        K.silu_done = sem("silu_done")
        K.back_done = sem("back_done")
        K.back_read = sem("back_read")
        K.tap_done = sem("tap_done")
        K.a_neg_done = sem("a_neg_done")
        K.cs_done = sem("cs_done")
        K.cs_read = sem("cs_read")
        K.decay_done = sem("decay_done")
        K.bc_done = sem("bc_done")
        K.diff_done = sem("diff_done")
        K.l_done = sem("l_done")
        K.m_done = sem("m_done")
        K.yd_done = sem("yd_done")
        K.yd_read = sem("yd_read")
        K.yo_done = sem("yo_done")
        K.y_read = sem("y_read")
        K.st_done = sem("st_done")
        K.state_done = sem("state_done")
        K.xdt_done = sem("xdt_done")
        K.xdt_part = sem("xdt_part")
        K.cb_done = sem("cb_done")
        K.cb_read = sem("cb_read")
        K.y_done = sem("y_done")
        K.ss_done = sem("ss_done")
        K.fin_done = sem("fin_done")
        K.pt_read = [sem(f"pt_read{m}") for m in range(2)]
        K.slabs = 0
        K.c_ident, K.c_shift, K.c_col_mask = A["const_ident"], A["const_shift"], A["const_col_mask"]
        K.c_tri, K.c_order_mask, K.c_ones = A["const_tri"], A["const_order_mask"], A["const_ones"]

        every, latent = list(range(TOK_TILES)), list(range(LAT_TILES))
        w_in = A["ssm_w_in_2"][0]
        streams = [
            columns_stream(A["a_w_qkv"][0], 6), columns_stream(A["a_w_o"][0], 2), mlp_stream(A["w_mlp1"][0], A["w_mlp2"][0]),
            columns_stream(A["b_w_qkv"][0], 6), columns_stream(A["b_w_o"][0], 2), mlp_stream(A["w_mlp1"][1], A["w_mlp2"][1]),
            columns_stream(A["att_w_in_2"][0], 3), columns_stream(A["att_w_out_2"][0], 2), mlp_stream(A["ff_w1_2"][0], A["ff_w2_2"][0]),
            columns_stream(w_in, 6, SSM_INNER), columns_stream(w_in, 4),
            rows_stream(A["ssm_w_out_2"][0]), mlp_stream(A["ff_w1_2"][1], A["ff_w2_2"][1])]
        following = iter(zip(streams, streams[1:] + [None]))

        def next_streams():
            s, n = next(following)
            return dict(stream=s, nxt=n)

        def modulated(first_shift):
            return dict(scale=lambda k, cls: K.mod_scale[:, k, cls:cls + 1],
                        bias=lambda k, cls: K.modT[:, first_shift * KD + k, cls:cls + 1])

        x_at = lambda t, k: K.x[:, t, k * P:(k + 1) * P]
        xhat_at = lambda t, k: K.xhat[:, t, k * P:(k + 1) * P]
        qkv_at = lambda t, k: K.qkv[:, t, k * P:(k + 1) * P]
        qkv2_at = lambda t, k: K.qkv2[:, t, k * P:(k + 1) * P]

        def to(dst):
            return lambda act, count, n, t, bank, j: copy_out(K, dst, act, count, n, t, bank, j)

        def gated(dve, count, n, t, bank, j):
            gate_out(K, dve, count, n, t, bank, j)

        def mlp(tiles):
            K.relu = K.relu_mlp
            mlp_stage(K, **next_streams(), tiles=tiles)

        def of_layer(n):
            K.modT = K.modT_all[:, n * 6 * KD:(n + 1) * 6 * KD, :]

        flat = lambda name: A[name].rearrange("l n -> (l n)")
        start_stage(K, A["x"][0], A["ctx"][0], streams[0], A["w_mod"][0],
                    ((A["c"][0], A["c_ctx"], A["c_2"][0], A["c_ctx_2"], flat("norm1_g"), flat("norm2_g"), A["a_subln_g"][0]),
                                     (flat("b_mod"),), (flat("b_mod_2"),)))
        of_layer(0)
        scale_stage(K, 1, NORM1_AT)
        operand_stage(K, xhat_at, KD, True, K.hT_hi, K.hT_lo, **modulated(0), rms_of=K.x)
        lambda_stage(K, *(A[f"a_lambda_{n}"][0] for n in ("q1", "k1", "q2", "k2")))
        heads_gemm_stage(K, **next_streams(), parts=((0, 2, every, 0), (2, 4, every, 1), (4, 6, every, None)),
                         gains=(A["a_q_norm_g"][0], A["a_k_norm_g"][0]), rope=(A["const_cos_pairs"], A["const_sin_pairs"]))

        def stage_qk(pool, i, pi, q_tiles=TOK_TILES):
            pool.tensor_copy(K.heads[0][:, 0:q_tiles, :], K.qkv[:, 0:q_tiles, ds(i * (2 * P) + pi * P, P)])
            pool.tensor_copy(K.heads[1][:, :, :], K.qkv[:, :, ds(i * (2 * P) + (pi * P + D), P)]).then_inc(K.staged.h, 1)

        full = [0, 1, 2, 3, 4, 5]
        mixed = [0, 4, 1, 5, 2, 3]
        attention_stage(K, [Unit(t, full if t < LAT_TILES else [4, 5]) for t in mixed], PAIRS // 2, stage_qk,
                        lambda i, pi, m, kt: K.qkv[:, kt, ds(i * (2 * P) + (pi * P + 2 * D), P)],
                        lambda i, pi, t: K.qkv[:, t, ds(i * (2 * P) + pi * P, P)],
                        mods=[Modulation(0, A["w_mod"][0], 2 * KD, 4), Modulation(1, A["w_mod"][1], 0, 6)], mods_at=[0, 2, 2, 2, 2, 2],
                        diff=True)
        head_norm_stage(K, K.qkv, PAIRS, P, every)
        operand_stage(K, qkv_at, KD, True, K.hT_hi, K.hT_lo, scale=lambda k, cls: K.sub_gain[:, 0:1], gate=2)
        gemm_stage(K, **next_streams(), k_tiles=KD, tiles=every, evacuate=gated, evac_on="dve")
        scale_stage(K, 4, NORM2_AT)
        operand_stage(K, xhat_at, KD, True, K.hT_hi, K.hT_lo, **modulated(3), rms_of=K.x, gate=5)
        mlp(every)

        of_layer(1)
        scale_stage(K, 1, NORM1_AT + KD)
        operand_stage(K, xhat_at, KD, True, K.hT_hi, K.hT_lo, **modulated(0), rms_of=K.x)
        heads_gemm_stage(K, **next_streams(), parts=((0, 2, latent, 0), (2, 4, every, 1), (4, 6, every, None)),
                         gains=(A["b_q_norm_g"][0], A["b_k_norm_g"][0]))
        bias_table_stage(K, A["b_rpb"][0])
        attention_stage(K, [Unit(t, full) for t in latent], PAIRS // 2, lambda pool, i, pi: stage_qk(pool, i, pi, LAT_TILES),
                        lambda i, pi, m, kt: K.qkv[:, kt, ds(i * (2 * P) + (pi * P + 2 * D + m * HEAD_DIM), HEAD_DIM)],
                        lambda i, pi, t: K.qkv[:, t, ds(i * (2 * P) + pi * P, P)],
                        mods=[Modulation(2, A["w_mod_2"][0], 0, 6)], mods_at=[0, 2, 2, 2], rel_bias=True, q_tiles=LAT_TILES)
        operand_stage(K, qkv_at, KD, False, K.hT_hi, K.hT_lo, gate=2)
        gemm_stage(K, **next_streams(), k_tiles=KD, tiles=latent, evacuate=gated, evac_on="dve")
        scale_stage(K, 4, NORM2_AT + KD)
        operand_stage(K, xhat_at, KD, False, K.hT_hi, K.hT_lo, **modulated(3), rms_of=K.x, gate=5)
        mlp(latent)

        of_layer(2)
        load_stage(K, [(K.x[:, LAT_TILES:TOK_TILES, :], A["ctx_2"][0].rearrange("(t p) n -> p t n", p=P))])
        scale_stage(K, 1)
        operand_stage(K, x_at, KD, True, K.hT_hi, K.hT_lo, **modulated(0))
        gemm_stage(K, **next_streams(), k_tiles=KD, tiles=every, evacuate=to(K.qkv2), evac_on="act")
        rope_stage(K, 20, (A["const_cos_axes"], A["const_sin_axes"]))
        load_stage(K, [(K.sink_b[:, 0:16], A["att_sink_2"][0].partition_broadcast(P)), (K.near_mask[:, :, :], A["const_near_mask"])])

        def stage_grouped(pool, i, pi):
            q, k = i * (2 * P) + pi * P, i * HEAD_DIM + (D + pi // 2 * HEAD_DIM)
            pool.tensor_copy(K.heads[0][:, 0:LAT_TILES, :], K.roped[:, :, ds(q, P)])
            pool.tensor_copy(K.heads[0][:, LAT_TILES:TOK_TILES, :], K.qkv2[:, LAT_TILES:TOK_TILES, ds(q, P)])
            for m in range(2):
                half = slice(m * HEAD_DIM, (m + 1) * HEAD_DIM)
                pool.tensor_copy(K.heads[1][:, 0:LAT_TILES, half], K.roped[:, :, ds(k, HEAD_DIM)])
                pool.tensor_copy(K.heads[1][:, LAT_TILES:TOK_TILES, half], K.qkv2[:, LAT_TILES:TOK_TILES, ds(k, HEAD_DIM)])
            pool.tensor_copy(K.heads[2][:, :, :], K.qkv2[:, :, ds(q, P)]).then_inc(K.staged.h, 1)

        units = []
        for t in mixed:
            near = [s for s in (t - 1, t, t + 1) if 0 <= s < LAT_TILES] if t < LAT_TILES else []
            masks = {2 + i: K.near_mask[:, 0 if s < t else 1, :] for i, s in enumerate(near) if s != t}
            units.append(Unit(t, [4, 5] + near, masks, unrotated=2))
        attention_stage(K, units, 4, stage_grouped, lambda i, pi, m, kt: K.qkv2[:, kt, ds(i * HEAD_DIM + (D + 4 * HEAD_DIM), HEAD_DIM)],
                        lambda i, pi, t: K.qkv2[:, t, ds(i * (2 * P) + pi * P, P)],
                        mods=[Modulation(3, A["w_mod_2"][1], 0, 6)], mods_at=[0, 2, 1, 1, 1, 1], sink=True, unrotated=True)
        operand_stage(K, qkv2_at, KD, True, K.hT_hi, K.hT_lo, gate=2, gate_scale=1 / ALPHA)
        gemm_stage(K, **next_streams(), k_tiles=KD, tiles=every, evacuate=gated, evac_on="dve")
        layer_norm_stage(K, A["ln_mix_g_2"][0], A["ln_mix_b_2"][0], every)
        scale_stage(K, 4)
        operand_stage(K, x_at, KD, True, K.hT_hi, K.hT_lo, **modulated(3), gate=5, gate_scale=1 / ALPHA)
        mlp(every)
        layer_norm_stage(K, A["ln_ff_g_2"][0], A["ln_ff_b_2"][0], every)

        of_layer(3)
        scale_stage(K, 1)
        operand_stage(K, x_at, KD, True, K.hT_hi, K.hT_lo, **modulated(0))
        spill_stage(K)
        dt_stage(K, w_in[:, SSM_INNER + 6 * SLAB_N:SSM_INNER + 6 * SLAB_N + 2 * SSM_HEADS],
                 A["ssm_dt_bias_2"][0].rearrange("d h -> (d h)"), A["ssm_a_log_2"][0].rearrange("d h -> (d h)"),
                 A["ssm_conv_w_2"][0], A["ssm_conv_b_2"][0], A["ssm_norm_g_2"][0])
        K.relu = K.relu_conv
        conv_stage(K, **next_streams())
        gemm_stage(K, **next_streams(), k_tiles=KD, tiles=latent, evac_on="act",
                   evacuate=lambda act, count, n, t, bank, j: silu_store_out(K, act, count, n, t, bank, j))
        for s in K.z_stored:
            s.n += 16 * 4
        scan_stage(K, A["ssm_d_2"][0])
        operand_stage(K, lambda t, k: K.x_tok[:, t, k * P:(k + 1) * P], 16, False, K.yT_hi, K.yT_lo,
                      scale=lambda k, cls: K.vec_cols[:, 32 + k:33 + k], feat=K.y_feat)
        reload_stage(K)
        gate_stage(K, 2, 1 / ALPHA)
        gemm_stage(K, **next_streams(), k_tiles=16, tiles=latent, evacuate=gated, evac_on="dve", hi_t=K.yT_hi, lo_t=K.yT_lo)
        layer_norm_stage(K, A["ln_mix_g_2"][1], A["ln_mix_b_2"][1], latent)
        scale_stage(K, 4)
        operand_stage(K, x_at, KD, False, K.hT_hi, K.hT_lo, **modulated(3), gate=5, gate_scale=1 / ALPHA)
        mlp(latent)
        layer_norm_stage(K, A["ln_ff_g_2"][1], A["ln_ff_b_2"][1], latent, store=out)


def constants():
    t = np.arange(N_LAT)
    row, col = (t // GRID_W).astype(np.float32), (t % GRID_W).astype(np.float32)
    lay = lambda a: np.ascontiguousarray(a.reshape(LAT_TILES, P, -1).transpose(1, 0, 2), np.float32)
    c = {"ident": np.eye(P, dtype=np.float32), "ones": np.ones((P, P), np.float32)}
    nf = HEAD_DIM // 4
    inv = (10000.0 ** (-np.arange(nf, dtype=np.float32) / nf)).astype(np.float32)
    ang = np.concatenate([row[:, None] * inv, col[:, None] * inv], axis=-1)
    c["cos_pairs"] = lay(np.repeat(np.cos(ang), 2, axis=-1))
    c["sin_pairs"] = lay(np.stack([-np.sin(ang), np.sin(ang)], axis=-1).reshape(N_LAT, HEAD_DIM))
    ar, ac = row[:, None] * inv, col[:, None] * inv
    c["cos_axes"] = lay(np.concatenate([np.cos(ar), np.cos(ar), np.cos(ac), np.cos(ac)], axis=-1))
    c["sin_axes"] = lay(np.concatenate([-np.sin(ar), np.sin(ar), -np.sin(ac), np.sin(ac)], axis=-1))
    shift = np.zeros((HEAD_DIM, 3 * GRID_W - 1), np.float32)
    for r in range(2):
        for j in range(REL_COLS):
            shift[32 * r + j, GRID_W * r + GRID_W - 1 + WINDOW_COLS - 1 - j] = 1
    c["shift"] = np.concatenate([shift, shift])
    q, k = np.arange(GRID_W)[:, None], np.arange(GRID_W)[None, :]
    start = np.clip(q - WINDOW_COLS // 2, 0, GRID_W - WINDOW_COLS)
    inside = (k >= start) & (k < start + WINDOW_COLS)
    c["col_mask"] = np.tile(np.where(inside, 0, NEG).astype(np.float32), (2, 1))
    q, k = np.arange(P)[:, None], np.arange(P)[None, :]
    c["near_mask"] = np.stack([np.where(k >= q, 0, NEG), np.where(k <= q, 0, NEG)], axis=1).astype(np.float32)
    c["tri"] = np.stack([q <= k, q >= k], axis=1).astype(np.float32)
    c["order_mask"] = np.where(c["tri"] > 0, 0, NEG).astype(np.float32)
    return c


_INS = ["x", "c", "ctx", "c_ctx", "norm1_g", "norm2_g", "w_mod", "b_mod", "w_mlp1", "w_mlp2", "a_w_qkv", "a_q_norm_g", "a_k_norm_g",
        "a_lambda_q1", "a_lambda_k1", "a_lambda_q2", "a_lambda_k2", "a_subln_g", "a_w_o", "b_w_qkv", "b_q_norm_g", "b_k_norm_g",
        "b_rpb", "b_w_o", "c_2", "ctx_2", "c_ctx_2", "w_mod_2", "b_mod_2", "ln_mix_g_2", "ln_mix_b_2", "ln_ff_g_2", "ln_ff_b_2",
        "att_w_in_2", "att_w_out_2", "att_sink_2", "ssm_w_in_2", "ssm_conv_w_2", "ssm_conv_b_2", "ssm_dt_bias_2", "ssm_a_log_2",
        "ssm_d_2", "ssm_norm_g_2", "ssm_w_out_2", "ff_w1_2", "ff_w2_2"]


def kernel(**inputs):
    import numpy as _np
    import concourse.bacc as _bacc
    from concourse import mybir as _mybir
    from concourse.bass_utils import run_bass_kernel_spmd as _run

    nc = _bacc.Bacc("TRN2", target_bir_lowering=False, num_devices=1)
    arrays, A = {}, {}
    for name in _INS:
        a = _np.ascontiguousarray(inputs[name])
        arrays[f"in_{name}"] = a
        A[name] = nc.dram_tensor(f"in_{name}", a.shape, _mybir.dt.from_np(a.dtype), kind="ExternalInput").ap()
    for name, a in constants().items():
        arrays[f"const_{name}"] = a
        A[f"const_{name}"] = nc.dram_tensor(f"const_{name}", a.shape, _mybir.dt.from_np(a.dtype), kind="ExternalInput").ap()
    out = nc.dram_tensor("out", (1, N_LAT, D), _mybir.dt.float32, kind="ExternalOutput").ap()
    program(nc, A, out[0])
    r = _run(nc, [arrays], core_ids=[0])
    return r.results[0]["out"]
```
